# Optimizing a Trainium2 kernel written in Bass

```python
import math
import jax, jax.numpy as jnp
from jax import lax
import numpy as np

D_MODEL = 2048
BATCH = 1
SEQ = 256
DEPTH = 1

GRID_W = 64
CTX_LEN = 256
EPS = 1e-6
N_MOD = 6

HY_WIDTH = D_MODEL // 2
FILT_EMB = 33
FILT_BANDS = (FILT_EMB - 1) // 2
FILT_ORDER = 64
FILT_TARGET = 1e-2
FILT_DECAY_FAST = 0.3
FILT_DECAY_SLOW = 1.5
FILT_MIN_DECAY = math.log(FILT_TARGET) / FILT_DECAY_SLOW
FILT_MAX_DECAY = math.log(FILT_TARGET) / FILT_DECAY_FAST
FILT_SHIFT = 0.05

DA_HEADS = 8
DA_HEAD_DIM = 64
DA_V_DIM = 2 * DA_HEAD_DIM
DA_WIDTH = DA_HEADS * DA_V_DIM
ROPE_BASE = 10000.0
ROPE_AXIS_DIM = DA_HEAD_DIM // 2
Q_BLOCK = 128

PEER_HEADS = 8
PEER_N_KEYS = 128
PEER_N_EXPERTS = PEER_N_KEYS * PEER_N_KEYS
PEER_TOPK = 16
PEER_DK = 256
PEER_DK_HALF = PEER_DK // 2
PEER_BLOCK = 128

DA_Q_OFF = 3 * HY_WIDTH
DA_K_OFF = DA_Q_OFF + DA_HEADS * 2 * DA_HEAD_DIM
DA_V_OFF = DA_K_OFF + DA_HEADS * 2 * DA_HEAD_DIM
GATE_OFF = DA_V_OFF + DA_WIDTH
IN_COLS = GATE_OFF + 2 * D_MODEL

kernel_name = "hyena_diffattn_peer_hybrid_block"

def rmsnorm(x, g):
    xf = x.astype(jnp.float32)
    y = xf * lax.rsqrt(jnp.mean(xf * xf, axis=-1, keepdims=True) + EPS)
    return (y * g.astype(jnp.float32)).astype(x.dtype)

def modulate(h, shift, scale):
    return h * (1 + scale) + shift

def short_conv(u, w, b):
    up = jnp.pad(u, ((0, 0), (1, 1), (0, 0)))
    return up[:, :-2] * w[0] + up[:, 1:-1] * w[1] + up[:, 2:] * w[2] + b

def hyena_filter_spectrum(L, f_w1, f_b1, f_w2, f_b2, f_w3, f_b3, f_wout, f_freq):
    f32 = jnp.float32
    t = jnp.linspace(0.0, 1.0, L, dtype=f32)[:, None]
    w = 2.0 * math.pi * jnp.arange(L, dtype=f32)[:, None] / L
    bands = jnp.linspace(1e-4, FILT_BANDS - 1, FILT_BANDS, dtype=f32)[None, :]
    z = jnp.concatenate([t, jnp.cos(bands * w), -jnp.sin(bands * w)], axis=-1).astype(f_w1.dtype)
    h = jnp.sin(f_freq * (z @ f_w1 + f_b1))
    h = jnp.sin(f_freq * (h @ f_w2 + f_b2))
    h = jnp.sin(f_freq * (h @ f_w3 + f_b3))
    h = (h @ f_wout).astype(f32)
    deltas = jnp.abs(jnp.linspace(FILT_MIN_DECAY, FILT_MAX_DECAY, HY_WIDTH, dtype=f32))
    window = jnp.exp(-t * deltas[None, :]) + FILT_SHIFT
    h_fwd = h[:, :HY_WIDTH] * window
    h_bwd = h[:, HY_WIDTH:] * window
    k = jnp.concatenate([h_fwd, jnp.zeros((1, HY_WIDTH), f32), h_bwd[1:][::-1]], axis=0)
    return jnp.fft.rfft(k, axis=0)

def fft_long_conv(u, k_spec, bias):
    L = u.shape[1]
    uf = jnp.fft.rfft(u.astype(jnp.float32), n=2 * L, axis=1)
    y = jnp.fft.irfft(uf * k_spec[None], n=2 * L, axis=1)[:, :L]
    return (y + u.astype(jnp.float32) * bias.astype(jnp.float32)).astype(u.dtype)

def hyena_mix(p_hy, conv_w, conv_b, f_w1, f_b1, f_w2, f_b2, f_w3, f_b3, f_wout, f_freq, bias):
    L = p_hy.shape[1]
    z = short_conv(p_hy, conv_w, conv_b)
    v, x1, x0 = jnp.split(z, 3, axis=-1)
    k_spec = hyena_filter_spectrum(L, f_w1, f_b1, f_w2, f_b2, f_w3, f_b3, f_wout, f_freq)
    return x0 * fft_long_conv(v * x1, k_spec, bias)

def split_qkv(p):
    B, L, _ = p.shape
    q = p[..., DA_Q_OFF:DA_K_OFF].reshape(B, L, DA_HEADS, 2, DA_HEAD_DIM)
    k = p[..., DA_K_OFF:DA_V_OFF].reshape(B, L, DA_HEADS, 2, DA_HEAD_DIM)
    v = p[..., DA_V_OFF:GATE_OFF].reshape(B, L, DA_HEADS, DA_V_DIM)
    return q, k, v

def rope_axis(xa, pos):
    half = ROPE_AXIS_DIM // 2
    inv = ROPE_BASE ** (-jnp.arange(0, half, dtype=jnp.float32) / half)
    ang = pos.astype(jnp.float32)[:, None] * inv[None, :]
    cos = jnp.cos(ang)[None, :, None, None, :].astype(xa.dtype)
    sin = jnp.sin(ang)[None, :, None, None, :].astype(xa.dtype)
    x1, x2 = xa[..., :half], xa[..., half:]
    return jnp.concatenate([x1 * cos - x2 * sin, x2 * cos + x1 * sin], axis=-1)

def rope2d(x, row_pos, col_pos):
    return jnp.concatenate([rope_axis(x[..., :ROPE_AXIS_DIM], row_pos),
                            rope_axis(x[..., ROPE_AXIS_DIM:], col_pos)], axis=-1)

def diff_attend(q, k, v, lam):
    s = jnp.einsum('bqhcd,bkhcd->bhcqk', q, k).astype(jnp.float32) * (DA_HEAD_DIM ** -0.5)
    p = jax.nn.softmax(s, axis=-1)
    a = (p[:, :, 0] - lam * p[:, :, 1]).astype(v.dtype)
    return jnp.einsum('bhqk,bkhe->bqhe', a, v)

def diff_head_out(o, subln, lam_init):
    B, L = o.shape[:2]
    return (rmsnorm(o, subln) * (1.0 - lam_init)).reshape(B, L, DA_WIDTH)

def merge_branches(y_hy, y_da, gates, w_hy_out, w_da_out, w_o):
    g_hy, g_da = jnp.split(gates, 2, axis=-1)
    m = jax.nn.sigmoid(g_hy) * (y_hy @ w_hy_out) + jax.nn.sigmoid(g_da) * (y_da @ w_da_out)
    return m @ w_o

def peer(h, w_q, keys, u_tab, v_tab):
    B, L, D = h.shape
    hb = h.reshape(-1, PEER_BLOCK, D)

    def block(hx):
        n = hx.shape[0]
        q = (hx @ w_q).reshape(n, PEER_HEADS, 2, PEER_DK_HALF)
        s = jnp.einsum('nhpd,phkd->nhpk', q, keys)
        sv, si = lax.top_k(s, PEER_TOPK)
        cand_s = (sv[:, :, 0, :, None] + sv[:, :, 1, None, :]).reshape(n, PEER_HEADS, PEER_TOPK * PEER_TOPK)
        cand_i = (si[:, :, 0, :, None] * PEER_N_KEYS + si[:, :, 1, None, :]).reshape(n, PEER_HEADS, PEER_TOPK * PEER_TOPK)
        top_s, top_p = lax.top_k(cand_s, PEER_TOPK)
        idx = jnp.take_along_axis(cand_i, top_p, axis=-1)
        g = jax.nn.softmax(top_s.astype(jnp.float32), axis=-1)
        act = jax.nn.gelu(jnp.einsum('nd,nhkd->nhk', hx, u_tab[idx]), approximate=False)
        wgt = (g * act.astype(jnp.float32)).astype(hx.dtype)
        return jnp.einsum('nhk,nhkd->nd', wgt, v_tab[idx])

    return lax.map(block, hb).reshape(B, L, D)

def setup_inputs(seed: int = 0) -> dict:
    key = jax.random.key(seed)
    ks = jax.random.split(key, 32)
    f32 = jnp.float32
    D, C = D_MODEL, HY_WIDTH

    def nrm(k, shape, scale):
        return jax.random.normal(k, shape, f32) * scale

    return {
        "x": nrm(ks[0], (BATCH, SEQ, D), 1.0),
        "c": nrm(ks[1], (BATCH, D), 1.0),
        "ctx": nrm(ks[2], (BATCH, CTX_LEN, D), 1.0),
        "c_ctx": nrm(ks[3], (D,), 1.0),
        "w_mod": nrm(ks[4], (DEPTH, D, N_MOD * D), 0.5 * D ** -0.5),
        "b_mod": nrm(ks[5], (DEPTH, N_MOD * D), 0.01),
        "norm_pre_mix": 1.0 + nrm(ks[6], (DEPTH, D), 0.05),
        "norm_post_mix": 1.0 + nrm(ks[7], (DEPTH, D), 0.05),
        "norm_pre_ffn": 1.0 + nrm(ks[8], (DEPTH, D), 0.05),
        "norm_post_ffn": 1.0 + nrm(ks[9], (DEPTH, D), 0.05),
        "w_in": nrm(ks[10], (DEPTH, D, IN_COLS), D ** -0.5),
        "hy_conv_w": nrm(ks[11], (DEPTH, 3, 3 * C), 3 ** -0.5),
        "hy_conv_b": nrm(ks[12], (DEPTH, 3 * C), 0.01),
        "filt_w1": nrm(ks[13], (DEPTH, FILT_EMB, FILT_ORDER), FILT_EMB ** -0.5),
        "filt_b1": nrm(ks[14], (DEPTH, FILT_ORDER), 0.1),
        "filt_w2": nrm(ks[15], (DEPTH, FILT_ORDER, FILT_ORDER), FILT_ORDER ** -0.5),
        "filt_b2": nrm(ks[16], (DEPTH, FILT_ORDER), 0.1),
        "filt_w3": nrm(ks[17], (DEPTH, FILT_ORDER, FILT_ORDER), FILT_ORDER ** -0.5),
        "filt_b3": nrm(ks[18], (DEPTH, FILT_ORDER), 0.1),
        "filt_w_out": nrm(ks[19], (DEPTH, FILT_ORDER, 2 * C), 0.1 * FILT_ORDER ** -0.5),
        "filt_freq": 1.0 + nrm(ks[20], (DEPTH, FILT_ORDER), 0.05),
        "hy_bias": nrm(ks[21], (DEPTH, C), 0.1),
        "da_lambda": nrm(ks[22], (DEPTH, 4, DA_HEAD_DIM), 0.1),
        "da_subln": 1.0 + nrm(ks[23], (DEPTH, DA_V_DIM), 0.05),
        "w_hy_out": nrm(ks[24], (DEPTH, C, D), C ** -0.5),
        "w_da_out": nrm(ks[25], (DEPTH, DA_WIDTH, D), DA_WIDTH ** -0.5),
        "w_o": nrm(ks[26], (DEPTH, D, D), D ** -0.5),
        "peer_w_q": nrm(ks[27], (DEPTH, D, PEER_HEADS * PEER_DK), D ** -0.5),
        "peer_keys": nrm(ks[28], (DEPTH, 2, PEER_HEADS, PEER_N_KEYS, PEER_DK_HALF), PEER_DK_HALF ** -0.5),
        "peer_u": nrm(ks[29], (DEPTH, PEER_N_EXPERTS, D), D ** -0.5),
        "peer_v": nrm(ks[30], (DEPTH, PEER_N_EXPERTS, D), D ** -0.5),
    }

def reference(x, c, ctx, c_ctx, w_mod, b_mod, norm_pre_mix, norm_post_mix, norm_pre_ffn, norm_post_ffn,
              w_in, hy_conv_w, hy_conv_b, filt_w1, filt_b1, filt_w2, filt_b2, filt_w3, filt_b3,
              filt_w_out, filt_freq, hy_bias, da_lambda, da_subln, w_hy_out, w_da_out, w_o,
              peer_w_q, peer_keys, peer_u, peer_v):
    B, T, D = x.shape
    rows = T // GRID_W
    row_pos = jnp.repeat(jnp.arange(rows, dtype=jnp.int32), GRID_W)
    col_pos = jnp.tile(jnp.arange(GRID_W, dtype=jnp.int32), rows)
    n_blocks = T // Q_BLOCK
    cx = ctx
    for l in range(DEPTH):
        last = l == DEPTH - 1
        mod_lat = (jax.nn.silu(c) @ w_mod[l] + b_mod[l]).reshape(B, 1, N_MOD, D)
        mod_ctx = (jax.nn.silu(c_ctx) @ w_mod[l] + b_mod[l]).reshape(1, 1, N_MOD, D)
        sh1, sc1, g1, sh2, sc2, g2 = [mod_lat[:, :, i] for i in range(N_MOD)]
        csh1, csc1, cg1, csh2, csc2, cg2 = [mod_ctx[:, :, i] for i in range(N_MOD)]
        hy_args = (hy_conv_w[l], hy_conv_b[l], filt_w1[l], filt_b1[l], filt_w2[l], filt_b2[l],
                   filt_w3[l], filt_b3[l], filt_w_out[l], filt_freq[l], hy_bias[l])
        lam_init = 0.8 - 0.6 * math.exp(-0.3 * l)
        lam_p = da_lambda[l].astype(jnp.float32)
        lam = jnp.exp(jnp.sum(lam_p[0] * lam_p[1])) - jnp.exp(jnp.sum(lam_p[2] * lam_p[3])) + lam_init

        u_lat = modulate(rmsnorm(x, norm_pre_mix[l]), sh1, sc1)
        u_ctx = modulate(rmsnorm(cx, norm_pre_mix[l]), csh1, csc1)
        p_lat = u_lat @ w_in[l]
        p_ctx = u_ctx @ w_in[l]

        y_hy = hyena_mix(p_lat[..., :DA_Q_OFF], *hy_args)
        q_lat, k_lat, v_lat = split_qkv(p_lat)
        q_lat = rope2d(q_lat, row_pos, col_pos)
        k_lat = rope2d(k_lat, row_pos, col_pos)
        q_ctx, k_ctx, v_ctx = split_qkv(p_ctx)
        k_all = jnp.concatenate([k_ctx, k_lat], axis=1)
        v_all = jnp.concatenate([v_ctx, v_lat], axis=1)
        q_blocks = q_lat.reshape(B, n_blocks, Q_BLOCK, DA_HEADS, 2, DA_HEAD_DIM).swapaxes(0, 1)
        o_blocks = lax.map(lambda qb: diff_attend(qb, k_all, v_all, lam), q_blocks)
        o_lat = o_blocks.swapaxes(0, 1).reshape(B, T, DA_HEADS, DA_V_DIM)
        y_da = diff_head_out(o_lat, da_subln[l], lam_init)
        mix_lat = merge_branches(y_hy, y_da, p_lat[..., GATE_OFF:], w_hy_out[l], w_da_out[l], w_o[l])
        x = x + g1 * rmsnorm(mix_lat, norm_post_mix[l])
        if not last:
            y_hy_c = hyena_mix(p_ctx[..., :DA_Q_OFF], *hy_args)
            y_da_c = diff_head_out(diff_attend(q_ctx, k_ctx, v_ctx, lam), da_subln[l], lam_init)
            mix_ctx = merge_branches(y_hy_c, y_da_c, p_ctx[..., GATE_OFF:], w_hy_out[l], w_da_out[l], w_o[l])
            cx = cx + cg1 * rmsnorm(mix_ctx, norm_post_mix[l])

        h_lat = modulate(rmsnorm(x, norm_pre_ffn[l]), sh2, sc2)
        x = x + g2 * rmsnorm(peer(h_lat, peer_w_q[l], peer_keys[l], peer_u[l], peer_v[l]), norm_post_ffn[l])
        if not last:
            h_ctx = modulate(rmsnorm(cx, norm_pre_ffn[l]), csh2, csc2)
            cx = cx + cg2 * rmsnorm(peer(h_ctx, peer_w_q[l], peer_keys[l], peer_u[l], peer_v[l]), norm_post_ffn[l])
    return x


_drawn_inputs = setup_inputs


def setup_inputs(seed=0):
    import zlib

    import numpy as np

    out = dict(_drawn_inputs(seed))
    spreads = {}
    factors = {'norm_post_ffn': 3.797, 'hy_conv_b': 3.23, 'da_lambda': 3.0}
    for name, (base, spread) in spreads.items():
        noise = np.random.default_rng([zlib.crc32(name.encode()), seed]).standard_normal(out[name].shape)
        drawn = base * np.exp(spread * noise) if base else spread * noise
        out[name] = __import__('jax').numpy.asarray(drawn.astype(out[name].dtype))
    for name, factor in factors.items():
        out[name] = (out[name] * factor).astype(out[name].dtype)
    return out
```

```python
from contextlib import ExitStack
import math

import numpy as np

import concourse.bass as bass
from concourse import mybir

F32 = mybir.dt.float32
U32 = mybir.dt.uint32
I32 = mybir.dt.int32
ALU = mybir.AluOpType
ACT = mybir.ActivationFunctionType
AX = mybir.AxisListType

P = 128
ARENA_KB = 204
D = 2048
SEQ = 256
CTX = 256
TT = SEQ // P
KD = D // P
C = D // 2
KC = C // P
GRID_W = 64
EPS = 1e-6
HEADS = 8
HD = 64
KV = CTX + SEQ
Q_OFF = 3 * C
K_OFF = Q_OFF + C
V_OFF = K_OFF + C
GATE_OFF = V_OFF + C
IN_COLS = GATE_OFF + 2 * D
N_MOD = 6
LAM_INIT = 0.8 - 0.6 * math.exp(0.0)
FILT_EMB = 33
FILT_ORDER = 64
PEER_HEADS = 8
N_KEYS = 128
N_EXPERTS = N_KEYS * N_KEYS
TOPK = 16
DK_HALF = 128
HP = 2 * PEER_HEADS
N = 512
KH = 8
RING = 4
SLOTS = 16
LOWEST = -3.0e38
TWO_PI_HI = 6.28125
TWO_PI_LO = 2.0 * math.pi - 6.28125
ROUND = 1.5 * 2.0 ** 23
MODULATE_END = 2 * (2 * D // N)
PROJECT_END = MODULATE_END + 2 * (2 * C // N) + 2 * (4 * C // N)
ATTEND_END = PROJECT_END + 2 * (2 * D // N)
BRANCH_END = ATTEND_END + 2 * (D // N)
OUT_END = BRANCH_END + 2 * (D // N)
ALL_END = OUT_END + 2 * (D // N)
V_C, V_CCTX, V_NORM, V_BSH, V_BSC = 0, 16, 32, 48, 64


def constants():
    f64 = np.float64
    t = np.arange(SEQ, dtype=f64)
    freq = np.arange(SEQ, dtype=f64) + 0.5
    ang = 2.0 * np.pi * np.outer(t, freq) / (2 * SEQ)
    scale = 2.0 / (2 * SEQ)
    bands_n = (FILT_EMB - 1) // 2
    tl = np.linspace(0.0, 1.0, SEQ)[:, None]
    w = 2.0 * math.pi * t[:, None] / SEQ
    bands = np.linspace(1e-4, bands_n - 1, bands_n)[None, :]
    z = np.concatenate([tl, np.cos(bands * w), -np.sin(bands * w)], axis=-1)
    deltas = np.abs(np.linspace(math.log(1e-2) / 1.5, math.log(1e-2) / 0.3, C))
    window = np.exp(-tl * deltas[None, :]) + 0.05
    window_b = window.copy()
    window_b[0] = 0.0
    half = HD // 4
    inv = 10000.0 ** (-np.arange(half, dtype=f64) / half)
    row = np.repeat(np.arange(SEQ // GRID_W), GRID_W)[:, None] * inv
    col = np.tile(np.arange(GRID_W), SEQ // GRID_W)[:, None] * inv
    cos = np.concatenate([np.cos(row), np.cos(row), np.cos(col), np.cos(col)], axis=1)
    sin = np.concatenate([-np.sin(row), np.sin(row), -np.sin(col), np.sin(col)], axis=1)
    f = lambda a: np.ascontiguousarray(a, dtype=np.float32)
    return {
        "k_ident": f(np.eye(P)), "k_cos": f(np.cos(ang)), "k_sin": f(np.sin(ang)),
        "k_icos": f(scale * np.cos(ang).T), "k_isin": f(-scale * np.sin(ang).T),
        "k_zT": f(z.T), "k_window": f(window), "k_window_b": f(window_b),
        "k_rope_cos": f(cos), "k_rope_sin": f(sin),
        "k_iota": f(np.tile(np.arange(TOPK), (P, 1))),
    }


def chunks():
    halves = []

    def full(name, col, banks):
        halves.append((name, 0, col, True, False, banks))
        halves.append((name, KH * P, col, False, True, banks))
    for j in range(2 * D // N):
        full("w_mod", j * N, 1)
    for j in range(2 * C // N):
        full("w_in", K_OFF + j * N, 2 * TT)
    for j in range(4 * C // N):
        full("w_in", j * N, TT)
    for j in range(2 * D // N):
        full("w_in", GATE_OFF + j * N, TT)
    for j in range(D // N):
        halves.append(("w_hy_out", 0, j * N, True, True, TT))
        halves.append(("w_da_out", 0, j * N, True, True, TT))
    for name in ("w_o", "peer_w_q"):
        for j in range(D // N):
            full(name, j * N, TT)
    return halves


def uses(halves):
    bank, partial, found = 0, 0, []
    for _, _, _, _, ends, banks in halves:
        if ends:
            found.append((bank, 1, bank + banks))
            bank += banks
        else:
            partial += 1
            found.append((bank, 0, partial))
    return found


class Chain:

    def __init__(self, eng, sem, base=0):
        self.eng, self.sem, self.base, self.n = eng, sem, base, 0

    def link(self, ins, then=None):
        ins.then_inc(self.sem, 1)
        self.n += 1
        self.eng.wait_ge(self.sem, self.base + self.n)
        if then is not None:
            self.eng.sem_inc(then, 1)


def rsqrt(nc, ch, x, y, tmp):
    ch.link(nc.vector.tensor_scalar(tmp.bitcast(I32), x.bitcast(I32), 1, None, ALU.logical_shift_right))
    ch.link(nc.vector.tensor_scalar(y.bitcast(I32), tmp.bitcast(I32), -1.0, 1597463007.0, ALU.mult, ALU.add))
    for _ in range(4):
        ch.link(nc.vector.tensor_tensor(tmp, x, y, ALU.mult))
        ch.link(nc.vector.tensor_tensor(tmp, tmp, y, ALU.mult))
        ch.link(nc.vector.tensor_scalar(tmp, tmp, -0.5, 1.5, ALU.mult, ALU.add))
        ch.link(nc.vector.tensor_tensor(y, y, tmp, ALU.mult))


def build(nc, io, out):
    with ExitStack() as whole:
        def sem(name):
            return whole.enter_context(nc.semaphore(name))

        def scratch(name, shape):
            return nc.dram_tensor(name, shape, F32).ap()

        mod_rows = scratch("mod_rows", (4, D))
        filt_spec = scratch("filt_spec", (P, 4, C))
        shifted = scratch("shifted", (SEQ + 2, 3 * C))

        psA = whole.enter_context(nc.psum_tensor("psA", [P, 4, N], F32))
        psB = whole.enter_context(nc.psum_tensor("psB", [P, 4, N], F32))
        arena = whole.enter_context(nc.sbuf_tensor("arena", [P, ARENA_KB * 256], F32))
        ident = whole.enter_context(nc.sbuf_tensor("ident", [P, P], F32))
        ones = whole.enter_context(nc.sbuf_tensor("ones", [P, 1], F32))
        cols = whole.enter_context(nc.sbuf_tensor("cols", [P, 80], F32))
        small = whole.enter_context(nc.sbuf_tensor("small", [P, 8 + 4 * HD], F32))

        def at(kb, *shape):
            size = int(np.prod(shape))
            flat = arena[:, int(kb * 256):int(kb * 256) + size]
            if len(shape) == 1:
                return flat
            names = "abcd"[:len(shape)]
            return flat.rearrange(f"p ({' '.join(names)}) -> p {' '.join(names)}",
                                  **dict(zip(names[1:], shape[1:])))

        ring = at(0, RING, KH, N)
        uT = at(64, KD, SEQ)
        uctxT = at(80, KD, CTX)
        kT = at(80, HEADS, KV)
        v_all = at(96, 2 * TT, C)
        k_all = at(112, 2 * TT, C)
        q_lat = at(128, TT, C)
        hy_u = at(136, TT, C)
        hy_x0 = at(144, TT, C)
        qT = at(188, HEADS, SEQ)
        y_hyT = at(196, KC, SEQ)
        gates = at(112, TT, 2 * D)
        y_daT = at(96, KC, SEQ)

        w_landed = [sem(f"w_landed{i}") for i in range(RING)]
        w_used = sem("w_used")
        a_full = sem("a_full")
        a_free = sem("a_free")
        halves = chunks()
        place = uses(halves)

        def stream(sp, first, upto):
            for n in range(first, upto):
                name, row, col = halves[n][:3]
                if n >= RING:
                    _, which, value = place[n - RING]
                    sp.wait_ge((w_used, a_full)[which], value)
                src = io[name][0, row:row + KH * P, col:col + N].rearrange("(k p) n -> p k n", p=P)
                sp.dma_start(ring[:, n % RING, :, :], src).then_inc(w_landed[n % RING], 16)

        def gemm_half(pe, n, lefts):
            _, _, _, begins, ends, banks = halves[n]
            bank, which, _ = place[n]
            assert banks == len(lefts)
            pe.wait_ge(w_landed[n % RING], 16 * (n // RING + 1))
            for b, left in enumerate(lefts, bank):
                if begins and b >= 4:
                    pe.wait_ge(a_free, b - 3)
                for k in range(KH):
                    last = nc.tensor.matmul(psA[0:left(k).shape[1], b % 4, :], left(k), ring[:, n % RING, k, :],
                                            start=begins and k == 0, stop=ends and k == KH - 1)
                if ends:
                    last.then_inc(a_full, 1)
            if not ends:
                last.then_inc(w_used, 1)

        x_rows = [io["x"][0, 0:P, :], io["x"][0, P:SEQ, :], io["ctx"][0, 0:P, :], io["ctx"][0, P:CTX, :]]
        with ExitStack() as st:
            xin = at(96, 4, D)
            mod_row = at(128, 2 * D)[0:2]
            bias_row = mod_row[0:1, 0:C]
            filt = at(144, 2, TT, C)
            spec = at(160, 4, C)
            window = at(176, 2, C)
            fwout = at(184, 2 * C)[0:FILT_ORDER]
            dft = at(192, 2, TT, SEQ)
            vecs = at(196, P)
            zT = at(196.5, SEQ)[0:FILT_EMB]
            arg = at(197.5, 2, SEQ)[0:FILT_ORDER]
            feat = at(199.5, 2, SEQ)[0:FILT_ORDER]
            fw1 = at(201.5, FILT_ORDER)[0:FILT_EMB]
            fw23 = at(201.75, 2, FILT_ORDER)[0:FILT_ORDER]
            fcol = at(202.25, 4)[0:FILT_ORDER]
            shift = at(202.75, 2, KD)
            gain = at(203, 2, KD)
            rstd = at(203.25, 4)
            rtmp = at(203.5, 2)

            s_vec, s_x, s_con, s_flt = sem("s_vec"), [sem(f"s_x{i}") for i in range(4)], sem("s_con"), sem("s_flt")
            s_win = sem("s_win")
            s_silu, s_cols, s_colsb = sem("s_silu"), sem("s_cols"), sem("s_colsb")
            s_norm, s_xt, s_xe = sem("s_norm"), sem("s_xt"), sem("s_xe")
            s_mt, s_mod, s_fp, s_fa, s_fs = sem("s_mt"), sem("s_mod"), sem("s_fp"), sem("s_fa"), sem("s_fs")
            s_v1, s_hf, s_sp, s_spe, s_spo, s_ones = (sem("s_v1"), sem("s_hf"), sem("s_sp"), sem("s_spe"),
                                                     sem("s_spo"), sem("s_ones"))
            s_wo2 = sem("s_wo2")
            block = st.enter_context(nc.Block())

            @block.sync
            def _(sp):
                sp.dma_start(vecs[V_C:V_C + 16, :], io["c"].rearrange("a (k p) -> (a k) p", p=P)).then_inc(s_vec, 16)
                sp.dma_start(vecs[V_CCTX:V_CCTX + 16, :], io["c_ctx"].rearrange("(k p) -> k p", p=P)).then_inc(s_vec, 16)
                sp.dma_start(vecs[V_NORM:V_NORM + 16, :], io["norm_pre_mix"].rearrange("a (k p) -> (a k) p", p=P)).then_inc(s_vec, 16)
                sp.dma_start(vecs[V_BSH:V_BSH + 32, :],
                             io["b_mod"][:, 0:2 * D].rearrange("a (k p) -> (a k) p", p=P)).then_inc(s_vec, 16)
                sp.dma_start(ident[:], io["k_ident"]).then_inc(s_con, 16)
                stream(sp, 0, 2)
                for i in range(4):
                    sp.dma_start(xin[:, i, :], x_rows[i]).then_inc(s_x[i], 16)
                stream(sp, 2, 4)
                stream(sp, 4, MODULATE_END + RING)

            @block.scalar
            def _(act):
                act.dma_start(zT[:], io["k_zT"]).then_inc(s_flt, 16)
                act.dma_start(fw1[:], io["filt_w1"][0]).then_inc(s_flt, 16)
                act.dma_start(fw23[:, 0, :], io["filt_w2"][0]).then_inc(s_flt, 16)
                act.dma_start(fw23[:, 1, :], io["filt_w3"][0]).then_inc(s_flt, 16)
                act.dma_start(fwout[:], io["filt_w_out"][0]).then_inc(s_flt, 16)
                for j, name in enumerate(("filt_b1", "filt_b2", "filt_b3", "filt_freq")):
                    act.dma_start(fcol[:, j:j + 1], io[name].rearrange("a f -> f a")).then_inc(s_flt, 16)
                act.dma_start(bias_row[:], io["hy_bias"]).then_inc(s_flt, 16)
                act.dma_start(dft[:, 0, :, :], io["k_cos"].rearrange("(t p) f -> p t f", p=P)).then_inc(s_flt, 16)
                act.dma_start(dft[:, 1, :, :], io["k_sin"].rearrange("(t p) f -> p t f", p=P)).then_inc(s_flt, 16)
                act.wait_ge(s_vec, 64)
                nc.scalar.activation(vecs[0:32, :], vecs[0:32, :], ACT.Silu).then_inc(s_silu, 1)
                for layer in range(3):
                    act.wait_ge(s_fa, layer + 1)
                    nc.scalar.activation(feat[:, layer % 2, :], arg[:, 0, :], ACT.Sin).then_inc(s_fs, 1)
                for i in range(4):
                    dst = uT if i < 2 else uctxT
                    for kq in range(4):
                        n = 4 * i + kq
                        act.wait_ge(s_xt, n + 1)
                        nc.scalar.activation(dst[:, 4 * kq:4 * kq + 4, (i % 2) * P:(i % 2) * P + P],
                                             psB[:, n % 2, :].rearrange("p (k t) -> p k t", k=4),
                                             ACT.Copy).then_inc(s_xe, 1)
                for m in range(8):
                    act.wait_ge(s_sp, m + 1)
                    part, nh = m // 2, m % 2
                    nc.scalar.activation(spec[:, part, nh * N:(nh + 1) * N], psB[:, m % 4, :], ACT.Copy).then_inc(s_spe, 1)
                act.wait_ge(s_spe, 8)
                act.dma_start(filt_spec, spec[:]).then_inc(s_spo, 16)
                act.wait_ge(s_spo, 16)

            @block.gpsimd
            def _(pool):
                nc.gpsimd.memset(ones[:], 1.0).then_inc(s_ones, 1)
                for t in range(TT):
                    if t:
                        pool.wait_ge(s_hf, 4)
                    pool.dma_start(window[:, 0, :], io["k_window"][t * P:(t + 1) * P, :]).then_inc(s_win, 16)
                    pool.dma_start(window[:, 1, :], io["k_window_b"][t * P:(t + 1) * P, :]).then_inc(s_win, 16)

            @block.tensor
            def _(pe):
                pe.wait_ge(s_con, 16)
                pe.wait_ge(s_silu, 1)
                nc.tensor.transpose(psB[:, 2, 0:80], vecs[0:80, :], ident[0:80, 0:80]).then_inc(s_cols, 1)
                pe.wait_ge(s_flt, 16 * 12)
                nc.tensor.matmul(psB[0:FILT_ORDER, 3, 0:SEQ], fw1[:], zT[:], start=True, stop=True).then_inc(s_fp, 1)
                for layer in range(2):
                    pe.wait_ge(s_fs, layer + 1)
                    nc.tensor.matmul(psB[0:FILT_ORDER, 3, 0:SEQ], fw23[:, layer, :], feat[:, layer % 2, :],
                                     start=True, stop=True).then_inc(s_fp, 1)
                for i in range(4):
                    pe.wait_ge(s_norm, i + 1)
                    for kq in range(4):
                        n = 4 * i + kq
                        if n >= 2:
                            pe.wait_ge(s_xe, n - 1)
                        for k in range(4 * kq, 4 * kq + 4):
                            m = nc.tensor.transpose(psB[:, n % 2, (k % 4) * P:(k % 4) * P + P],
                                                    xin[:, i, k * P:(k + 1) * P], ident[:])
                        m.then_inc(s_xt, 1)
                pe.wait_ge(s_fs, 3)
                pe.wait_ge(s_xe, 16)
                for t in range(TT):
                    if t:
                        pe.wait_ge(s_hf, 4)
                    for j in range(4):
                        m = nc.tensor.matmul(psB[:, j, :], feat[:, 0, t * P:(t + 1) * P], fwout[:, j * N:(j + 1) * N],
                                             start=True, stop=True)
                        m.then_inc(s_wo2, 1)
                pe.wait_ge(s_colsb, 1)
                for j in range(8):
                    for hf in range(2):
                        n = 2 * j + hf
                        gemm_half(pe, n, [lambda k, hf=hf: cols[:, hf * KH + k:hf * KH + k + 17:16]])
                    if j == 1:
                        pe.wait_ge(s_hf, 8)
                        for part in range(4):
                            for nh in range(2):
                                q = 2 * part + nh
                                if q >= 4:
                                    pe.wait_ge(s_spe, q - 3)
                                f0 = (part % 2) * P
                                for t in range(TT):
                                    m = nc.tensor.matmul(psB[:, q % 4, :], dft[:, part // 2, t, f0:f0 + P],
                                                         filt[:, part // 2, t, nh * N:(nh + 1) * N],
                                                         start=(t == 0), stop=(t == TT - 1))
                                m.then_inc(s_sp, 1)
                pe.wait_ge(a_free, 8)
                pe.wait_ge(s_spe, 8)
                for j in range(2 * KD):
                    m = nc.tensor.transpose(psB[:, 0, 2 * j:2 * j + 2], mod_row[:, j * P:(j + 1) * P], ident[0:2, 0:2])
                m.then_inc(s_mt, 1)

            @block.vector
            def _(v):
                ch = Chain(v, s_v1)
                v.wait_ge(s_cols, 1)
                nc.vector.tensor_copy(cols[:, 0:80], psB[:, 2, 0:80]).then_inc(s_colsb, 1)

                def sine_argument(layer):
                    v.wait_ge(s_flt, 16 * 12)
                    v.wait_ge(s_fp, layer + 1)
                    ch.link(nc.vector.tensor_scalar(arg[:, 0, :], psB[0:FILT_ORDER, 3, 0:SEQ], fcol[:, layer:layer + 1],
                                                    fcol[:, 3:4], ALU.add, ALU.mult))
                    ch.link(nc.vector.tensor_scalar(arg[:, 1, :], arg[:, 0, :], 0.5 / math.pi, ROUND, ALU.mult, ALU.add))
                    ch.link(nc.vector.tensor_scalar(arg[:, 1, :], arg[:, 1, :], -ROUND, None, ALU.add))
                    ch.link(nc.vector.scalar_tensor_tensor(arg[:, 0, :], arg[:, 1, :], -TWO_PI_HI, arg[:, 0, :], ALU.mult, ALU.add))
                    ch.link(nc.vector.scalar_tensor_tensor(arg[:, 0, :], arg[:, 1, :], -TWO_PI_LO, arg[:, 0, :], ALU.mult, ALU.add))
                    nc.vector.tensor_scalar(arg[:, 0, :], arg[:, 0, :], 3.1415925, -3.1415925, ALU.min, ALU.max).then_inc(s_fa, 1)

                sine_argument(0)
                for i in range(4):
                    v.wait_ge(s_x[i], 16)
                    ch.link(nc.vector.tensor_tensor_reduce(spec[:, 0:2, :].rearrange("p a c -> p (a c)"), xin[:, i, :],
                                                           xin[:, i, :], 1.0, 0.0, ALU.mult, ALU.add, rstd[:, i:i + 1]))
                    ch.link(nc.vector.tensor_scalar(rstd[:, i:i + 1], rstd[:, i:i + 1], 1.0 / D, EPS, ALU.mult, ALU.add))
                    rsqrt(nc, ch, rstd[:, i:i + 1], rtmp[:, 0:1], rtmp[:, 1:2])
                    nc.vector.tensor_scalar(xin[:, i, :], xin[:, i, :], rtmp[:, 0:1], None, ALU.mult).then_inc(s_norm, 1)
                    if i < 2:
                        sine_argument(i + 1)
                for t in range(TT):
                    v.wait_ge(s_win, 32 * (t + 1))
                    for nh in range(2):
                        cs = slice(nh * N, (nh + 1) * N)
                        v.wait_ge(s_wo2, 4 * t + nh + 3)
                        ch.link(nc.vector.tensor_tensor(window[:, 1, cs], psB[:, 2 + nh, :], window[:, 1, cs], ALU.mult))
                        ch.link(nc.vector.tensor_tensor(window[:, 0, cs], psB[:, nh, :], window[:, 0, cs], ALU.mult))
                        nc.vector.tensor_tensor(filt[:, 0, t, cs], window[:, 0, cs], window[:, 1, cs], ALU.add).then_inc(s_hf, 1)
                        nc.vector.tensor_tensor(filt[:, 1, t, cs], window[:, 1, cs], window[:, 0, cs], ALU.subtract).then_inc(s_hf, 1)
                    if t == 0:
                        v.wait_ge(s_hf, 4)
                        ch.link(nc.vector.tensor_tensor(filt[0:1, 0, 0, :], filt[0:1, 0, 0, :], bias_row[:], ALU.add))
                for j in range(8):
                    v.wait_ge(a_full, j + 1)
                    nc.vector.tensor_copy(mod_row[:, j * N:(j + 1) * N], psA[0:2, j % 4, :]).then_inc(a_free, 1)
                v.wait_ge(s_mt, 1)
                mc = psB[:, 0, 0:4 * KD].rearrange("p (j r) -> p j r", r=2)
                for r in range(2):
                    ch.link(nc.vector.tensor_tensor(shift[:, r, :], mc[:, 0:KD, r], cols[:, V_BSH:V_BSH + KD], ALU.add))
                    ch.link(nc.vector.tensor_tensor(gain[:, r, :], mc[:, KD:2 * KD, r], cols[:, V_BSC:V_BSC + KD], ALU.add))
                    ch.link(nc.vector.scalar_tensor_tensor(gain[:, r, :], gain[:, r, :], 1.0, cols[:, V_NORM:V_NORM + KD],
                                                           ALU.add, ALU.mult))
                v.wait_ge(s_xe, 16)
                for r, dst in ((0, uT), (1, uctxT)):
                    for k in range(KD):
                        nc.vector.tensor_scalar(dst[:, k, :], dst[:, k, :], gain[:, r, k:k + 1], shift[:, r, k:k + 1],
                                                ALU.mult, ALU.add).then_inc(s_mod, 1)


        with ExitStack() as st:
            p_in = at(152, TT, N)
            p_prev = at(156, TT, N)
            p_next = at(160, TT, N)
            taps = at(164, 3, N)
            tap_bias = at(170, N)
            t_tmp = at(172, TT, N)
            z_tmp = at(176, TT, N)
            wm = at(180, 2, 2, C)
            acc = at(196, 2, C)
            rope = at(180, 2, TT, HD)
            H_CHUNKS = 3 * C // N
            KV_CHUNKS = 2 * C // N
            VECS = 4

            s_wm = [sem("s_wm0"), sem("s_wm1")]
            s_wmu, s_acc, s_mrow, s_mcopy = sem("s_wmu"), sem("s_acc"), sem("s_mrow"), sem("s_mcopy")
            s_mout, s_mfree = sem("s_mout"), sem("s_mfree")
            s_zero, s_zout, s_pout, s_shift, s_taps, s_conv = (sem("s_zero"), sem("s_zout"), sem("s_pout"),
                                                               sem("s_shift"), sem("s_taps"), sem("s_conv"))
            s_rope, s_v2, s_v2m = sem("s_rope"), sem("s_v2"), sem("s_v2m")
            block = st.enter_context(nc.Block())
            first_bank = place[MODULATE_END][0]
            kv_bank = first_bank
            hy_bank = kv_bank + KV_CHUNKS * 2 * TT
            q_bank = hy_bank + H_CHUNKS * TT

            @block.sync
            def _(sp):
                n = MODULATE_END + RING
                for i in range(8 * VECS * 2):
                    vec, half, kp = i // 16, (i // 8) % 2, i % 8
                    if i >= 2:
                        sp.wait_ge(s_wmu, i - 1)
                    col = (2 + vec) * D + half * C
                    sp.dma_start(wm[:, i % 2, :, :],
                                 io["w_mod"][0, 2 * kp * P:2 * (kp + 1) * P, col:col + C].rearrange("(k p) n -> p k n", p=P)
                                 ).then_inc(s_wm[i % 2], 16)
                    if i % 8 == 7:
                        stream(sp, n, n + 1)
                        n += 1
                stream(sp, n, PROJECT_END + RING)

            @block.scalar
            def _(act):
                act.sem_inc(s_mfree, 2)

                def evacuate(bank, dst):
                    act.wait_ge(a_full, bank + 1)
                    return nc.scalar.activation(dst, psA[:, bank % 4, :], ACT.Copy).then_inc(a_free, 1)

                def mod_row_out(i):
                    act.wait_ge(s_mrow, i + 1)
                    nc.scalar.activation(acc[0:1, i % 2, :], psB[0:1, 2 * (i % 2):2 * (i % 2) + 2, :].rearrange("p a n -> p (a n)"),
                                         ACT.Copy).then_inc(s_mcopy, 1)
                    act.wait_ge(s_mcopy, i + 1)
                    act.dma_start(mod_rows[i // 2:i // 2 + 1, (i % 2) * C:(i % 2 + 1) * C], acc[0:1, i % 2, :]).then_inc(s_mout, 16)
                    act.wait_ge(s_mout, 16 * (i + 1))
                    act.sem_inc(s_mfree, 1)

                for j in range(KV_CHUNKS):
                    dst = (k_all, v_all)[j // 2]
                    for i in range(2 * TT):
                        evacuate(kv_bank + 2 * TT * j + i, dst[:, i, (j % 2) * N:(j % 2 + 1) * N])
                    if j:
                        mod_row_out(2 * j - 2)
                        mod_row_out(2 * j - 1)
                for j in range(H_CHUNKS):
                    if j:
                        act.wait_ge(s_conv, j)
                        act.wait_ge(s_pout, 16 * j)
                    for t in range(TT):
                        evacuate(hy_bank + TT * j + t, p_in[:, t, :])
                    if j == 0:
                        mod_row_out(2 * KV_CHUNKS - 2)
                        mod_row_out(2 * KV_CHUNKS - 1)
                for j in range(C // N):
                    for t in range(TT):
                        evacuate(q_bank + TT * j + t, q_lat[:, t, j * N:(j + 1) * N])

            @block.gpsimd
            def _(pool):
                nc.gpsimd.memset(z_tmp[0:3, :, :], 0.0).then_inc(s_zero, 1)
                pool.wait_ge(s_zero, 1)
                zeros = z_tmp[0:3, :, :].rearrange("p t n -> p (t n)")
                pool.dma_start(shifted[0, :].rearrange("(a n) -> a n", n=C), zeros).then_inc(s_zout, 16)
                pool.dma_start(shifted[SEQ + 1, :].rearrange("(a n) -> a n", n=C), zeros).then_inc(s_zout, 16)
                pool.wait_ge(s_zout, 32)
                for j in range(H_CHUNKS):
                    cs = slice(j * N, (j + 1) * N)
                    if j:
                        pool.wait_ge(s_conv, j)
                    pool.dma_start(taps, io["hy_conv_w"][0, :, cs].partition_broadcast(P)).then_inc(s_taps, 16)
                    pool.dma_start(tap_bias, io["hy_conv_b"][0, cs].partition_broadcast(P)).then_inc(s_taps, 16)
                    pool.wait_ge(a_free, hy_bank + TT * (j + 1))
                    pool.dma_start(shifted[1:SEQ + 1, cs].rearrange("(t p) n -> p t n", p=P), p_in).then_inc(s_pout, 16)
                    pool.wait_ge(s_pout, 16 * (j + 1))
                    pool.dma_start(p_prev, shifted[0:SEQ, cs].rearrange("(t p) n -> p t n", p=P)).then_inc(s_shift, 16)
                    pool.dma_start(p_next, shifted[2:SEQ + 2, cs].rearrange("(t p) n -> p t n", p=P)).then_inc(s_shift, 16)
                    if j == 0:
                        pool.wait_ge(s_acc, 2 * VECS)
                        pool.dma_start(rope[:, 0, :, :], io["k_rope_cos"].rearrange("(t p) d -> p t d", p=P)).then_inc(s_rope, 16)
                        pool.dma_start(rope[:, 1, :, :], io["k_rope_sin"].rearrange("(t p) d -> p t d", p=P)).then_inc(s_rope, 16)

            @block.tensor
            def _(pe):
                def token_tile(src, t, half):
                    return lambda k: src[:, half * KH + k, t * P:(t + 1) * P]

                def mod_sum(i):
                    pe.wait_ge(s_acc, i + 1)
                    if i >= 2:
                        pe.wait_ge(s_mcopy, i - 1)
                    for q in range(2):
                        last = nc.tensor.matmul(psB[0:1, 2 * (i % 2) + q, :], ones[:], acc[:, i % 2, q * N:(q + 1) * N],
                                                start=True, stop=True)
                    last.then_inc(s_mrow, 1)

                n = MODULATE_END
                for j in range(KV_CHUNKS):
                    for half in range(2):
                        gemm_half(pe, n, [token_tile(uT, t, half) for t in range(TT)]
                                  + [token_tile(uctxT, t, half) for t in range(TT)])
                        n += 1
                    if j:
                        mod_sum(2 * j - 2)
                        mod_sum(2 * j - 1)
                for j in range(H_CHUNKS + C // N):
                    for half in range(2):
                        gemm_half(pe, n, [token_tile(uT, t, half) for t in range(TT)])
                        n += 1
                    if j == 0:
                        mod_sum(2 * KV_CHUNKS - 2)
                        mod_sum(2 * KV_CHUNKS - 1)

            @block.vector
            def _(v):
                MOD_LINKS = KD
                with v.Fori(0, VECS) as vec:
                    for half in range(2):
                        ch = Chain(v, s_v2m, (2 * vec + half) * MOD_LINKS)
                        for kp in range(8):
                            v.wait_ge(s_wm[kp % 2], (vec * 8 + half * 4 + kp // 2 + 1) * 16)
                            if kp == 0:
                                v.wait_ge(s_mfree, 2 * vec + half + 1)
                            for j in range(2):
                                k = 2 * kp + j
                                if k == 0:
                                    ins = nc.vector.tensor_scalar(acc[:, half, :], wm[:, 0, 0, :], cols[:, 0:1], None, ALU.mult)
                                else:
                                    ins = nc.vector.scalar_tensor_tensor(acc[:, half, :], wm[:, kp % 2, j, :], cols[:, k:k + 1],
                                                                         acc[:, half, :], ALU.mult, ALU.add)
                                ch.link(ins)
                            v.sem_inc(s_wmu, 1)
                        assert ch.n == MOD_LINKS
                        v.sem_inc(s_acc, 1)

                ch = Chain(v, s_v2)

                def rotate(x, t):
                    heads = x.rearrange("p (h d) -> p h d", d=HD)
                    quarter = HD // 4
                    halves_ = lambda a: a.rearrange("p (h a b i) -> p h a b i", a=2, b=2, i=quarter)
                    one, two = (a.rearrange("p t n -> p (t n)") for a in (z_tmp, t_tmp))
                    cos = rope[:, 0, t, :].unsqueeze(1).broadcast_to((P, 2 * HEADS, HD))
                    ch.link(nc.vector.tensor_tensor(one.rearrange("p (h d) -> p h d", d=HD), heads, cos, ALU.mult))
                    for b in range(2):
                        sin = rope[:, 1, t, :].rearrange("p (a b i) -> p a b i", a=2, b=2)[:, :, b, :]
                        sin = sin.unsqueeze(1).broadcast_to((P, 2 * HEADS, 2, quarter))
                        ch.link(nc.vector.tensor_tensor(halves_(two)[:, :, :, b, :], halves_(x)[:, :, :, 1 - b, :], sin, ALU.mult))
                    ch.link(nc.vector.tensor_tensor(x, one, two, ALU.add))

                def over_tiles(w):
                    return w.unsqueeze(1).broadcast_to((P, TT, N))

                for j in range(H_CHUNKS):
                    cs = slice((j % 2) * N, (j % 2 + 1) * N)
                    v.wait_ge(s_taps, 32 * (j + 1))
                    v.wait_ge(s_shift, 32 * (j + 1))
                    ch.link(nc.vector.tensor_tensor(z_tmp, p_in, over_tiles(taps[:, 1, :]), ALU.mult))
                    for other, w in ((p_prev, 0), (p_next, 2)):
                        ch.link(nc.vector.tensor_tensor(t_tmp, other, over_tiles(taps[:, w, :]), ALU.mult))
                        ch.link(nc.vector.tensor_tensor(z_tmp, z_tmp, t_tmp, ALU.add))
                    bias = over_tiles(tap_bias)
                    if j // 2 == 0:
                        ch.link(nc.vector.tensor_tensor(hy_u[:, :, cs], z_tmp, bias, ALU.add))
                    elif j // 2 == 1:
                        ch.link(nc.vector.tensor_tensor(z_tmp, z_tmp, bias, ALU.add))
                        ch.link(nc.vector.tensor_tensor(hy_u[:, :, cs], hy_u[:, :, cs], z_tmp, ALU.mult))
                    else:
                        ch.link(nc.vector.tensor_tensor(hy_x0[:, :, cs], z_tmp, bias, ALU.add))
                    v.sem_inc(s_conv, 1)
                    if j == 2:
                        v.wait_ge(s_rope, 32)
                        for t in range(TT):
                            rotate(k_all[:, t, :], t)
                v.wait_ge(a_free, q_bank + TT * (C // N))
                for t in range(TT):
                    rotate(q_lat[:, t, :], t)


        neg_lam = small[:, 0:1]
        with ExitStack() as st:
            spec = at(152, 4, C)
            dft = at(168, 2, TT, SEQ)
            idft = at(172, 2, TT, SEQ)
            y_re = at(176, TT, C)
            y_im = hy_u
            tmp = at(184, 2, N)
            lam_in = small[:, 8:8 + 4 * HD].rearrange("p (a d) -> p a d", a=4)
            lam_sum = small[:, 1:3]
            lam_exp = small[:, 3:5]
            s_spec, s_lam, s_lsum, s_lexp = sem("s_spec"), sem("s_lam"), sem("s_lsum"), sem("s_lexp")
            s_uf, s_prod, s_kt, s_kte, s_inv, s_yt, s_yt_e, s_y = (
                sem("s_uf"), sem("s_prod"), sem("s_kt"), sem("s_kte"), sem("s_inv"), sem("s_yt"), sem("s_yt_e"), sem("s_y"))
            s_v3 = sem("s_v3")
            block = st.enter_context(nc.Block())

            @block.scalar
            def _(act):
                act.dma_start(dft[:, 0, :, :], io["k_cos"].rearrange("(t p) f -> p t f", p=P)).then_inc(s_spec, 16)
                act.dma_start(dft[:, 1, :, :], io["k_sin"].rearrange("(t p) f -> p t f", p=P)).then_inc(s_spec, 16)
                act.dma_start(spec, filt_spec).then_inc(s_spec, 16)
                act.dma_start(idft[:, 0, :, :], io["k_icos"].rearrange("(t p) f -> p t f", p=P)).then_inc(s_spec, 16)
                act.dma_start(idft[:, 1, :, :], io["k_isin"].rearrange("(t p) f -> p t f", p=P)).then_inc(s_spec, 16)
                act.dma_start(small[:, 8:8 + 4 * HD], io["da_lambda"][0].rearrange("a d -> (a d)").partition_broadcast(P)).then_inc(s_lam, 16)
                for h in range(HEADS):
                    act.wait_ge(s_kt, 2 * h + 1)
                    nc.scalar.activation(kT[:, h, :], psA[:, (2 * h) % 4, :], ACT.Copy).then_inc(s_kte, 1)
                    act.wait_ge(s_kt, 2 * h + 2)
                    nc.scalar.activation(qT[:, h, :], psA[:, (2 * h + 1) % 4, 0:SEQ], ACT.Copy).then_inc(s_kte, 1)
                for n in range(2 * TT):
                    act.wait_ge(s_yt, n + 1)
                    t, kq = n // 2, n % 2
                    nc.scalar.activation(y_hyT[:, 4 * kq:4 * kq + 4, t * P:(t + 1) * P],
                                         psA[:, n, :].rearrange("p (k t) -> p k t", k=4), ACT.Copy).then_inc(s_yt_e, 1)
                act.wait_ge(s_lsum, 1)
                nc.scalar.activation(lam_exp, lam_sum, ACT.Exp).then_inc(s_lexp, 1)

            @block.tensor
            def _(pe):
                pe.wait_ge(s_spec, 80)
                for nh, ps in ((0, psA), (1, psB)):
                    for part in range(4):
                        f0 = (part % 2) * P
                        for t in range(TT):
                            last = nc.tensor.matmul(ps[:, part, :], dft[:, part // 2, t, f0:f0 + P],
                                                    hy_u[:, t, nh * N:(nh + 1) * N], start=(t == 0), stop=(t == TT - 1))
                    last.then_inc(s_uf, 1)
                pe.wait_ge(s_prod, 1)
                for h in range(HEADS):
                    if h >= 2:
                        pe.wait_ge(s_kte, 2 * h - 3)
                    for t in range(2 * TT):
                        last = nc.tensor.transpose(psA[:, (2 * h) % 4, t * P:(t + 1) * P], k_all[:, t, h * P:(h + 1) * P], ident[:])
                    last.then_inc(s_kt, 1)
                    if h >= 2:
                        pe.wait_ge(s_kte, 2 * h - 2)
                    for t in range(TT):
                        last = nc.tensor.transpose(psA[:, (2 * h + 1) % 4, t * P:(t + 1) * P], q_lat[:, t, h * P:(h + 1) * P], ident[:])
                    last.then_inc(s_kt, 1)
                pe.wait_ge(s_prod, 2)
                for t in range(TT):
                    for nh in range(2):
                        for f in range(TT):
                            nc.tensor.matmul(psB[:, 2 * t + nh, :], idft[:, 0, f, t * P:(t + 1) * P],
                                             y_re[:, f, nh * N:(nh + 1) * N], start=(f == 0), stop=False)
                        for f in range(TT):
                            last = nc.tensor.matmul(psB[:, 2 * t + nh, :], idft[:, 1, f, t * P:(t + 1) * P],
                                                    y_im[:, f, nh * N:(nh + 1) * N], start=False, stop=(f == TT - 1))
                        last.then_inc(s_inv, 1)
                pe.wait_ge(s_kte, 2 * HEADS)
                for n in range(2 * TT):
                    t, kq = n // 2, n % 2
                    pe.wait_ge(s_y, n + 1)
                    for k in range(4):
                        c0 = (4 * kq + k) * P
                        last = nc.tensor.transpose(psA[:, n, k * P:(k + 1) * P], hy_x0[:, t, c0:c0 + P], ident[:])
                    last.then_inc(s_yt, 1)

            @block.vector
            def _(v):
                ch = Chain(v, s_v3)
                for nh, ps in ((0, psA), (1, psB)):
                    v.wait_ge(s_uf, 2)
                    cs = slice(nh * N, (nh + 1) * N)
                    for f in range(TT):
                        re, im, k_re, k_im = ps[:, f, :], ps[:, 2 + f, :], spec[:, f, cs], spec[:, 2 + f, cs]
                        ch.link(nc.vector.tensor_tensor(tmp[:, 0, :], re, k_re, ALU.mult))
                        ch.link(nc.vector.tensor_tensor(tmp[:, 1, :], im, k_im, ALU.mult))
                        ch.link(nc.vector.tensor_tensor(y_re[:, f, cs], tmp[:, 0, :], tmp[:, 1, :], ALU.add))
                        ch.link(nc.vector.tensor_tensor(tmp[:, 0, :], re, k_im, ALU.mult))
                        ch.link(nc.vector.tensor_tensor(tmp[:, 1, :], im, k_re, ALU.mult))
                        ch.link(nc.vector.tensor_tensor(y_im[:, f, cs], tmp[:, 0, :], tmp[:, 1, :], ALU.subtract))
                    v.sem_inc(s_prod, 1)
                v.wait_ge(s_lam, 16)
                for i in range(2):
                    ch.link(nc.vector.tensor_tensor_reduce(tmp[:, 0, 0:HD], lam_in[:, 2 * i, :], lam_in[:, 2 * i + 1, :],
                                                           1.0, 0.0, ALU.mult, ALU.add, lam_sum[:, i:i + 1]))
                v.sem_inc(s_lsum, 1)
                for t in range(TT):
                    for nh in range(2):
                        v.wait_ge(s_inv, 2 * t + nh + 1)
                        cs = slice(nh * N, (nh + 1) * N)
                        nc.vector.tensor_tensor(hy_x0[:, t, cs], psB[:, 2 * t + nh, :], hy_x0[:, t, cs], ALU.mult).then_inc(s_y, 1)
                v.wait_ge(s_lexp, 1)
                ch.link(nc.vector.tensor_tensor(neg_lam, lam_exp[:, 1:2], lam_exp[:, 0:1], ALU.subtract))
                ch.link(nc.vector.tensor_scalar(neg_lam, neg_lam, -LAM_INIT, None, ALU.add))

        o_all = at(168, TT, C)
        with ExitStack() as st:
            probs = at(144, 2, 4, KV)
            aT = at(160, 2, 2 * TT, SEQ)
            stat = at(176, 2, 4, 4)
            squares = at(177, 2 * HEADS)
            o_rstd = at(177.25, 2 * HEADS)
            r_tmp = at(177.5, 2 * HEADS)
            junk = at(178, P)
            subln = at(178.5, P)
            s_sub, s_sc, s_max, s_exp, s_diff, s_at, s_ate, s_pv, s_o, s_v4, s_v4b = (
                sem("s_sub"), sem("s_sc"), sem("s_max"), sem("s_exp"), sem("s_diff"), sem("s_at"), sem("s_ate"),
                sem("s_pv"), sem("s_o"), sem("s_v4"), sem("s_v4b"))
            block = st.enter_context(nc.Block())
            gate_bank = place[PROJECT_END][0]
            SCALE = HD ** -0.5

            @block.sync
            def _(sp):
                sp.dma_start(subln, io["da_subln"][0].partition_broadcast(P)).then_inc(s_sub, 16)
                stream(sp, PROJECT_END + RING, ATTEND_END + RING)

            @block.scalar
            def _(act):
                for h in range(HEADS):
                    for i in range(4):
                        act.wait_ge(s_max, 4 * h + i + 1)
                        nc.scalar.activation(probs[:, h % 2, i, :], psB[:, i, :], ACT.Exp, scale=SCALE,
                                             bias=stat[:, h % 2, 0, i:i + 1],
                                             accum_out=stat[:, h % 2, 1, i:i + 1]).then_inc(s_exp, 1)
                    for t in range(TT):
                        act.wait_ge(s_at, TT * h + t + 1)
                        nc.scalar.activation(aT[:, h % 2, :, t * P:(t + 1) * P],
                                             psB[:, t, :].rearrange("p (k t) -> p k t", k=4), ACT.Copy).then_inc(s_ate, 1)
                    for t in range(TT):
                        act.wait_ge(a_full, gate_bank + TT * h + t + 1)
                        nc.scalar.activation(gates[:, t, h * N:(h + 1) * N], psA[:, (gate_bank + TT * h + t) % 4, :],
                                             ACT.Tanh, scale=0.5).then_inc(a_free, 1)

            @block.tensor
            def _(pe):
                for h in range(HEADS):
                    if h:
                        pe.wait_ge(s_o, TT * h)
                    for i in range(4):
                        comp, t = i // TT, i % TT
                        d0 = comp * HD
                        nc.tensor.matmul(psB[:, i, :], qT[d0:d0 + HD, h, t * P:(t + 1) * P], kT[d0:d0 + HD, h, :],
                                         start=True, stop=True).then_inc(s_sc, 1)
                    n = PROJECT_END + 2 * h
                    gemm_half(pe, n, [lambda k, t=t: uT[:, k, t * P:(t + 1) * P] for t in range(TT)])
                    for t in range(TT):
                        pe.wait_ge(s_diff, TT * h + t + 1)
                        for b in range(4):
                            last = nc.tensor.transpose(psB[:, t, b * P:(b + 1) * P], probs[:, h % 2, t, b * P:(b + 1) * P], ident[:])
                        last.then_inc(s_at, 1)
                    gemm_half(pe, n + 1, [lambda k, t=t: uT[:, KH + k, t * P:(t + 1) * P] for t in range(TT)])
                    for t in range(TT):
                        pe.wait_ge(s_ate, TT * h + t + 1)
                        for b in range(4):
                            last = nc.tensor.matmul(psB[:, 2 + t, 0:P], aT[:, h % 2, b, t * P:(t + 1) * P],
                                                    v_all[:, b, h * P:(h + 1) * P], start=(b == 0), stop=(b == 3))
                        last.then_inc(s_pv, 1)

            @block.vector
            def _(v):
                ch = Chain(v, s_v4)
                for h in range(HEADS):
                    st_ = stat[:, h % 2, :, :]
                    for i in range(4):
                        v.wait_ge(s_sc, 4 * h + i + 1)
                        ch.link(nc.vector.tensor_reduce(st_[:, 0, i:i + 1], psB[:, i, :], AX.X, ALU.max))
                        nc.vector.tensor_scalar(st_[:, 0, i:i + 1], st_[:, 0, i:i + 1], -SCALE, None, ALU.mult).then_inc(s_max, 1)
                    v.wait_ge(s_exp, 4 * h + 4)
                    ch.link(nc.vector.reciprocal(st_[:, 2, :], st_[:, 1, :]))
                    ch.link(nc.vector.tensor_scalar(st_[:, 2, TT:4], st_[:, 2, TT:4], neg_lam, None, ALU.mult))
                    for t in range(TT):
                        one, two = probs[:, h % 2, t, :], probs[:, h % 2, TT + t, :]
                        ch.link(nc.vector.tensor_scalar(one, one, st_[:, 2, t:t + 1], None, ALU.mult))
                        nc.vector.scalar_tensor_tensor(one, two, st_[:, 2, TT + t:TT + t + 1], one, ALU.mult, ALU.add).then_inc(s_diff, 1)
                    for t in range(TT):
                        v.wait_ge(s_pv, TT * h + t + 1)
                        o = o_all[:, t, h * P:(h + 1) * P]
                        nc.vector.tensor_copy(o, psB[:, 2 + t, 0:P]).then_inc(s_o, 1)
                        v.wait_ge(s_o, TT * h + t + 1)
                        ch.link(nc.vector.tensor_tensor_reduce(junk, o, o, 1.0, 0.0, ALU.mult, ALU.add,
                                                               squares[:, t * HEADS + h:t * HEADS + h + 1]))
                ch.link(nc.vector.tensor_scalar(squares, squares, 1.0 / P, EPS, ALU.mult, ALU.add))
                rsqrt(nc, ch, squares, o_rstd, r_tmp)
                v.wait_ge(s_sub, 16)
                ch.link(nc.vector.tensor_scalar(subln, subln, 1.0 - LAM_INIT, None, ALU.mult))
                heads = o_all.rearrange("p t (h d) -> p (t h) d", d=P)
                ch.link(nc.vector.tensor_tensor(heads, heads, o_rstd.unsqueeze(2).broadcast_to((P, 2 * HEADS, P)), ALU.mult))
                ch.link(nc.vector.tensor_tensor(heads, heads, subln.unsqueeze(1).broadcast_to((P, 2 * HEADS, P)), ALU.mult))


        x1 = at(128, TT, D)
        h = at(144, TT, D)
        scores = at(160, TT, HP, N_KEYS)
        g2_row = at(184, D)
        with ExitStack() as st:
            m = at(64, TT, D)
            mT = at(80, KD, SEQ)
            da_part = at(144, TT, N)
            mix = h
            x_in = at(160, TT, D)
            g1_row = at(176, D)
            gain_row = at(112, D)
            shift_row = at(120, D)
            row_tmp = at(196, D)
            hT = at(64, KD, SEQ)
            q = at(80, TT, D)
            q_T = at(112, HP, SEQ)
            keys = at(96, HP, DK_HALF)
            keysT = at(104, HP, N_KEYS)
            rs = small[:, 8:40]
            s_keys, s_kt4, s_kt4e, s_ydt, s_ydte, s_m, s_mt4, s_mte = (
                sem("s_keys"), sem("s_kt4"), sem("s_kt4e"), sem("s_ydt"), sem("s_ydte"), sem("s_m"), sem("s_mt4"), sem("s_mte"))
            s_row, s_rowd, s_xin, s_mix, s_h, s_ht, s_hte, s_q, s_qt, s_qte, s_s, s_se, s_v5 = (
                sem("s_row"), sem("s_rowd"), sem("s_xin"), sem("s_mix"), sem("s_h"), sem("s_ht"), sem("s_hte"), sem("s_q"),
                sem("s_qt"), sem("s_qte"), sem("s_s"), sem("s_se"), sem("s_v5"))
            block = st.enter_context(nc.Block())
            s_rdst = [sem(f"s_rdst{r}") for r in range(4)]
            m_bank = place[ATTEND_END][0]
            o_bank = place[BRANCH_END][0]
            pq_bank = place[OUT_END][0]
            CH = D // N
            ROWS = [(0, 2, "norm_post_mix", g1_row), (1, 3, None, shift_row), (2, 4, "norm_pre_ffn", gain_row),
                    (3, 5, "norm_post_ffn", g2_row)]

            @block.sync
            def _(sp):
                stream(sp, ATTEND_END + RING, ALL_END)

            @block.gpsimd
            def _(pool):
                used = 0
                for r, b, norm, dst in ROWS:
                    if r == 0:
                        pool.wait_ge(a_full, m_bank + 4 * CH - TT)
                    if r == 1:
                        pool.wait_ge(s_m, TT * CH)
                    pool.dma_start(dst, mod_rows[r].partition_broadcast(P)).then_inc(s_rdst[r], 16)
                    if used:
                        pool.wait_ge(s_rowd, used)
                    pool.dma_start(row_tmp, io["b_mod"][0, b * D:(b + 1) * D].partition_broadcast(P)).then_inc(s_row, 16)
                    used += 1
                    if norm:
                        pool.wait_ge(s_rowd, used)
                        pool.dma_start(row_tmp, io[norm][0].partition_broadcast(P)).then_inc(s_row, 16)
                        used += 1

            @block.scalar
            def _(act):
                def evacuate(bank, dst, **how):
                    act.wait_ge(a_full, bank + 1)
                    return nc.scalar.activation(dst, psA[:, bank % 4, :], ACT.Copy, **how).then_inc(a_free, 1)

                for n in range(2 * TT):
                    act.wait_ge(s_ydt, n + 1)
                    t, kq = n // 2, n % 2
                    nc.scalar.activation(y_daT[:, 4 * kq:4 * kq + 4, t * P:(t + 1) * P],
                                         psB[:, n, :].rearrange("p (k t) -> p k t", k=4), ACT.Copy).then_inc(s_ydte, 1)
                act.wait_ge(s_ydt, 4)
                for t in range(TT):
                    act.dma_start(x_in[:, t, :], io["x"][0, t * P:(t + 1) * P, :]).then_inc(s_xin, 16)
                for j in range(CH):
                    for t in range(TT):
                        act.wait_ge(s_mt4, TT * j + t + 1)
                        nc.scalar.activation(mT[:, 4 * j:4 * j + 4, t * P:(t + 1) * P],
                                             psB[:, 2 * (j % 2) + t, :].rearrange("p (k t) -> p k t", k=4),
                                             ACT.Copy, scale=0.5).then_inc(s_mte, 1)
                act.dma_start(keys.rearrange("n (h a) d -> n h a d", a=2)[:, :, 0, :],
                              io["peer_keys"][0, 0].rearrange("h n d -> n h d")).then_inc(s_keys, 16)
                act.dma_start(keys.rearrange("n (h a) d -> n h a d", a=2)[:, :, 1, :],
                              io["peer_keys"][0, 1].rearrange("h n d -> n h d")).then_inc(s_keys, 16)
                for j in range(CH):
                    for t in range(TT):
                        evacuate(o_bank + TT * j + t, mix[:, t, j * N:(j + 1) * N])
                    if j == 0:
                        for n in range(4):
                            act.wait_ge(s_kt4, n + 1)
                            nc.scalar.activation(keysT[:, 4 * n:4 * n + 4, :], psB[:, n, :].rearrange("p (b k) -> p b k", b=4),
                                                 ACT.Copy).then_inc(s_kt4e, 1)
                for n in range(TT * 4):
                    act.wait_ge(s_ht, n + 1)
                    t, kq = n // 4, n % 4
                    nc.scalar.activation(hT[:, 4 * kq:4 * kq + 4, t * P:(t + 1) * P],
                                         psB[:, n % 4, :].rearrange("p (k t) -> p k t", k=4), ACT.Copy).then_inc(s_hte, 1)
                for j in range(CH):
                    for t in range(TT):
                        evacuate(pq_bank + TT * j + t, q[:, t, j * N:(j + 1) * N])
                    for t in range(TT):
                        act.wait_ge(s_qt, TT * j + t + 1)
                        nc.scalar.activation(q_T[:, 4 * j:4 * j + 4, t * P:(t + 1) * P],
                                             psB[:, t, :].rearrange("p (b t) -> p b t", b=4), ACT.Copy).then_inc(s_qte, 1)
                    for t in range(TT):
                        act.wait_ge(s_s, TT * j + t + 1)
                        nc.scalar.activation(scores[:, t, 4 * j:4 * j + 4, :],
                                             psB[:, 2 + t, :].rearrange("p (b k) -> p b k", b=4), ACT.Copy).then_inc(s_se, 1)

            @block.tensor
            def _(pe):
                def part(src, t, half=0):
                    return lambda k: src[:, half * KH + k, t * P:(t + 1) * P]

                def turn(src, t, c0, bank):
                    for k in range(4):
                        last = nc.tensor.transpose(psB[:, bank, k * P:(k + 1) * P], src[:, t, c0 + k * P:c0 + (k + 1) * P], ident[:])
                    return last

                def turn_m(j):
                    for t in range(TT):
                        pe.wait_ge(s_m, TT * j + t + 1)
                        if j >= 2:
                            pe.wait_ge(s_mte, TT * (j - 2) + t + 1)
                        turn(m, t, j * N, 2 * (j % 2) + t).then_inc(s_mt4, 1)

                for n in range(2 * TT):
                    turn(o_all, n // 2, (n % 2) * N, n).then_inc(s_ydt, 1)
                n = ATTEND_END
                for j in range(CH):
                    gemm_half(pe, n, [part(y_hyT, t) for t in range(TT)])
                    if j == 0:
                        pe.wait_ge(s_ydte, 2 * TT)
                    else:
                        turn_m(j - 1)
                    gemm_half(pe, n + 1, [part(y_daT, t) for t in range(TT)])
                    n += 2
                turn_m(CH - 1)
                pe.wait_ge(s_mte, TT * CH)
                for j in range(CH):
                    for half in range(2):
                        gemm_half(pe, n, [part(mT, t, half) for t in range(TT)])
                        n += 1
                    if j == 0:
                        pe.wait_ge(s_keys, 32)
                        for b in range(4):
                            for k in range(4):
                                last = nc.tensor.transpose(psB[:, b, k * P:(k + 1) * P], keys[:, 4 * b + k, :], ident[:])
                            last.then_inc(s_kt4, 1)
                pe.wait_ge(s_kt4e, 4)
                for t in range(TT):
                    pe.wait_ge(s_h, t + 1)
                    for kq in range(4):
                        if t:
                            pe.wait_ge(s_hte, kq + 1)
                        turn(h, t, kq * N, kq).then_inc(s_ht, 1)
                pe.wait_ge(s_hte, 4 * TT)

                def score(j):
                    for t in range(TT):
                        pe.wait_ge(a_free, pq_bank + TT * j + t + 1)
                        turn(q, t, j * N, t).then_inc(s_qt, 1)
                    for t in range(TT):
                        pe.wait_ge(s_qte, TT * j + t + 1)
                        if j:
                            pe.wait_ge(s_se, TT * (j - 1) + t + 1)
                        for k in range(4):
                            b = 4 * j + k
                            last = nc.tensor.matmul(psB[:, 2 + t, k * P:(k + 1) * P], q_T[:, b, t * P:(t + 1) * P], keysT[:, b, :],
                                                    start=True, stop=True)
                        last.then_inc(s_s, 1)

                for j in range(CH):
                    for half in range(2):
                        gemm_half(pe, n, [part(hT, t, half) for t in range(TT)])
                        n += 1
                        if half == 0 and j:
                            score(j - 1)
                score(CH - 1)

            @block.vector
            def _(v):
                ch = Chain(v, s_v5)
                for j in range(CH):
                    cs = slice(j * N, (j + 1) * N)
                    for t in range(TT):
                        hy = m_bank + 4 * j + t
                        v.wait_ge(a_full, hy + 1)
                        ch.link(nc.vector.scalar_tensor_tensor(m[:, t, cs], gates[:, t, cs], 1.0, psA[:, hy % 4, :], ALU.add, ALU.mult))
                        v.sem_inc(a_free, 1)
                    for t in range(TT):
                        da = m_bank + 4 * j + TT + t
                        v.wait_ge(a_full, da + 1)
                        ch.link(nc.vector.scalar_tensor_tensor(da_part[:, t, :], gates[:, t, D + j * N:D + (j + 1) * N], 1.0,
                                                               psA[:, da % 4, :], ALU.add, ALU.mult))
                        v.sem_inc(a_free, 1)
                        nc.vector.tensor_tensor(m[:, t, cs], m[:, t, cs], da_part[:, t, :], ALU.add).then_inc(s_m, 1)
                loads = 0
                for r, b, norm, dst in ROWS:
                    loads += 1
                    v.wait_ge(s_rdst[r], 16)
                    v.wait_ge(s_row, 16 * loads)
                    ch.link(nc.vector.tensor_tensor(dst, dst, row_tmp, ALU.add))
                    v.sem_inc(s_rowd, 1)
                    if norm:
                        loads += 1
                        v.wait_ge(s_row, 16 * loads)
                        one = 1.0 if norm == "norm_pre_ffn" else 0.0
                        ch.link(nc.vector.scalar_tensor_tensor(dst, dst, one, row_tmp, ALU.add, ALU.mult))
                        v.sem_inc(s_rowd, 1)
                v.wait_ge(s_xin, 16 * TT)
                for t in range(TT):
                    ss, r, tmp = rs[:, 0:1], rs[:, 1:2], rs[:, 2:3]
                    v.wait_ge(a_free, o_bank + TT * (CH - 1) + t + 1)
                    ch.link(nc.vector.tensor_tensor_reduce(x1[:, t, :], mix[:, t, :], mix[:, t, :], 1.0, 0.0, ALU.mult, ALU.add, ss))
                    ch.link(nc.vector.tensor_scalar(ss, ss, 1.0 / D, EPS, ALU.mult, ALU.add))
                    rsqrt(nc, ch, ss, r, tmp)
                    ch.link(nc.vector.scalar_tensor_tensor(x1[:, t, :], mix[:, t, :], r, g1_row, ALU.mult, ALU.mult))
                    ch.link(nc.vector.tensor_tensor(x1[:, t, :], x1[:, t, :], x_in[:, t, :], ALU.add))
                    ch.link(nc.vector.tensor_tensor_reduce(h[:, t, :], x1[:, t, :], x1[:, t, :], 1.0, 0.0, ALU.mult, ALU.add, ss))
                    ch.link(nc.vector.tensor_scalar(ss, ss, 1.0 / D, EPS, ALU.mult, ALU.add))
                    rsqrt(nc, ch, ss, r, tmp)
                    ch.link(nc.vector.scalar_tensor_tensor(h[:, t, :], x1[:, t, :], r, gain_row, ALU.mult, ALU.mult))
                    nc.vector.tensor_tensor(h[:, t, :], h[:, t, :], shift_row, ALU.add).then_inc(s_h, 1)

        with ExitStack() as st:
            slots = at(0, SLOTS, D)
            total = at(176, D)
            s_key = at(192, 2, 2, N_KEYS)
            cand = at(194, N_KEYS * 2)
            hot = at(195, TOPK, TOPK)
            iota = at(196, TOPK)
            top_v = at(196.25, 2, TOPK)
            top_vu = at(196.5, 2, TOPK).bitcast(U32)
            top_vf = at(196.75, 2, TOPK)
            best = at(197, 2, TOPK)
            best_u = at(197.25, TOPK).bitcast(U32)
            ab_u = at(197.5, 2, TOPK).bitcast(U32)
            ab = at(197.75, 2, TOPK)
            pick = at(198, 2, TOPK)
            rows = at(198.25, 2, TOPK).bitcast(U32)
            neg_max = at(198.5, 2)
            e_sum = at(198.75, 2, 2)
            e_g = at(199, 2, TOPK)
            dots = at(199.25, 2, TOPK)
            act_ = at(199.5, 2, TOPK)
            wgt = at(199.75, 2, TOPK)
            rs = at(200, 4)
            s_iota = sem("s_iota")
            s_row_idx, s_gathers = sem("s_row_idx"), sem("s_gathers")
            s_slot = [sem(f"s_slot{i}") for i in range(SLOTS)]
            s_used, s_nmax, s_eg, s_dots, s_gelu, s_v6, s_top, s_vsum, s_out = (
                sem("s_used"), sem("s_nmax"), sem("s_eg"), sem("s_dots"), sem("s_gelu"), sem("s_v6"), sem("s_top"),
                sem("s_vsum"), sem("s_out"))
            s_done, s_step = sem("s_done"), sem("s_step")
            block = st.enter_context(nc.Block())
            u_tab, v_tab = io["peer_u"][0], io["peer_v"][0]
            PAIRS = PEER_HEADS // 2

            @block.gpsimd
            def _(pool):
                pool.dma_start(iota, io["k_iota"]).then_inc(s_iota, 16)
                pool.sem_inc(s_used, SLOTS)
                with pool.Fori(0, TT * PAIRS) as pair:
                    for par in range(2):
                        head = 2 * pair + par
                        pool.wait_ge(s_row_idx, head + 1)
                        pool.sem_inc(s_gathers, 1)
                        for table in (u_tab, v_tab):
                            for j in range(TOPK):
                                pool.wait_ge(s_used, head * 2 * TOPK + (TOPK if table is v_tab else 0) + j + 1)
                                pool.sem_inc(s_gathers, 1)
                                nc.gpsimd.indirect_dma_start(
                                    out=slots[:, j, :], out_offset=None, in_=table,
                                    in_offset=bass.IndirectOffsetOnAxis(ap=rows[:, par, j:j + 1], axis=0)).then_inc(s_slot[j], 16)

            @block.scalar
            def _(act):
                with act.Fori(0, TT * PAIRS) as pair:
                    for par in range(2):
                        head = 2 * pair + par
                        act.wait_ge(s_nmax, head + 1)
                        nc.scalar.activation(e_g[:, par, :], best[:, par, :], ACT.Exp, bias=neg_max[:, par:par + 1],
                                             accum_out=e_sum[:, par, 0:1]).then_inc(s_eg, 1)
                        act.wait_ge(s_dots, head + 1)
                        nc.scalar.activation(act_[:, par, :], dots[:, par, :], ACT.Gelu).then_inc(s_gelu, 1)

            @block.vector
            def _(v):
                TOP_LINKS = 27
                all_scores = scores.rearrange("p t b k -> p (t b) k")

                def top16(ch, values, out_v, out_i):
                    ch.link(nc.vector.max(out=out_v[:, 0:8], in_=values), s_step)
                    ch.link(nc.vector.max_index(out=out_i[:, 0:8], in_max=out_v[:, 0:8], in_values=values), s_step)
                    ch.link(nc.vector.match_replace(out=values, in_to_replace=out_v[:, 0:8], in_values=values, imm_value=LOWEST), s_step)
                    ch.link(nc.vector.max(out=out_v[:, 8:16], in_=values), s_step)
                    ch.link(nc.vector.max_index(out=out_i[:, 8:16], in_max=out_v[:, 8:16], in_values=values), s_step)

                def choose(head, par):
                    ch = Chain(v, s_top, head * TOP_LINKS)
                    ch.link(nc.vector.tensor_copy(s_key[:, par, :, :], all_scores[:, bass.ds(2 * head, 2), :]), s_step)
                    for i in range(2):
                        top16(ch, s_key[:, par, i, :], top_v[:, i, :], top_vu[:, i, :])
                    ch.link(nc.vector.tensor_copy(top_vf, top_vu))
                    a_side = top_v[:, 0, :].unsqueeze(2).broadcast_to((P, TOPK, TOPK))
                    b_side = top_v[:, 1, :].unsqueeze(1).broadcast_to((P, TOPK, TOPK))
                    ch.link(nc.vector.tensor_tensor(cand.rearrange("p (a b) -> p a b", b=TOPK), a_side, b_side, ALU.add), s_step)
                    top16(ch, cand, best[:, par, :], best_u)
                    nc.vector.tensor_scalar(neg_max[:, par:par + 1], best[:, par, 0:1], -1.0, None, ALU.mult).then_inc(s_nmax, 1)
                    ch.link(nc.vector.tensor_scalar(ab_u[:, 0, :], best_u, 4, None, ALU.logical_shift_right))
                    ch.link(nc.vector.tensor_scalar(ab_u[:, 1, :], best_u, TOPK - 1, None, ALU.bitwise_and))
                    ch.link(nc.vector.tensor_copy(ab, ab_u))
                    for i in range(2):
                        where = ab[:, i, :].unsqueeze(2).broadcast_to((P, TOPK, TOPK))
                        numbers = iota.unsqueeze(1).broadcast_to((P, TOPK, TOPK))
                        of_key = top_vf[:, i, :].unsqueeze(1).broadcast_to((P, TOPK, TOPK))
                        ch.link(nc.vector.tensor_tensor(hot, where, numbers, ALU.is_equal))
                        ch.link(nc.vector.tensor_tensor(hot, hot, of_key, ALU.mult))
                        ch.link(nc.vector.tensor_reduce(pick[:, i, :], hot, AX.X, ALU.add))
                    nc.vector.scalar_tensor_tensor(rows[:, par, :], pick[:, 0, :], float(N_KEYS), pick[:, 1, :],
                                                   ALU.mult, ALU.add).then_inc(s_row_idx, 1)
                    assert ch.n == TOP_LINKS, ch.n

                def multiply(head, t, par):
                    for j in range(TOPK):
                        v.wait_ge(s_slot[j], 32 * head + 16)
                        nc.vector.tensor_tensor_reduce(slots[:, j, :], slots[:, j, :], h[:, t, :], 1.0, 0.0, ALU.mult, ALU.add,
                                                       dots[:, par, j:j + 1]).then_inc(s_used, 1)
                    v.wait_ge(s_used, head * 2 * TOPK + TOPK + SLOTS)
                    v.sem_inc(s_dots, 1)

                def add_up(head, par):
                    v.wait_ge(s_eg, head + 1)
                    ch = Chain(v, s_v6, head * 3)
                    ch.link(nc.vector.reciprocal(e_sum[:, par, 1:2], e_sum[:, par, 0:1]))
                    ch.link(nc.vector.tensor_scalar(e_g[:, par, :], e_g[:, par, :], e_sum[:, par, 1:2], None, ALU.mult))
                    v.wait_ge(s_gelu, head + 1)
                    ch.link(nc.vector.tensor_tensor(wgt[:, par, :], e_g[:, par, :], act_[:, par, :], ALU.mult))
                    for j in range(TOPK):
                        v.wait_ge(s_slot[j], 32 * head + 32)
                        nc.vector.scalar_tensor_tensor(total, slots[:, j, :], wgt[:, par, j:j + 1], total, ALU.mult, ALU.add).then_inc(s_used, 1)
                        v.wait_ge(s_used, head * 2 * TOPK + TOPK + j + 1 + SLOTS)

                v.wait_ge(s_iota, 16)
                choose(0, 0)
                end = Chain(v, s_vsum)
                for t in range(TT):
                    end.link(nc.vector.memset(total, 0.0))
                    def two_heads(pair, last=False):
                        for par in range(2):
                            head = 2 * pair + par
                            multiply(head, t, par)
                            if not (last and par == 1):
                                choose(head + 1, 1 - par)
                            add_up(head, par)

                    first = t * PAIRS
                    end_pair = first + PAIRS
                    if t < TT - 1:
                        with v.Fori(first, end_pair) as pair:
                            two_heads(pair)
                    else:
                        with v.Fori(first, end_pair - 1) as pair:
                            two_heads(pair)
                        two_heads(end_pair - 1, last=True)
                    ss, r, tmp = rs[:, 0:1], rs[:, 1:2], rs[:, 2:3]
                    res = x1[:, t, :]
                    sq = h[:, t, :]
                    end.link(nc.vector.tensor_tensor_reduce(sq, total, total, 1.0, 0.0, ALU.mult, ALU.add, ss))
                    end.link(nc.vector.tensor_scalar(ss, ss, 1.0 / D, EPS, ALU.mult, ALU.add))
                    rsqrt(nc, end, ss, r, tmp)
                    end.link(nc.vector.scalar_tensor_tensor(total, total, r, g2_row, ALU.mult, ALU.mult))
                    nc.vector.tensor_tensor(res, res, total, ALU.add).then_inc(s_vsum, 1)
                    end.n += 1
                    v.wait_ge(s_vsum, end.n)
                    v.sem_inc(s_done, 1)

            @block.sync
            def _(sp):
                for t in range(TT):
                    sp.wait_ge(s_done, t + 1)
                    sp.dma_start(out[0, t * P:(t + 1) * P, :], x1[:, t, :]).then_inc(s_out, 16)
                sp.wait_ge(s_out, 16 * TT)



_INS = ["x", "c", "ctx", "c_ctx", "w_mod", "b_mod", "norm_pre_mix", "norm_post_mix", "norm_pre_ffn", "norm_post_ffn",
        "w_in", "hy_conv_w", "hy_conv_b", "filt_w1", "filt_b1", "filt_w2", "filt_b2", "filt_w3", "filt_b3",
        "filt_w_out", "filt_freq", "hy_bias", "da_lambda", "da_subln", "w_hy_out", "w_da_out", "w_o",
        "peer_w_q", "peer_keys", "peer_u", "peer_v"]


def kernel(**inputs):
    import numpy as _np
    import concourse.bacc as _bacc
    from concourse import mybir as _mybir
    from concourse.bass_utils import run_bass_kernel_spmd as _run

    nc = _bacc.Bacc("TRN2", target_bir_lowering=False, num_devices=1)
    arrays, io = {}, {}
    for name, a in [(n, inputs[n]) for n in _INS] + list(constants().items()):
        a = _np.ascontiguousarray(a)
        arrays[f"in_{name}_dram"] = a
        io[name] = nc.dram_tensor(f"in_{name}_dram", a.shape, _mybir.dt.from_np(a.dtype), kind="ExternalInput").ap()
    out = nc.dram_tensor("out_0_dram", (1, SEQ, D), F32, kind="ExternalOutput").ap()
    build(nc, io, out)
    r = _run(nc, [arrays], core_ids=[0])
    return r.results[0]["out_0_dram"]
```

```python
from contextlib import ExitStack
import math

import numpy as np

import concourse.bass as bass
from concourse import mybir

F32 = mybir.dt.float32
U32 = mybir.dt.uint32
I32 = mybir.dt.int32
ALU = mybir.AluOpType
ACT = mybir.ActivationFunctionType
AX = mybir.AxisListType

P = 128
ARENA_KB = 204
D = 2048
SEQ = 256
CTX = 256
TT = SEQ // P
KD = D // P
C = D // 2
KC = C // P
GRID_W = 64
EPS = 1e-6
HEADS = 8
HD = 64
KV = CTX + SEQ
Q_OFF = 3 * C
K_OFF = Q_OFF + C
V_OFF = K_OFF + C
GATE_OFF = V_OFF + C
IN_COLS = GATE_OFF + 2 * D
N_MOD = 6
LAM_INIT = 0.8 - 0.6 * math.exp(0.0)
FILT_EMB = 33
FILT_ORDER = 64
PEER_HEADS = 8
N_KEYS = 128
N_EXPERTS = N_KEYS * N_KEYS
TOPK = 16
DK_HALF = 128
HP = 2 * PEER_HEADS
N = 512
KH = 8
RING = 4
SLOTS = 16
LOWEST = -3.0e38
TWO_PI_HI = 6.28125
TWO_PI_LO = 2.0 * math.pi - 6.28125
ROUND = 1.5 * 2.0 ** 23
MODULATE_END = 2 * (2 * D // N)
PROJECT_END = MODULATE_END + 2 * (2 * C // N) + 2 * (4 * C // N)
ATTEND_END = PROJECT_END + 2 * (2 * D // N)
BRANCH_END = ATTEND_END + 2 * (D // N)
OUT_END = BRANCH_END + 2 * (D // N)
ALL_END = OUT_END + 2 * (D // N)
HY_Q_ORDER = (0, 1, 2, 6, 3, 4, 5, 7)
V_C, V_CCTX, V_NORM, V_BSH, V_BSC = 0, 16, 32, 48, 64


def constants():
    f64 = np.float64
    t = np.arange(SEQ, dtype=f64)
    freq = np.arange(SEQ, dtype=f64) + 0.5
    ang = 2.0 * np.pi * np.outer(t, freq) / (2 * SEQ)
    scale = 2.0 / (2 * SEQ)
    bands_n = (FILT_EMB - 1) // 2
    tl = np.linspace(0.0, 1.0, SEQ)[:, None]
    w = 2.0 * math.pi * t[:, None] / SEQ
    bands = np.linspace(1e-4, bands_n - 1, bands_n)[None, :]
    z = np.concatenate([tl, np.cos(bands * w), -np.sin(bands * w)], axis=-1)
    deltas = np.abs(np.linspace(math.log(1e-2) / 1.5, math.log(1e-2) / 0.3, C))
    window = np.exp(-tl * deltas[None, :]) + 0.05
    window_b = window.copy()
    window_b[0] = 0.0
    half = HD // 4
    inv = 10000.0 ** (-np.arange(half, dtype=f64) / half)
    row = np.repeat(np.arange(SEQ // GRID_W), GRID_W)[:, None] * inv
    col = np.tile(np.arange(GRID_W), SEQ // GRID_W)[:, None] * inv
    cos = np.concatenate([np.cos(row), np.cos(row), np.cos(col), np.cos(col)], axis=1)
    sin = np.concatenate([-np.sin(row), np.sin(row), -np.sin(col), np.sin(col)], axis=1)
    f = lambda a: np.ascontiguousarray(a, dtype=np.float32)
    return {
        "k_ident": f(np.eye(P)), "k_cos": f(np.cos(ang)), "k_sin": f(np.sin(ang)),
        "k_icos": f(scale * np.cos(ang).T), "k_isin": f(-scale * np.sin(ang).T),
        "k_zT": f(z.T), "k_window": f(window), "k_window_b": f(window_b),
        "k_rope_cos": f(cos), "k_rope_sin": f(sin),
        "k_iota": f(np.tile(np.arange(TOPK), (P, 1))),
    }


def chunks():
    halves = []

    def full(name, col, banks):
        halves.append((name, 0, col, True, False, banks))
        halves.append((name, KH * P, col, False, True, banks))
    for j in range(2 * D // N):
        full("w_mod", j * N, 1)
    for j in range(2 * C // N):
        full("w_in", K_OFF + j * N, 2 * TT)
    for j in HY_Q_ORDER:
        full("w_in", j * N, TT)
    for j in range(2 * D // N):
        full("w_in", GATE_OFF + j * N, TT)
    for j in range(D // N):
        halves.append(("w_hy_out", 0, j * N, True, True, TT))
        halves.append(("w_da_out", 0, j * N, True, True, TT))
    for name in ("w_o", "peer_w_q"):
        for j in range(D // N):
            full(name, j * N, TT)
    return halves


def uses(halves):
    bank, partial, found = 0, 0, []
    for _, _, _, _, ends, banks in halves:
        if ends:
            found.append((bank, 1, bank + banks))
            bank += banks
        else:
            partial += 1
            found.append((bank, 0, partial))
    return found


class Chain:

    def __init__(self, eng, sem, base=0):
        self.eng, self.sem, self.base, self.n = eng, sem, base, 0

    def link(self, ins, then=None):
        ins.then_inc(self.sem, 1)
        self.n += 1
        self.eng.wait_ge(self.sem, self.base + self.n)
        if then is not None:
            self.eng.sem_inc(then, 1)


def rsqrt(nc, ch, x, y, tmp):
    ch.link(nc.vector.tensor_scalar(tmp.bitcast(I32), x.bitcast(I32), 1, None, ALU.logical_shift_right))
    ch.link(nc.vector.tensor_scalar(y.bitcast(I32), tmp.bitcast(I32), -1.0, 1597463007.0, ALU.mult, ALU.add))
    for _ in range(4):
        ch.link(nc.vector.tensor_tensor(tmp, x, y, ALU.mult))
        ch.link(nc.vector.tensor_tensor(tmp, tmp, y, ALU.mult))
        ch.link(nc.vector.tensor_scalar(tmp, tmp, -0.5, 1.5, ALU.mult, ALU.add))
        ch.link(nc.vector.tensor_tensor(y, y, tmp, ALU.mult))


def build(nc, io, out):
    with ExitStack() as whole:
        def sem(name):
            return whole.enter_context(nc.semaphore(name))

        def scratch(name, shape):
            return nc.dram_tensor(name, shape, F32).ap()

        mod_rows = scratch("mod_rows", (4, D))
        filt_spec = scratch("filt_spec", (P, 4, C))
        shifted = scratch("shifted", (SEQ + 2, 3 * C))

        psA = whole.enter_context(nc.psum_tensor("psA", [P, 4, N], F32))
        psB = whole.enter_context(nc.psum_tensor("psB", [P, 4, N], F32))
        arena = whole.enter_context(nc.sbuf_tensor("arena", [P, ARENA_KB * 256], F32))
        ident = whole.enter_context(nc.sbuf_tensor("ident", [P, P], F32))
        ones = whole.enter_context(nc.sbuf_tensor("ones", [P, 1], F32))
        cols = whole.enter_context(nc.sbuf_tensor("cols", [P, 80], F32))
        small = whole.enter_context(nc.sbuf_tensor("small", [P, 8 + 4 * HD], F32))

        def at(kb, *shape):
            size = int(np.prod(shape))
            flat = arena[:, int(kb * 256):int(kb * 256) + size]
            if len(shape) == 1:
                return flat
            names = "abcd"[:len(shape)]
            return flat.rearrange(f"p ({' '.join(names)}) -> p {' '.join(names)}",
                                  **dict(zip(names[1:], shape[1:])))

        ring = at(0, RING, KH, N)
        uT = at(64, KD, SEQ)
        uctxT = at(80, KD, CTX)
        kT = at(80, HEADS, KV)
        v_all = at(96, 2 * TT, C)
        k_all = at(112, 2 * TT, C)
        q_lat = at(128, TT, C)
        hy_u = at(136, TT, C)
        hy_x0 = at(144, TT, C)
        qT = at(188, HEADS, SEQ)
        y_hyT = at(196, KC, SEQ)
        gates = at(112, TT, 2 * D)
        y_daT = at(96, KC, SEQ)

        w_landed = [sem(f"w_landed{i}") for i in range(RING)]
        w_used = sem("w_used")
        a_full = sem("a_full")
        a_free = sem("a_free")
        halves = chunks()
        place = uses(halves)

        def stream(sp, first, upto):
            for n in range(first, upto):
                name, row, col = halves[n][:3]
                if n >= RING:
                    _, which, value = place[n - RING]
                    sp.wait_ge((w_used, a_full)[which], value)
                src = io[name][0, row:row + KH * P, col:col + N].rearrange("(k p) n -> p k n", p=P)
                sp.dma_start(ring[:, n % RING, :, :], src).then_inc(w_landed[n % RING], 16)

        def gemm_half(pe, n, lefts, only=None):
            _, _, _, begins, ends, banks = halves[n]
            bank, which, _ = place[n]
            assert banks == len(lefts)
            pe.wait_ge(w_landed[n % RING], 16 * (n // RING + 1))
            for b, left in enumerate(lefts, bank):
                if only is not None and b != bank + only:
                    continue
                if begins and b >= 4:
                    pe.wait_ge(a_free, b - 3)
                for k in range(KH):
                    last = nc.tensor.matmul(psA[0:left(k).shape[1], b % 4, :], left(k), ring[:, n % RING, k, :],
                                            start=begins and k == 0, stop=ends and k == KH - 1)
                if ends:
                    last.then_inc(a_full, 1)
            if not ends and only in (None, banks - 1):
                last.then_inc(w_used, 1)

        def gemm_chunk_by_tile(pe, n, src):
            for t in range(TT):
                for half in range(2):
                    gemm_half(pe, n + half, [lambda k, t=t, half=half: src[:, half * KH + k, t * P:(t + 1) * P]] * TT, only=t)

        x_rows = [io["x"][0, 0:P, :], io["x"][0, P:SEQ, :], io["ctx"][0, 0:P, :], io["ctx"][0, P:CTX, :]]
        with ExitStack() as st:
            xin = at(96, 4, D)
            mod_row = at(128, 2 * D)[0:2]
            bias_row = mod_row[0:1, 3 * C:4 * C]
            filt = at(144, 2, TT, C)
            spec = at(160, 4, C)
            window = at(176, 2, C)
            fwout = at(184, 2 * C)[0:FILT_ORDER]
            dft = at(192, 2, TT, SEQ)
            vecs = at(196, P)
            zT = at(196.5, SEQ)[0:FILT_EMB]
            arg = at(197.5, 2, SEQ)[0:FILT_ORDER]
            feat = at(199.5, 2, SEQ)[0:FILT_ORDER]
            fw1 = at(201.5, FILT_ORDER)[0:FILT_EMB]
            fw23 = at(201.75, 2, FILT_ORDER)[0:FILT_ORDER]
            fcol = at(202.25, 4)[0:FILT_ORDER]
            shift = at(202.75, 2, KD)
            gain = at(203, 2, KD)
            rstd = at(203.25, 4)
            rtmp = at(203.5, 2)

            s_vec, s_x, s_con, s_flt = sem("s_vec"), [sem(f"s_x{i}") for i in range(4)], sem("s_con"), sem("s_flt")
            s_win = sem("s_win")
            s_silu, s_cols, s_colsb = sem("s_silu"), sem("s_cols"), sem("s_colsb")
            s_norm, s_xt, s_xe = sem("s_norm"), sem("s_xt"), sem("s_xe")
            s_mt, s_mod, s_fp, s_fa, s_fs = sem("s_mt"), sem("s_mod"), sem("s_fp"), sem("s_fa"), sem("s_fs")
            s_v1, s_hf, s_sp, s_spe, s_spo, s_ones = (sem("s_v1"), sem("s_hf"), sem("s_sp"), sem("s_spe"),
                                                     sem("s_spo"), sem("s_ones"))
            s_wo2, s_gain = sem("s_wo2"), sem("s_gain")
            block = st.enter_context(nc.Block())

            @block.sync
            def _(sp):
                sp.dma_start(vecs[V_C:V_C + 16, :], io["c"].rearrange("a (k p) -> (a k) p", p=P)).then_inc(s_vec, 16)
                sp.dma_start(vecs[V_CCTX:V_CCTX + 16, :], io["c_ctx"].rearrange("(k p) -> k p", p=P)).then_inc(s_vec, 16)
                sp.dma_start(vecs[V_NORM:V_NORM + 16, :], io["norm_pre_mix"].rearrange("a (k p) -> (a k) p", p=P)).then_inc(s_vec, 16)
                sp.dma_start(vecs[V_BSH:V_BSH + 32, :],
                             io["b_mod"][:, 0:2 * D].rearrange("a (k p) -> (a k) p", p=P)).then_inc(s_vec, 16)
                sp.dma_start(ident[:], io["k_ident"]).then_inc(s_con, 16)
                stream(sp, 0, RING)
                for i in range(4):
                    sp.dma_start(xin[:, i, :], x_rows[i]).then_inc(s_x[i], 16)
                    if i == 1:
                        stream(sp, RING, RING + 2)
                stream(sp, RING + 2, MODULATE_END + RING)

            @block.scalar
            def _(act):
                act.dma_start(zT[:], io["k_zT"]).then_inc(s_flt, 16)
                act.dma_start(fw1[:], io["filt_w1"][0]).then_inc(s_flt, 16)
                act.dma_start(fw23[:, 0, :], io["filt_w2"][0]).then_inc(s_flt, 16)
                act.dma_start(fw23[:, 1, :], io["filt_w3"][0]).then_inc(s_flt, 16)
                act.dma_start(fwout[:], io["filt_w_out"][0]).then_inc(s_flt, 16)
                for j, name in enumerate(("filt_b1", "filt_b2", "filt_b3", "filt_freq")):
                    act.dma_start(fcol[:, j:j + 1], io[name].rearrange("a f -> f a")).then_inc(s_flt, 16)
                act.dma_start(bias_row[:], io["hy_bias"]).then_inc(s_flt, 16)
                act.dma_start(dft[:, 0, :, :], io["k_cos"].rearrange("(t p) f -> p t f", p=P)).then_inc(s_flt, 16)
                act.dma_start(dft[:, 1, :, :], io["k_sin"].rearrange("(t p) f -> p t f", p=P)).then_inc(s_flt, 16)
                act.wait_ge(s_vec, 64)
                nc.scalar.activation(vecs[0:32, :], vecs[0:32, :], ACT.Silu).then_inc(s_silu, 1)
                for layer in range(3):
                    act.wait_ge(s_fa, layer + 1)
                    nc.scalar.activation(feat[:, layer % 2, :], arg[:, 0, :], ACT.Sin).then_inc(s_fs, 1)
                for i in range(4):
                    dst = uT if i < 2 else uctxT
                    for kq in range(4):
                        n = 4 * i + kq
                        act.wait_ge(s_xt, n + 1)
                        nc.scalar.activation(dst[:, 4 * kq:4 * kq + 4, (i % 2) * P:(i % 2) * P + P],
                                             psB[:, n % 2, :].rearrange("p (k t) -> p k t", k=4),
                                             ACT.Copy).then_inc(s_xe, 1)
                for m in range(8):
                    act.wait_ge(s_sp, m + 1)
                    part, nh = m // 2, m % 2
                    nc.scalar.activation(spec[:, part, nh * N:(nh + 1) * N], psB[:, m % 4, :], ACT.Copy).then_inc(s_spe, 1)
                act.wait_ge(s_spe, 8)
                act.dma_start(filt_spec, spec[:]).then_inc(s_spo, 16)
                for q in range(4):
                    act.wait_ge(s_gain, q + 1)
                    for k in range(4 * q, 4 * q + 4):
                        nc.scalar.activation(uctxT[:, k, :], uctxT[:, k, :], ACT.Identity, scale=gain[:, 1, k:k + 1],
                                             bias=shift[:, 1, k:k + 1]).then_inc(s_mod, 1)
                act.wait_ge(s_spo, 16)

            @block.gpsimd
            def _(pool):
                nc.gpsimd.memset(ones[:], 1.0).then_inc(s_ones, 1)
                for t in range(TT):
                    if t:
                        pool.wait_ge(s_hf, 4)
                    pool.dma_start(window[:, 0, :], io["k_window"][t * P:(t + 1) * P, :]).then_inc(s_win, 16)
                    pool.dma_start(window[:, 1, :], io["k_window_b"][t * P:(t + 1) * P, :]).then_inc(s_win, 16)

            @block.tensor
            def _(pe):
                pe.wait_ge(s_con, 16)
                pe.wait_ge(s_silu, 1)
                nc.tensor.transpose(psB[:, 2, 0:80], vecs[0:80, :], ident[0:80, 0:80]).then_inc(s_cols, 1)

                def filter_layer(layer):
                    if layer == 0:
                        pe.wait_ge(s_flt, 16 * 12)
                        left, right = fw1, zT
                    else:
                        pe.wait_ge(s_fs, layer)
                        left, right = fw23[:, layer - 1, :], feat[:, (layer - 1) % 2, :]
                    nc.tensor.matmul(psB[0:FILT_ORDER, 3, 0:SEQ], left, right, start=True, stop=True).then_inc(s_fp, 1)

                def transpose_x(i):
                    pe.wait_ge(s_norm, i + 1)
                    for kq in range(4):
                        n = 4 * i + kq
                        if n >= 2:
                            pe.wait_ge(s_xe, n - 1)
                        for k in range(4 * kq, 4 * kq + 4):
                            m = nc.tensor.transpose(psB[:, n % 2, (k % 4) * P:(k % 4) * P + P],
                                                    xin[:, i, k * P:(k + 1) * P], ident[:])
                        m.then_inc(s_xt, 1)

                def filter_out(t):
                    if t:
                        pe.wait_ge(s_hf, 4)
                    else:
                        pe.wait_ge(s_fs, 3)
                        pe.wait_ge(s_xe, 16)
                    for j in range(4):
                        nc.tensor.matmul(psB[:, j, :], feat[:, 0, t * P:(t + 1) * P], fwout[:, j * N:(j + 1) * N],
                                         start=True, stop=True).then_inc(s_wo2, 1)

                def filter_spectrum():
                    pe.wait_ge(s_hf, 8)
                    for part in range(4):
                        for nh in range(2):
                            q = 2 * part + nh
                            if q >= 4:
                                pe.wait_ge(s_spe, q - 3)
                            f0 = (part % 2) * P
                            for t in range(TT):
                                m = nc.tensor.matmul(psB[:, q % 4, :], dft[:, part // 2, t, f0:f0 + P],
                                                     filt[:, part // 2, t, nh * N:(nh + 1) * N],
                                                     start=(t == 0), stop=(t == TT - 1))
                            m.then_inc(s_sp, 1)

                def rows_to_columns(first, upto):
                    pe.wait_ge(a_free, upto)
                    pe.wait_ge(s_spe, 8)
                    for j in range(4 * first, 4 * upto):
                        m = nc.tensor.transpose(psB[:, 0, 2 * j:2 * j + 2], mod_row[:, j * P:(j + 1) * P], ident[0:2, 0:2])
                    m.then_inc(s_mt, 1)

                pe.wait_ge(s_colsb, 1)
                for n in range(MODULATE_END):
                    gemm_half(pe, n, [lambda k, hf=n % 2: cols[:, hf * KH + k:hf * KH + k + 17:16]])
                    if n in (1, 2, 3):
                        filter_layer(n - 1)
                    if n in (4, 5, 6, 7):
                        transpose_x(n - 4)
                    if n in (8, 9):
                        filter_out(n - 8)
                    if n == 10:
                        filter_spectrum()
                    if n == 13:
                        rows_to_columns(0, 6)
                    if n == 14:
                        rows_to_columns(6, 7)
                    if n == 15:
                        rows_to_columns(7, 8)

            @block.vector
            def _(v):
                ch = Chain(v, s_v1)
                v.wait_ge(s_cols, 1)
                nc.vector.tensor_copy(cols[:, 0:80], psB[:, 2, 0:80]).then_inc(s_colsb, 1)

                def sine_argument(layer):
                    v.wait_ge(s_flt, 16 * 12)
                    v.wait_ge(s_fp, layer + 1)
                    ch.link(nc.vector.tensor_scalar(arg[:, 0, :], psB[0:FILT_ORDER, 3, 0:SEQ], fcol[:, layer:layer + 1],
                                                    fcol[:, 3:4], ALU.add, ALU.mult))
                    ch.link(nc.vector.tensor_scalar(arg[:, 1, :], arg[:, 0, :], 0.5 / math.pi, ROUND, ALU.mult, ALU.add))
                    ch.link(nc.vector.tensor_scalar(arg[:, 1, :], arg[:, 1, :], -ROUND, None, ALU.add))
                    ch.link(nc.vector.scalar_tensor_tensor(arg[:, 0, :], arg[:, 1, :], -TWO_PI_HI, arg[:, 0, :], ALU.mult, ALU.add))
                    ch.link(nc.vector.scalar_tensor_tensor(arg[:, 0, :], arg[:, 1, :], -TWO_PI_LO, arg[:, 0, :], ALU.mult, ALU.add))
                    nc.vector.tensor_scalar(arg[:, 0, :], arg[:, 0, :], 3.1415925, -3.1415925, ALU.min, ALU.max).then_inc(s_fa, 1)

                def normalise(i):
                    v.wait_ge(s_x[i], 16)
                    ch.link(nc.vector.tensor_tensor_reduce(spec[:, 0:2, :].rearrange("p a c -> p (a c)"), xin[:, i, :],
                                                           xin[:, i, :], 1.0, 0.0, ALU.mult, ALU.add, rstd[:, i:i + 1]))
                    ch.link(nc.vector.tensor_scalar(rstd[:, i:i + 1], rstd[:, i:i + 1], 1.0 / D, EPS, ALU.mult, ALU.add))
                    rsqrt(nc, ch, rstd[:, i:i + 1], rtmp[:, 0:1], rtmp[:, 1:2])
                    nc.vector.tensor_scalar(xin[:, i, :], xin[:, i, :], rtmp[:, 0:1], None, ALU.mult).then_inc(s_norm, 1)

                def window_filter(t):
                    v.wait_ge(s_win, 32 * (t + 1))
                    for nh in range(2):
                        cs = slice(nh * N, (nh + 1) * N)
                        v.wait_ge(s_wo2, 4 * t + nh + 3)
                        ch.link(nc.vector.tensor_tensor(window[:, 1, cs], psB[:, 2 + nh, :], window[:, 1, cs], ALU.mult))
                        ch.link(nc.vector.tensor_tensor(window[:, 0, cs], psB[:, nh, :], window[:, 0, cs], ALU.mult))
                        nc.vector.tensor_tensor(filt[:, 0, t, cs], window[:, 0, cs], window[:, 1, cs], ALU.add).then_inc(s_hf, 1)
                        nc.vector.tensor_tensor(filt[:, 1, t, cs], window[:, 1, cs], window[:, 0, cs], ALU.subtract).then_inc(s_hf, 1)
                    if t == 0:
                        v.wait_ge(s_hf, 4)
                        ch.link(nc.vector.tensor_tensor(filt[0:1, 0, 0, :], filt[0:1, 0, 0, :], bias_row[:], ALU.add))

                def keep_rows(j):
                    v.wait_ge(a_full, j + 1)
                    nc.vector.tensor_copy(mod_row[:, j * N:(j + 1) * N], psA[0:2, j % 4, :]).then_inc(a_free, 1)

                mc = psB[:, 0, 0:4 * KD].rearrange("p (j r) -> p j r", r=2)

                def scale(q0, q1, with_shift):
                    ks = slice(4 * q0, 4 * q1)
                    for r in range(2):
                        if with_shift:
                            ch.link(nc.vector.tensor_tensor(shift[:, r, :], mc[:, 0:KD, r], cols[:, V_BSH:V_BSH + KD], ALU.add))
                        ch.link(nc.vector.tensor_tensor(gain[:, r, ks], mc[:, KD + 4 * q0:KD + 4 * q1, r],
                                                        cols[:, V_BSC + 4 * q0:V_BSC + 4 * q1], ALU.add))
                        ch.link(nc.vector.scalar_tensor_tensor(gain[:, r, ks], gain[:, r, ks], 1.0,
                                                               cols[:, V_NORM + 4 * q0:V_NORM + 4 * q1], ALU.add, ALU.mult))
                    v.sem_inc(s_gain, q1 - q0)
                    for k in range(4 * q0, 4 * q1):
                        nc.vector.tensor_scalar(uT[:, k, :], uT[:, k, :], gain[:, 0, k:k + 1], shift[:, 0, k:k + 1],
                                                ALU.mult, ALU.add).then_inc(s_mod, 1)

                sine_argument(0)
                normalise(0)
                sine_argument(1)
                normalise(1)
                keep_rows(0)
                sine_argument(2)
                keep_rows(1)
                normalise(2)
                normalise(3)
                keep_rows(2)
                keep_rows(3)
                window_filter(0)
                window_filter(1)
                keep_rows(4)
                keep_rows(5)
                v.wait_ge(s_xe, 16)
                v.wait_ge(s_mt, 1)
                scale(0, 2, True)
                keep_rows(6)
                v.wait_ge(s_mt, 2)
                scale(2, 3, False)
                keep_rows(7)
                v.wait_ge(s_mt, 3)
                scale(3, 4, False)

        spec = at(184, 4, C)
        dft = at(200, 2, TT, SEQ)
        t_tmp = at(172, TT, N)
        z_tmp = at(176, TT, N)
        rope = at(180, 2, TT, HD)
        s_spec = sem("s_spec")

        def rotate(ch, x, t):
            heads = x.rearrange("p (h d) -> p h d", d=HD)
            quarter = HD // 4
            halves_ = lambda a: a.rearrange("p (h a b i) -> p h a b i", a=2, b=2, i=quarter)
            one, two = (a.rearrange("p t n -> p (t n)") for a in (z_tmp, t_tmp))
            cos = rope[:, 0, t, :].unsqueeze(1).broadcast_to((P, 2 * HEADS, HD))
            ch.link(nc.vector.tensor_tensor(one.rearrange("p (h d) -> p h d", d=HD), heads, cos, ALU.mult))
            for b in range(2):
                sin = rope[:, 1, t, :].rearrange("p (a b i) -> p a b i", a=2, b=2)[:, :, b, :]
                sin = sin.unsqueeze(1).broadcast_to((P, 2 * HEADS, 2, quarter))
                ch.link(nc.vector.tensor_tensor(halves_(two)[:, :, :, b, :], halves_(x)[:, :, :, 1 - b, :], sin, ALU.mult))
            ch.link(nc.vector.tensor_tensor(x, one, two, ALU.add))

        with ExitStack() as st:
            p_in = at(152, TT, N)
            p_prev = at(156, TT, N)
            p_next = at(160, TT, N)
            taps = at(164, 3, N)
            tap_bias = at(170, N)
            wm = at(164, 4, 2, C)
            acc = at(196, 2, C)
            H_CHUNKS = 3 * C // N
            KV_CHUNKS = 2 * C // N
            VECS = 4
            WM = 4

            s_wm = [sem(f"s_wm{b}") for b in range(WM)]
            s_wmu, s_acc, s_mrow, s_mcopy = sem("s_wmu"), sem("s_acc"), sem("s_mrow"), sem("s_mcopy")
            s_mout, s_mfree = sem("s_mout"), sem("s_mfree")
            s_zero, s_zout, s_pout, s_shift, s_taps, s_conv = (sem("s_zero"), sem("s_zout"), sem("s_pout"),
                                                               sem("s_shift"), sem("s_taps"), sem("s_conv"))
            s_rope, s_v2, s_v2m = sem("s_rope"), sem("s_v2"), sem("s_v2m")
            block = st.enter_context(nc.Block())
            first_bank = place[MODULATE_END][0]
            kv_bank = first_bank
            hy_bank = kv_bank + KV_CHUNKS * 2 * TT

            def bank_of(j):
                return hy_bank + TT * HY_Q_ORDER.index(j)

            @block.sync
            def _(sp):
                n = MODULATE_END + RING
                for i in range(8 * VECS * 2):
                    vec, half, kp = i // 16, (i // 8) % 2, i % 8
                    if i >= WM:
                        sp.wait_ge(s_wmu, i - WM + 1)
                    col = (2 + vec) * D + half * C
                    sp.dma_start(wm[:, i % WM, :, :],
                                 io["w_mod"][0, 2 * kp * P:2 * (kp + 1) * P, col:col + C].rearrange("(k p) n -> p k n", p=P)
                                 ).then_inc(s_wm[i % WM], 16)
                    if i % 8 == 7:
                        stream(sp, n, n + 1)
                        n += 1
                stream(sp, n, PROJECT_END + RING)

            @block.scalar
            def _(act):
                act.sem_inc(s_mfree, 2)

                def evacuate(bank, dst):
                    act.wait_ge(a_full, bank + 1)
                    return nc.scalar.activation(dst, psA[:, bank % 4, :], ACT.Copy).then_inc(a_free, 1)

                def mod_row_out(i):
                    act.wait_ge(s_mrow, i + 1)
                    nc.scalar.activation(acc[0:1, i % 2, :], psB[0:1, 2 * (i % 2):2 * (i % 2) + 2, :].rearrange("p a n -> p (a n)"),
                                         ACT.Copy).then_inc(s_mcopy, 1)
                    act.wait_ge(s_mcopy, i + 1)
                    act.dma_start(mod_rows[i // 2:i // 2 + 1, (i % 2) * C:(i % 2 + 1) * C], acc[0:1, i % 2, :]).then_inc(s_mout, 16)
                    act.wait_ge(s_mout, 16 * (i + 1))
                    act.sem_inc(s_mfree, 1)

                for j in range(KV_CHUNKS):
                    dst = (k_all, v_all)[j // 2]
                    if j:
                        mod_row_out(2 * j - 1)
                    for i in range(2 * TT):
                        evacuate(kv_bank + 2 * TT * j + i, dst[:, i, (j % 2) * N:(j % 2 + 1) * N])
                    mod_row_out(2 * j)
                for j in HY_Q_ORDER:
                    if j >= H_CHUNKS:
                        c0 = (j - H_CHUNKS) * N
                        for t in range(TT):
                            evacuate(bank_of(j) + t, q_lat[:, t, c0:c0 + N])
                        continue
                    if j:
                        act.wait_ge(s_conv, j)
                        act.wait_ge(s_pout, 16 * j)
                    for t in range(TT):
                        evacuate(bank_of(j) + t, p_in[:, t, :])
                    if j == 0:
                        mod_row_out(2 * VECS - 1)
                        act.dma_start(spec, filt_spec).then_inc(s_spec, 16)
                        act.dma_start(dft[:, 0, :, :], io["k_cos"].rearrange("(t p) f -> p t f", p=P)).then_inc(s_spec, 16)
                        act.dma_start(dft[:, 1, :, :], io["k_sin"].rearrange("(t p) f -> p t f", p=P)).then_inc(s_spec, 16)

            @block.gpsimd
            def _(pool):
                pool.wait_ge(s_acc, 2 * VECS)
                nc.gpsimd.memset(z_tmp[0:3, :, :], 0.0).then_inc(s_zero, 1)
                pool.wait_ge(s_zero, 1)
                zeros = z_tmp[0:3, :, :].rearrange("p t n -> p (t n)")
                pool.dma_start(shifted[0, :].rearrange("(a n) -> a n", n=C), zeros).then_inc(s_zout, 16)
                pool.dma_start(shifted[SEQ + 1, :].rearrange("(a n) -> a n", n=C), zeros).then_inc(s_zout, 16)
                pool.wait_ge(s_zout, 32)
                for j in range(H_CHUNKS):
                    cs = slice(j * N, (j + 1) * N)
                    if j:
                        pool.wait_ge(s_conv, j)
                    pool.dma_start(taps, io["hy_conv_w"][0, :, cs].partition_broadcast(P)).then_inc(s_taps, 16)
                    pool.dma_start(tap_bias, io["hy_conv_b"][0, cs].partition_broadcast(P)).then_inc(s_taps, 16)
                    pool.wait_ge(a_free, bank_of(j) + TT)
                    pool.dma_start(shifted[1:SEQ + 1, cs].rearrange("(t p) n -> p t n", p=P), p_in).then_inc(s_pout, 16)
                    pool.wait_ge(s_pout, 16 * (j + 1))
                    pool.dma_start(p_prev, shifted[0:SEQ, cs].rearrange("(t p) n -> p t n", p=P)).then_inc(s_shift, 16)
                    pool.dma_start(p_next, shifted[2:SEQ + 2, cs].rearrange("(t p) n -> p t n", p=P)).then_inc(s_shift, 16)
                    if j == 0:
                        pool.dma_start(rope[:, 0, :, :], io["k_rope_cos"].rearrange("(t p) d -> p t d", p=P)).then_inc(s_rope, 16)
                        pool.dma_start(rope[:, 1, :, :], io["k_rope_sin"].rearrange("(t p) d -> p t d", p=P)).then_inc(s_rope, 16)

            @block.tensor
            def _(pe):
                def token_tile(src, t, half):
                    return lambda k: src[:, half * KH + k, t * P:(t + 1) * P]

                def mod_sum(i):
                    pe.wait_ge(s_acc, i + 1)
                    if i >= 2:
                        pe.wait_ge(s_mcopy, i - 1)
                    for q in range(2):
                        last = nc.tensor.matmul(psB[0:1, 2 * (i % 2) + q, :], ones[:], acc[:, i % 2, q * N:(q + 1) * N],
                                                start=True, stop=True)
                    last.then_inc(s_mrow, 1)

                n = MODULATE_END
                for j in range(KV_CHUNKS):
                    for half in range(2):
                        gemm_half(pe, n, [token_tile(uT, t, half) for t in range(TT)]
                                  + [token_tile(uctxT, t, half) for t in range(TT)])
                        n += 1
                        if j or half:
                            mod_sum(2 * j + half - 1)
                for j in HY_Q_ORDER:
                    for half in range(2):
                        gemm_half(pe, n, [token_tile(uT, t, half) for t in range(TT)])
                        n += 1
                    if j == 0:
                        mod_sum(2 * VECS - 1)

            @block.vector
            def _(v):
                MOD_LINKS = KD
                with v.Fori(0, VECS) as vec:
                    for half in range(2):
                        ch = Chain(v, s_v2m, (2 * vec + half) * MOD_LINKS)
                        for kp in range(8):
                            v.wait_ge(s_wm[kp % WM], (vec * 4 + half * 2 + kp // WM + 1) * 16)
                            if kp == 0:
                                v.wait_ge(s_mfree, 2 * vec + half + 1)
                            for j in range(2):
                                k = 2 * kp + j
                                if k == 0:
                                    ins = nc.vector.tensor_scalar(acc[:, half, :], wm[:, 0, 0, :], cols[:, 0:1], None, ALU.mult)
                                else:
                                    ins = nc.vector.scalar_tensor_tensor(acc[:, half, :], wm[:, kp % WM, j, :], cols[:, k:k + 1],
                                                                         acc[:, half, :], ALU.mult, ALU.add)
                                ch.link(ins)
                            v.sem_inc(s_wmu, 1)
                        assert ch.n == MOD_LINKS
                        v.sem_inc(s_acc, 1)

                ch = Chain(v, s_v2)

                def over_tiles(w):
                    return w.unsqueeze(1).broadcast_to((P, TT, N))

                for j in range(H_CHUNKS):
                    cs = slice((j % 2) * N, (j % 2 + 1) * N)
                    v.wait_ge(s_taps, 32 * (j + 1))
                    v.wait_ge(s_shift, 32 * (j + 1))
                    ch.link(nc.vector.tensor_tensor(z_tmp, p_in, over_tiles(taps[:, 1, :]), ALU.mult))
                    for other, w in ((p_prev, 0), (p_next, 2)):
                        ch.link(nc.vector.tensor_tensor(t_tmp, other, over_tiles(taps[:, w, :]), ALU.mult))
                        ch.link(nc.vector.tensor_tensor(z_tmp, z_tmp, t_tmp, ALU.add))
                    bias = over_tiles(tap_bias)
                    if j // 2 == 0:
                        ch.link(nc.vector.tensor_tensor(hy_u[:, :, cs], z_tmp, bias, ALU.add))
                    elif j // 2 == 1:
                        ch.link(nc.vector.tensor_tensor(z_tmp, z_tmp, bias, ALU.add))
                        ch.link(nc.vector.tensor_tensor(hy_u[:, :, cs], hy_u[:, :, cs], z_tmp, ALU.mult))
                    else:
                        ch.link(nc.vector.tensor_tensor(hy_x0[:, :, cs], z_tmp, bias, ALU.add))
                    v.sem_inc(s_conv, 1)
                    if j == 2:
                        v.wait_ge(s_rope, 32)
                        for t in range(TT):
                            rotate(ch, k_all[:, t, :], t)


        neg_lam = small[:, 0:1]
        with ExitStack() as st:
            tmp = at(152, 2, N)
            idft = at(156, 2, TT, SEQ)
            y_re = at(160, TT, C)
            y_im = hy_u
            lam_in = small[:, 8:8 + 4 * HD].rearrange("p (a d) -> p a d", a=4)
            lam_sum = small[:, 1:3]
            lam_exp = small[:, 3:5]
            s_idft, s_lam, s_lsum, s_lexp = sem("s_idft"), sem("s_lam"), sem("s_lsum"), sem("s_lexp")
            s_uf, s_prod, s_kt, s_kte, s_inv, s_yt, s_yt_e, s_y = (
                sem("s_uf"), sem("s_prod"), sem("s_kt"), sem("s_kte"), sem("s_inv"), sem("s_yt"), sem("s_yt_e"), sem("s_y"))
            s_v3, s_qrot = sem("s_v3"), sem("s_qrot")
            block = st.enter_context(nc.Block())

            @block.scalar
            def _(act):
                act.dma_start(idft[:, 0, :, :], io["k_icos"].rearrange("(t p) f -> p t f", p=P)).then_inc(s_idft, 16)
                act.dma_start(idft[:, 1, :, :], io["k_isin"].rearrange("(t p) f -> p t f", p=P)).then_inc(s_idft, 16)
                act.dma_start(small[:, 8:8 + 4 * HD], io["da_lambda"][0].rearrange("a d -> (a d)").partition_broadcast(P)).then_inc(s_lam, 16)
                for h in range(HEADS):
                    act.wait_ge(s_kt, h + 1)
                    nc.scalar.activation(kT[:, h, :], psA[:, h % 4, :], ACT.Copy).then_inc(s_kte, 1)
                act.wait_ge(s_prod, 2)
                for h in range(0, HEADS, 2):
                    act.wait_ge(s_kt, HEADS + h // 2 + 1)
                    nc.scalar.activation(qT[:, h:h + 2, :], psA[:, (h // 2) % 4, :].rearrange("p (h t) -> p h t", h=2),
                                         ACT.Copy).then_inc(s_kte, 1)
                for n in range(2 * TT):
                    act.wait_ge(s_yt, n + 1)
                    t, kq = n // 2, n % 2
                    nc.scalar.activation(y_hyT[:, 4 * kq:4 * kq + 4, t * P:(t + 1) * P],
                                         psA[:, n, :].rearrange("p (k t) -> p k t", k=4), ACT.Copy).then_inc(s_yt_e, 1)
                act.wait_ge(s_lsum, 1)
                nc.scalar.activation(lam_exp, lam_sum, ACT.Exp).then_inc(s_lexp, 1)

            @block.tensor
            def _(pe):
                pe.wait_ge(s_spec, 48)
                for nh, ps in ((0, psA), (1, psB)):
                    for part in range(4):
                        f0 = (part % 2) * P
                        for t in range(TT):
                            last = nc.tensor.matmul(ps[:, part, :], dft[:, part // 2, t, f0:f0 + P],
                                                    hy_u[:, t, nh * N:(nh + 1) * N], start=(t == 0), stop=(t == TT - 1))
                    last.then_inc(s_uf, 1)
                pe.wait_ge(s_prod, 1)
                for h in range(HEADS):
                    if h >= 4:
                        pe.wait_ge(s_kte, h - 3)
                    for t in range(2 * TT):
                        last = nc.tensor.transpose(psA[:, h % 4, t * P:(t + 1) * P], k_all[:, t, h * P:(h + 1) * P], ident[:])
                    last.then_inc(s_kt, 1)
                pe.wait_ge(s_qrot, 1)
                for h in range(0, HEADS, 2):
                    pe.wait_ge(s_kte, HEADS + h // 2 - 3)
                    for i in range(2):
                        for t in range(TT):
                            last = nc.tensor.transpose(psA[:, (h // 2) % 4, i * SEQ + t * P:i * SEQ + (t + 1) * P],
                                                       q_lat[:, t, (h + i) * P:(h + i + 1) * P], ident[:])
                    last.then_inc(s_kt, 1)
                pe.wait_ge(s_idft, 32)
                pe.wait_ge(s_prod, 2)
                for t in range(TT):
                    for nh in range(2):
                        for f in range(TT):
                            nc.tensor.matmul(psB[:, 2 * t + nh, :], idft[:, 0, f, t * P:(t + 1) * P],
                                             y_re[:, f, nh * N:(nh + 1) * N], start=(f == 0), stop=False)
                        for f in range(TT):
                            last = nc.tensor.matmul(psB[:, 2 * t + nh, :], idft[:, 1, f, t * P:(t + 1) * P],
                                                    y_im[:, f, nh * N:(nh + 1) * N], start=False, stop=(f == TT - 1))
                        last.then_inc(s_inv, 1)
                pe.wait_ge(s_kte, HEADS + HEADS // 2)
                for n in range(2 * TT):
                    t, kq = n // 2, n % 2
                    pe.wait_ge(s_y, n + 1)
                    for k in range(4):
                        c0 = (4 * kq + k) * P
                        last = nc.tensor.transpose(psA[:, n, k * P:(k + 1) * P], hy_x0[:, t, c0:c0 + P], ident[:])
                    last.then_inc(s_yt, 1)

            @block.vector
            def _(v):
                ch = Chain(v, s_v3)
                for t in range(TT):
                    rotate(ch, q_lat[:, t, :], t)
                v.sem_inc(s_qrot, 1)
                for nh, ps in ((0, psA), (1, psB)):
                    v.wait_ge(s_uf, 2)
                    cs = slice(nh * N, (nh + 1) * N)
                    for f in range(TT):
                        re, im, k_re, k_im = ps[:, f, :], ps[:, 2 + f, :], spec[:, f, cs], spec[:, 2 + f, cs]
                        ch.link(nc.vector.tensor_tensor(tmp[:, 0, :], re, k_re, ALU.mult))
                        ch.link(nc.vector.tensor_tensor(tmp[:, 1, :], im, k_im, ALU.mult))
                        ch.link(nc.vector.tensor_tensor(y_re[:, f, cs], tmp[:, 0, :], tmp[:, 1, :], ALU.add))
                        ch.link(nc.vector.tensor_tensor(tmp[:, 0, :], re, k_im, ALU.mult))
                        ch.link(nc.vector.tensor_tensor(tmp[:, 1, :], im, k_re, ALU.mult))
                        ch.link(nc.vector.tensor_tensor(y_im[:, f, cs], tmp[:, 0, :], tmp[:, 1, :], ALU.subtract))
                    v.sem_inc(s_prod, 1)
                v.wait_ge(s_lam, 16)
                for i in range(2):
                    ch.link(nc.vector.tensor_tensor_reduce(tmp[:, 0, 0:HD], lam_in[:, 2 * i, :], lam_in[:, 2 * i + 1, :],
                                                           1.0, 0.0, ALU.mult, ALU.add, lam_sum[:, i:i + 1]))
                v.sem_inc(s_lsum, 1)
                for t in range(TT):
                    for nh in range(2):
                        v.wait_ge(s_inv, 2 * t + nh + 1)
                        cs = slice(nh * N, (nh + 1) * N)
                        nc.vector.tensor_tensor(hy_x0[:, t, cs], psB[:, 2 * t + nh, :], hy_x0[:, t, cs], ALU.mult).then_inc(s_y, 1)
                v.wait_ge(s_lexp, 1)
                ch.link(nc.vector.tensor_tensor(neg_lam, lam_exp[:, 1:2], lam_exp[:, 0:1], ALU.subtract))
                ch.link(nc.vector.tensor_scalar(neg_lam, neg_lam, -LAM_INIT, None, ALU.add))

        o_all = at(168, TT, C)
        squares = at(177, 2 * HEADS)
        o_rstd = at(177.25, 2 * HEADS)
        r_tmp = at(177.5, 2 * HEADS)
        subln = at(178.5, P)
        s_sub = sem("s_sub")
        with ExitStack() as st:
            probs = at(144, 2, 4, KV)
            aT = at(160, 2, 2 * TT, SEQ)
            stat = at(176, 2, 4, 4)
            junk = at(178, P)
            s_sc, s_max, s_exp, s_diff, s_at, s_ate, s_pv, s_o, s_v4, s_v4b = (
                sem("s_sc"), sem("s_max"), sem("s_exp"), sem("s_diff"), sem("s_at"), sem("s_ate"),
                sem("s_pv"), sem("s_o"), sem("s_v4"), sem("s_v4b"))
            block = st.enter_context(nc.Block())
            gate_bank = place[PROJECT_END][0]
            SCALE = HD ** -0.5

            @block.sync
            def _(sp):
                sp.dma_start(subln, io["da_subln"][0].partition_broadcast(P)).then_inc(s_sub, 16)
                stream(sp, PROJECT_END + RING, ATTEND_END + RING)

            @block.scalar
            def _(act):
                for h in range(HEADS):
                    for i in range(4):
                        act.wait_ge(s_max, 4 * h + i + 1)
                        nc.scalar.activation(probs[:, h % 2, i, :], psB[:, i, :], ACT.Exp, scale=SCALE,
                                             bias=stat[:, h % 2, 0, i:i + 1],
                                             accum_out=stat[:, h % 2, 1, i:i + 1]).then_inc(s_exp, 1)
                    for t in range(TT):
                        act.wait_ge(s_at, TT * h + t + 1)
                        nc.scalar.activation(aT[:, h % 2, :, t * P:(t + 1) * P],
                                             psB[:, t, :].rearrange("p (k t) -> p k t", k=4), ACT.Copy).then_inc(s_ate, 1)
                    for t in range(TT):
                        act.wait_ge(a_full, gate_bank + TT * h + t + 1)
                        nc.scalar.activation(gates[:, t, h * N:(h + 1) * N], psA[:, (gate_bank + TT * h + t) % 4, :],
                                             ACT.Tanh, scale=0.5).then_inc(a_free, 1)

            @block.tensor
            def _(pe):
                for h in range(HEADS):
                    if h:
                        pe.wait_ge(s_o, TT * h)
                    for i in range(4):
                        comp, t = i // TT, i % TT
                        d0 = comp * HD
                        nc.tensor.matmul(psB[:, i, :], qT[d0:d0 + HD, h, t * P:(t + 1) * P], kT[d0:d0 + HD, h, :],
                                         start=True, stop=True).then_inc(s_sc, 1)
                    n = PROJECT_END + 2 * h
                    gemm_half(pe, n, [lambda k, t=t: uT[:, k, t * P:(t + 1) * P] for t in range(TT)])
                    for t in range(TT):
                        pe.wait_ge(s_diff, TT * h + t + 1)
                        for b in range(4):
                            last = nc.tensor.transpose(psB[:, t, b * P:(b + 1) * P], probs[:, h % 2, t, b * P:(b + 1) * P], ident[:])
                        last.then_inc(s_at, 1)
                    gemm_half(pe, n + 1, [lambda k, t=t: uT[:, KH + k, t * P:(t + 1) * P] for t in range(TT)])
                    for t in range(TT):
                        pe.wait_ge(s_ate, TT * h + t + 1)
                        for b in range(4):
                            last = nc.tensor.matmul(psB[:, 2 + t, 0:P], aT[:, h % 2, b, t * P:(t + 1) * P],
                                                    v_all[:, b, h * P:(h + 1) * P], start=(b == 0), stop=(b == 3))
                        last.then_inc(s_pv, 1)

            @block.vector
            def _(v):
                ch = Chain(v, s_v4)
                for h in range(HEADS):
                    st_ = stat[:, h % 2, :, :]
                    for i in range(4):
                        v.wait_ge(s_sc, 4 * h + i + 1)
                        ch.link(nc.vector.tensor_reduce(st_[:, 0, i:i + 1], psB[:, i, :], AX.X, ALU.max))
                        nc.vector.tensor_scalar(st_[:, 0, i:i + 1], st_[:, 0, i:i + 1], -SCALE, None, ALU.mult).then_inc(s_max, 1)
                    v.wait_ge(s_exp, 4 * h + 4)
                    ch.link(nc.vector.reciprocal(st_[:, 2, :], st_[:, 1, :]))
                    ch.link(nc.vector.tensor_scalar(st_[:, 2, TT:4], st_[:, 2, TT:4], neg_lam, None, ALU.mult))
                    for t in range(TT):
                        one, two = probs[:, h % 2, t, :], probs[:, h % 2, TT + t, :]
                        ch.link(nc.vector.tensor_scalar(one, one, st_[:, 2, t:t + 1], None, ALU.mult))
                        nc.vector.scalar_tensor_tensor(one, two, st_[:, 2, TT + t:TT + t + 1], one, ALU.mult, ALU.add).then_inc(s_diff, 1)
                    for t in range(TT):
                        v.wait_ge(s_pv, TT * h + t + 1)
                        o = o_all[:, t, h * P:(h + 1) * P]
                        nc.vector.tensor_copy(o, psB[:, 2 + t, 0:P]).then_inc(s_o, 1)
                        v.wait_ge(s_o, TT * h + t + 1)
                        ch.link(nc.vector.tensor_tensor_reduce(junk, o, o, 1.0, 0.0, ALU.mult, ALU.add,
                                                               squares[:, t * HEADS + h:t * HEADS + h + 1]))

        x1 = at(128, TT, D)
        h = at(144, TT, D)
        scores = at(160, TT, HP, N_KEYS)
        g2_row = at(184, D)

        total = at(176, D)
        s_key = at(192, 2, 2, N_KEYS)
        cand = at(194, N_KEYS * 2)
        hot = at(195, TOPK, TOPK)
        iota = at(196, TOPK)
        top_v = at(196.25, 2, TOPK)
        top_vu = at(196.5, 2, TOPK).bitcast(U32)
        top_vf = at(196.75, 2, TOPK)
        best = at(197, 2, TOPK)
        best_u = at(197.25, TOPK).bitcast(U32)
        ab_u = at(197.5, 2, TOPK).bitcast(U32)
        ab = at(197.75, 2, TOPK)
        pick = at(198, 2, TOPK)
        rows = at(198.25, 2, TOPK).bitcast(U32)
        neg_max = at(198.5, 2)
        e_sum = at(198.75, 2, 2)
        e_g = at(199, 2, TOPK)
        dots = at(199.25, 2, TOPK)
        act_ = at(199.5, 2, TOPK)
        wgt = at(199.75, 2, TOPK)
        all_scores = scores.rearrange("p t b k -> p (t b) k")
        u_tab, v_tab = io["peer_u"][0], io["peer_v"][0]
        s_iota, s_row_idx, s_gathers, s_nmax, s_eg, s_dots, s_gelu, s_v6, s_top, s_step = (
            sem("s_iota"), sem("s_row_idx"), sem("s_gathers"), sem("s_nmax"), sem("s_eg"), sem("s_dots"), sem("s_gelu"),
            sem("s_v6"), sem("s_top"), sem("s_step"))
        TOP_LINKS = 27

        def gather(table, par, j, dst):
            return nc.gpsimd.indirect_dma_start(
                out=dst, out_offset=None, in_=table,
                in_offset=bass.IndirectOffsetOnAxis(ap=rows[:, par, j:j + 1], axis=0))

        def softmax_terms(act, head, par):
            act.wait_ge(s_nmax, head + 1)
            nc.scalar.activation(e_g[:, par, :], best[:, par, :], ACT.Exp, bias=neg_max[:, par:par + 1],
                                 accum_out=e_sum[:, par, 0:1]).then_inc(s_eg, 1)

        def gelu(act, head, par):
            act.wait_ge(s_dots, head + 1)
            nc.scalar.activation(act_[:, par, :], dots[:, par, :], ACT.Gelu).then_inc(s_gelu, 1)

        def top16(ch, values, out_v, out_i):
            ch.link(nc.vector.max(out=out_v[:, 0:8], in_=values), s_step)
            ch.link(nc.vector.max_index(out=out_i[:, 0:8], in_max=out_v[:, 0:8], in_values=values), s_step)
            ch.link(nc.vector.match_replace(out=values, in_to_replace=out_v[:, 0:8], in_values=values, imm_value=LOWEST), s_step)
            ch.link(nc.vector.max(out=out_v[:, 8:16], in_=values), s_step)
            ch.link(nc.vector.max_index(out=out_i[:, 8:16], in_max=out_v[:, 8:16], in_values=values), s_step)

        def choose(v, head, par):
            ch = Chain(v, s_top, head * TOP_LINKS)
            ch.link(nc.vector.tensor_copy(s_key[:, par, :, :], all_scores[:, bass.ds(2 * head, 2), :]), s_step)
            for i in range(2):
                top16(ch, s_key[:, par, i, :], top_v[:, i, :], top_vu[:, i, :])
            ch.link(nc.vector.tensor_copy(top_vf, top_vu))
            a_side = top_v[:, 0, :].unsqueeze(2).broadcast_to((P, TOPK, TOPK))
            b_side = top_v[:, 1, :].unsqueeze(1).broadcast_to((P, TOPK, TOPK))
            ch.link(nc.vector.tensor_tensor(cand.rearrange("p (a b) -> p a b", b=TOPK), a_side, b_side, ALU.add), s_step)
            top16(ch, cand, best[:, par, :], best_u)
            nc.vector.tensor_scalar(neg_max[:, par:par + 1], best[:, par, 0:1], -1.0, None, ALU.mult).then_inc(s_nmax, 1)
            ch.link(nc.vector.tensor_scalar(ab_u[:, 0, :], best_u, 4, None, ALU.logical_shift_right))
            ch.link(nc.vector.tensor_scalar(ab_u[:, 1, :], best_u, TOPK - 1, None, ALU.bitwise_and))
            ch.link(nc.vector.tensor_copy(ab, ab_u))
            for i in range(2):
                where = ab[:, i, :].unsqueeze(2).broadcast_to((P, TOPK, TOPK))
                numbers = iota.unsqueeze(1).broadcast_to((P, TOPK, TOPK))
                of_key = top_vf[:, i, :].unsqueeze(1).broadcast_to((P, TOPK, TOPK))
                ch.link(nc.vector.tensor_tensor(hot, where, numbers, ALU.is_equal))
                ch.link(nc.vector.tensor_tensor(hot, hot, of_key, ALU.mult))
                ch.link(nc.vector.tensor_reduce(pick[:, i, :], hot, AX.X, ALU.add))
            nc.vector.scalar_tensor_tensor(rows[:, par, :], pick[:, 0, :], float(N_KEYS), pick[:, 1, :],
                                           ALU.mult, ALU.add).then_inc(s_row_idx, 1)
            assert ch.n == TOP_LINKS, ch.n

        def dot(row, t, par, j):
            return nc.vector.tensor_tensor_reduce(row, row, h[:, t, :], 1.0, 0.0, ALU.mult, ALU.add, dots[:, par, j:j + 1])

        def weigh(v, head, par):
            v.wait_ge(s_eg, head + 1)
            ch = Chain(v, s_v6, head * 3)
            ch.link(nc.vector.reciprocal(e_sum[:, par, 1:2], e_sum[:, par, 0:1]))
            ch.link(nc.vector.tensor_scalar(e_g[:, par, :], e_g[:, par, :], e_sum[:, par, 1:2], None, ALU.mult))
            v.wait_ge(s_gelu, head + 1)
            ch.link(nc.vector.tensor_tensor(wgt[:, par, :], e_g[:, par, :], act_[:, par, :], ALU.mult))

        def add_row(row, par, j):
            return nc.vector.scalar_tensor_tensor(total, row, wgt[:, par, j:j + 1], total, ALU.mult, ALU.add)

        with ExitStack() as st:
            m = at(64, TT, D)
            mT = at(80, KD, SEQ)
            da_part = at(144, TT, N)
            mix = h
            x_in = at(160, TT, D)
            g1_row = at(176, D)
            gain_row = at(112, D)
            shift_row = at(120, D)
            row_tmp = at(196, D)
            hT = at(64, KD, SEQ)
            q = at(80, TT, N)
            q_T = at(84, 4, SEQ)
            first_rows = [at(kb, D) for kb in (88, 96, 112, 120)]
            keys = at(96, HP, DK_HALF)
            keysT = at(104, HP, N_KEYS)
            rs = small[:, 8:16]
            mix_sq = small[:, 16:16 + TT * (D // N)].rearrange("p (t j) -> p t j", t=TT)
            x1_sq = small[:, 32:32 + TT]
            mix_junk = at(192, N)
            sq_junk = at(196, D)
            s_keys, s_kt4, s_kt4e, s_ydt, s_ydte, s_m, s_mt4, s_mte = (
                sem("s_keys"), sem("s_kt4"), sem("s_kt4e"), sem("s_ydt"), sem("s_ydte"), sem("s_m"), sem("s_mt4"), sem("s_mte"))
            s_row, s_rowd, s_xin, s_mix, s_h, s_ht, s_hte, s_q, s_qt, s_qte, s_s, s_se, s_v5 = (
                sem("s_row"), sem("s_rowd"), sem("s_xin"), sem("s_mix"), sem("s_h"), sem("s_ht"), sem("s_hte"), sem("s_q"),
                sem("s_qt"), sem("s_qte"), sem("s_s"), sem("s_se"), sem("s_v5"))
            block = st.enter_context(nc.Block())
            s_rdst = [sem(f"s_rdst{r}") for r in range(4)]
            e_slot, e_used = [sem(f"e_slot{i}") for i in range(len(first_rows))], sem("e_used")
            s_onorm, s_sqr, s_x1 = sem("s_onorm"), sem("s_sqr"), sem("s_x1done")
            m_bank = place[ATTEND_END][0]
            o_bank = place[BRANCH_END][0]
            pq_bank = place[OUT_END][0]
            CH = D // N
            ROWS = [(0, 2, "norm_post_mix", g1_row), (1, 3, None, shift_row), (2, 4, "norm_pre_ffn", gain_row),
                    (3, 5, "norm_post_ffn", g2_row)]

            @block.sync
            def _(sp):
                stream(sp, ATTEND_END + RING, ALL_END)

            @block.gpsimd
            def _(pool):
                used = 0
                for r, b, norm, dst in ROWS:
                    if r == 0:
                        pool.wait_ge(a_full, m_bank + 4 * CH - TT)
                    if r == 1:
                        pool.wait_ge(s_m, TT * CH)
                    pool.dma_start(dst, mod_rows[r].partition_broadcast(P)).then_inc(s_rdst[r], 16)
                    if used:
                        pool.wait_ge(s_rowd, used)
                    pool.dma_start(row_tmp, io["b_mod"][0, b * D:(b + 1) * D].partition_broadcast(P)).then_inc(s_row, 16)
                    used += 1
                    if norm:
                        pool.wait_ge(s_rowd, used)
                        pool.dma_start(row_tmp, io[norm][0].partition_broadcast(P)).then_inc(s_row, 16)
                        used += 1
                pool.wait_ge(s_h, 4 * TT)
                pool.dma_start(iota, io["k_iota"]).then_inc(s_iota, 16)
                pool.wait_ge(s_row_idx, 1)
                slots_n = len(first_rows)
                for g in range(2 * TOPK):
                    if g >= slots_n:
                        pool.wait_ge(e_used, g - slots_n + 1)
                    gather((u_tab, v_tab)[g // TOPK], 0, g % TOPK, first_rows[g % slots_n]).then_inc(e_slot[g % slots_n], 16)

            @block.scalar
            def _(act):
                def evacuate(bank, dst, **how):
                    act.wait_ge(a_full, bank + 1)
                    return nc.scalar.activation(dst, psA[:, bank % 4, :], ACT.Copy, **how).then_inc(a_free, 1)

                for n in range(2 * TT):
                    act.wait_ge(s_ydt, n + 1)
                    t, kq = n // 2, n % 2
                    nc.scalar.activation(y_daT[:, 4 * kq:4 * kq + 4, t * P:(t + 1) * P],
                                         psB[:, n, :].rearrange("p (k t) -> p k t", k=4), ACT.Copy).then_inc(s_ydte, 1)
                act.wait_ge(s_ydt, 4)
                for t in range(TT):
                    act.dma_start(x_in[:, t, :], io["x"][0, t * P:(t + 1) * P, :]).then_inc(s_xin, 16)
                for j in range(CH):
                    for t in range(TT):
                        act.wait_ge(s_mt4, TT * j + t + 1)
                        nc.scalar.activation(mT[:, 4 * j:4 * j + 4, t * P:(t + 1) * P],
                                             psB[:, 2 * (j % 2) + t, :].rearrange("p (k t) -> p k t", k=4),
                                             ACT.Copy, scale=0.5).then_inc(s_mte, 1)
                act.dma_start(keys.rearrange("n (h a) d -> n h a d", a=2)[:, :, 0, :],
                              io["peer_keys"][0, 0].rearrange("h n d -> n h d")).then_inc(s_keys, 16)
                act.dma_start(keys.rearrange("n (h a) d -> n h a d", a=2)[:, :, 1, :],
                              io["peer_keys"][0, 1].rearrange("h n d -> n h d")).then_inc(s_keys, 16)
                for j in range(CH):
                    for t in range(TT):
                        act.wait_ge(a_full, o_bank + TT * j + t + 1)
                        bank = psA[:, (o_bank + TT * j + t) % 4, :]
                        nc.scalar.activation(mix[:, t, j * N:(j + 1) * N], bank, ACT.Copy).then_inc(s_mix, 1)
                        nc.scalar.activation(mix_junk, bank, ACT.Square, accum_out=mix_sq[:, t, j:j + 1]).then_inc(s_sqr, 1)
                        act.wait_ge(s_mix, TT * j + t + 1)
                        act.wait_ge(s_sqr, TT * j + t + 1)
                        act.sem_inc(a_free, 1)
                    if j == 0:
                        for n in range(4):
                            act.wait_ge(s_kt4, n + 1)
                            nc.scalar.activation(keysT[:, 4 * n:4 * n + 4, :], psB[:, n, :].rearrange("p (b k) -> p b k", b=4),
                                                 ACT.Copy).then_inc(s_kt4e, 1)
                for n in range(TT * 4):
                    if n % 4 == 0:
                        act.wait_ge(s_x1, n // 4 + 1)
                        nc.scalar.activation(sq_junk, x1[:, n // 4, :], ACT.Square, accum_out=x1_sq[:, n // 4:n // 4 + 1]).then_inc(s_sqr, 1)
                    act.wait_ge(s_ht, n + 1)
                    t, kq = n // 4, n % 4
                    nc.scalar.activation(hT[:, 4 * kq:4 * kq + 4, t * P:(t + 1) * P],
                                         psB[:, n % 4, :].rearrange("p (k t) -> p k t", k=4), ACT.Copy).then_inc(s_hte, 1)
                for j in range(CH):
                    for t in range(TT):
                        evacuate(pq_bank + TT * j + t, q[:, t, :])
                    for t in range(TT):
                        act.wait_ge(s_qt, TT * j + t + 1)
                        nc.scalar.activation(q_T[:, :, t * P:(t + 1) * P],
                                             psB[:, t, :].rearrange("p (b t) -> p b t", b=4), ACT.Copy).then_inc(s_qte, 1)
                    for t in range(TT):
                        act.wait_ge(s_s, TT * j + t + 1)
                        nc.scalar.activation(scores[:, t, 4 * j:4 * j + 4, :],
                                             psB[:, 2 + t, :].rearrange("p (b k) -> p b k", b=4), ACT.Copy).then_inc(s_se, 1)
                    if j == 0:
                        softmax_terms(act, 0, 0)
                    if j == 2:
                        gelu(act, 0, 0)

            @block.tensor
            def _(pe):
                def part(src, t, half=0):
                    return lambda k: src[:, half * KH + k, t * P:(t + 1) * P]

                def turn(src, t, c0, bank):
                    for k in range(4):
                        last = nc.tensor.transpose(psB[:, bank, k * P:(k + 1) * P], src[:, t, c0 + k * P:c0 + (k + 1) * P], ident[:])
                    return last

                def turn_m(j):
                    for t in range(TT):
                        pe.wait_ge(s_m, TT * j + t + 1)
                        if j >= 2:
                            pe.wait_ge(s_mte, TT * (j - 2) + t + 1)
                        turn(m, t, j * N, 2 * (j % 2) + t).then_inc(s_mt4, 1)

                n = ATTEND_END
                for j in range(CH):
                    gemm_half(pe, n, [part(y_hyT, t) for t in range(TT)])
                    if j == 0:
                        pe.wait_ge(s_onorm, 1)
                        for i in range(2 * TT):
                            turn(o_all, i // 2, (i % 2) * N, i).then_inc(s_ydt, 1)
                        pe.wait_ge(s_ydte, 2 * TT)
                    else:
                        turn_m(j - 1)
                    gemm_half(pe, n + 1, [part(y_daT, t) for t in range(TT)])
                    n += 2
                turn_m(CH - 1)
                pe.wait_ge(s_mte, TT * CH)
                for j in range(CH):
                    if j < CH - 1:
                        for half in range(2):
                            gemm_half(pe, n + half, [part(mT, t, half) for t in range(TT)])
                    else:
                        gemm_chunk_by_tile(pe, n, mT)
                    n += 2
                    if j == 0:
                        pe.wait_ge(s_keys, 32)
                        for b in range(4):
                            for k in range(4):
                                last = nc.tensor.transpose(psB[:, b, k * P:(k + 1) * P], keys[:, 4 * b + k, :], ident[:])
                            last.then_inc(s_kt4, 1)
                pe.wait_ge(s_kt4e, 4)
                for t in range(TT):
                    for kq in range(4):
                        pe.wait_ge(s_h, 4 * t + kq + 1)
                        if t:
                            pe.wait_ge(s_hte, kq + 1)
                        turn(h, t, kq * N, kq).then_inc(s_ht, 1)
                    pe.wait_ge(s_hte, 4 * (t + 1))
                    for half in range(2):
                        gemm_half(pe, n + half, [part(hT, t, half)] * TT, only=t)
                n += 2

                def score(j):
                    for t in range(TT):
                        pe.wait_ge(a_free, pq_bank + TT * j + t + 1)
                        turn(q, t, 0, t).then_inc(s_qt, 1)
                    for t in range(TT):
                        pe.wait_ge(s_qte, TT * j + t + 1)
                        if j:
                            pe.wait_ge(s_se, TT * (j - 1) + t + 1)
                        for k in range(4):
                            b = 4 * j + k
                            last = nc.tensor.matmul(psB[:, 2 + t, k * P:(k + 1) * P], q_T[:, k, t * P:(t + 1) * P], keysT[:, b, :],
                                                    start=True, stop=True)
                        last.then_inc(s_s, 1)

                score(0)
                for j in range(1, CH):
                    for half in range(2):
                        gemm_half(pe, n, [part(hT, t, half) for t in range(TT)])
                        n += 1
                        if half == 0 and j > 1:
                            score(j - 1)
                score(CH - 1)

            @block.vector
            def _(v):
                ch = Chain(v, s_v5)
                ch.link(nc.vector.tensor_scalar(squares, squares, 1.0 / P, EPS, ALU.mult, ALU.add))
                rsqrt(nc, ch, squares, o_rstd, r_tmp)
                v.wait_ge(s_sub, 16)
                ch.link(nc.vector.tensor_scalar(subln, subln, 1.0 - LAM_INIT, None, ALU.mult))
                heads = o_all.rearrange("p t (h d) -> p (t h) d", d=P)
                ch.link(nc.vector.tensor_tensor(heads, heads, o_rstd.unsqueeze(2).broadcast_to((P, 2 * HEADS, P)), ALU.mult))
                ch.link(nc.vector.tensor_tensor(heads, heads, subln.unsqueeze(1).broadcast_to((P, 2 * HEADS, P)), ALU.mult))
                v.sem_inc(s_onorm, 1)
                for j in range(CH):
                    cs = slice(j * N, (j + 1) * N)
                    for t in range(TT):
                        hy = m_bank + 4 * j + t
                        v.wait_ge(a_full, hy + 1)
                        ch.link(nc.vector.scalar_tensor_tensor(m[:, t, cs], gates[:, t, cs], 1.0, psA[:, hy % 4, :], ALU.add, ALU.mult))
                        v.sem_inc(a_free, 1)
                    for t in range(TT):
                        da = m_bank + 4 * j + TT + t
                        v.wait_ge(a_full, da + 1)
                        ch.link(nc.vector.scalar_tensor_tensor(da_part[:, t, :], gates[:, t, D + j * N:D + (j + 1) * N], 1.0,
                                                               psA[:, da % 4, :], ALU.add, ALU.mult))
                        v.sem_inc(a_free, 1)
                        nc.vector.tensor_tensor(m[:, t, cs], m[:, t, cs], da_part[:, t, :], ALU.add).then_inc(s_m, 1)
                loads = 0
                for r, b, norm, dst in ROWS:
                    loads += 1
                    v.wait_ge(s_rdst[r], 16)
                    v.wait_ge(s_row, 16 * loads)
                    ch.link(nc.vector.tensor_tensor(dst, dst, row_tmp, ALU.add))
                    v.sem_inc(s_rowd, 1)
                    if norm:
                        loads += 1
                        v.wait_ge(s_row, 16 * loads)
                        one = 1.0 if norm == "norm_pre_ffn" else 0.0
                        ch.link(nc.vector.scalar_tensor_tensor(dst, dst, one, row_tmp, ALU.add, ALU.mult))
                        v.sem_inc(s_rowd, 1)
                v.wait_ge(s_xin, 16 * TT)
                for t in range(TT):
                    ss, r, tmp = rs[:, 0:1], rs[:, 1:2], rs[:, 2:3]
                    v.wait_ge(a_free, o_bank + TT * (CH - 1) + t + 1)
                    ch.link(nc.vector.tensor_reduce(ss, mix_sq[:, t, :], AX.X, ALU.add))
                    ch.link(nc.vector.tensor_scalar(ss, ss, 1.0 / D, EPS, ALU.mult, ALU.add))
                    rsqrt(nc, ch, ss, r, tmp)
                    ch.link(nc.vector.scalar_tensor_tensor(x1[:, t, :], mix[:, t, :], r, g1_row, ALU.mult, ALU.mult))
                    ch.link(nc.vector.tensor_tensor(x1[:, t, :], x1[:, t, :], x_in[:, t, :], ALU.add))
                    v.sem_inc(s_x1, 1)
                    ch.link(nc.vector.tensor_tensor(h[:, t, :], x1[:, t, :], gain_row, ALU.mult))
                    v.wait_ge(s_sqr, TT * CH + t + 1)
                    ch.link(nc.vector.tensor_scalar(ss, x1_sq[:, t:t + 1], 1.0 / D, EPS, ALU.mult, ALU.add))
                    rsqrt(nc, ch, ss, r, tmp)
                    for kq in range(4):
                        cs = slice(kq * N, (kq + 1) * N)
                        nc.vector.scalar_tensor_tensor(h[:, t, cs], h[:, t, cs], r, shift_row[:, cs], ALU.mult, ALU.add).then_inc(s_h, 1)
                v.wait_ge(s_h, 4 * TT)
                v.wait_ge(s_iota, 16)
                v.wait_ge(s_se, 1)
                choose(v, 0, 0)
                ch.link(nc.vector.memset(total, 0.0))
                slots_n = len(first_rows)
                for j in range(TOPK):
                    v.wait_ge(e_slot[j % slots_n], 16 * (j // slots_n + 1))
                    dot(first_rows[j % slots_n], 0, 0, j).then_inc(e_used, 1)
                v.wait_ge(e_used, TOPK)
                v.sem_inc(s_dots, 1)
                choose(v, 1, 1)
                weigh(v, 0, 0)
                for j in range(TOPK):
                    g = TOPK + j
                    v.wait_ge(e_slot[g % slots_n], 16 * (g // slots_n + 1))
                    add_row(first_rows[g % slots_n], 0, j).then_inc(e_used, 1)
                    v.wait_ge(e_used, g + 1)

        with ExitStack() as st:
            slots = at(0, SLOTS, D)
            rs = at(200, 4)
            s_slot = [sem(f"s_slot{i}") for i in range(SLOTS)]
            s_used, s_vsum, s_out, s_done = sem("s_used"), sem("s_vsum"), sem("s_out"), sem("s_done")
            block = st.enter_context(nc.Block())
            ALL = TT * PEER_HEADS

            @block.gpsimd
            def _(pool):
                pool.sem_inc(s_used, SLOTS)

                def gather_head(head, par):
                    pool.wait_ge(s_row_idx, head + 1)
                    pool.sem_inc(s_gathers, 1)
                    for table in (u_tab, v_tab):
                        for j in range(TOPK):
                            pool.wait_ge(s_used, (head - 1) * 2 * TOPK + (TOPK if table is v_tab else 0) + j + 1)
                            pool.sem_inc(s_gathers, 1)
                            gather(table, par, j, slots[:, j, :]).then_inc(s_slot[j], 16)

                with pool.Fori(0, ALL // 2 - 1) as pair:
                    gather_head(2 * pair + 1, 1)
                    gather_head(2 * pair + 2, 0)
                gather_head(ALL - 1, 1)

            @block.scalar
            def _(act):
                with act.Fori(0, ALL // 2 - 1) as pair:
                    for head, par in ((2 * pair + 1, 1), (2 * pair + 2, 0)):
                        softmax_terms(act, head, par)
                        gelu(act, head, par)
                softmax_terms(act, ALL - 1, 1)
                gelu(act, ALL - 1, 1)

            @block.vector
            def _(v):
                def one_head(head, t, par, last=False):
                    before = (head - 1) * 2 * TOPK
                    for j in range(TOPK):
                        v.wait_ge(s_slot[j], (head - 1) * 32 + 16)
                        dot(slots[:, j, :], t, par, j).then_inc(s_used, 1)
                    v.wait_ge(s_used, before + TOPK + SLOTS)
                    v.sem_inc(s_dots, 1)
                    if not last:
                        choose(v, head + 1, 1 - par)
                    weigh(v, head, par)
                    for j in range(TOPK):
                        v.wait_ge(s_slot[j], (head - 1) * 32 + 32)
                        add_row(slots[:, j, :], par, j).then_inc(s_used, 1)
                        v.wait_ge(s_used, before + TOPK + j + 1 + SLOTS)

                end = Chain(v, s_vsum)
                for t in range(TT):
                    if t == 0:
                        with v.Fori(0, PEER_HEADS // 2 - 1) as pair:
                            one_head(2 * pair + 1, t, 1)
                            one_head(2 * pair + 2, t, 0)
                        one_head(PEER_HEADS - 1, t, 1)
                    else:
                        end.link(nc.vector.memset(total, 0.0))
                        with v.Fori(t * PEER_HEADS // 2, (t + 1) * PEER_HEADS // 2 - 1) as pair:
                            one_head(2 * pair, t, 0)
                            one_head(2 * pair + 1, t, 1)
                        one_head((t + 1) * PEER_HEADS - 2, t, 0)
                        one_head((t + 1) * PEER_HEADS - 1, t, 1, last=True)
                    ss, r, tmp = rs[:, 0:1], rs[:, 1:2], rs[:, 2:3]
                    res = x1[:, t, :]
                    sq = h[:, t, :]
                    end.link(nc.vector.tensor_tensor_reduce(sq, total, total, 1.0, 0.0, ALU.mult, ALU.add, ss))
                    end.link(nc.vector.tensor_scalar(ss, ss, 1.0 / D, EPS, ALU.mult, ALU.add))
                    rsqrt(nc, end, ss, r, tmp)
                    end.link(nc.vector.scalar_tensor_tensor(total, total, r, g2_row, ALU.mult, ALU.mult))
                    end.link(nc.vector.tensor_tensor(res, res, total, ALU.add))
                    v.sem_inc(s_done, 1)

            @block.sync
            def _(sp):
                for t in range(TT):
                    sp.wait_ge(s_done, t + 1)
                    sp.dma_start(out[0, t * P:(t + 1) * P, :], x1[:, t, :]).then_inc(s_out, 16)
                sp.wait_ge(s_out, 16 * TT)



_INS = ["x", "c", "ctx", "c_ctx", "w_mod", "b_mod", "norm_pre_mix", "norm_post_mix", "norm_pre_ffn", "norm_post_ffn",
        "w_in", "hy_conv_w", "hy_conv_b", "filt_w1", "filt_b1", "filt_w2", "filt_b2", "filt_w3", "filt_b3",
        "filt_w_out", "filt_freq", "hy_bias", "da_lambda", "da_subln", "w_hy_out", "w_da_out", "w_o",
        "peer_w_q", "peer_keys", "peer_u", "peer_v"]


def kernel(**inputs):
    import numpy as _np
    import concourse.bacc as _bacc
    from concourse import mybir as _mybir
    from concourse.bass_utils import run_bass_kernel_spmd as _run

    nc = _bacc.Bacc("TRN2", target_bir_lowering=False, num_devices=1)
    arrays, io = {}, {}
    for name, a in [(n, inputs[n]) for n in _INS] + list(constants().items()):
        a = _np.ascontiguousarray(a)
        arrays[f"in_{name}_dram"] = a
        io[name] = nc.dram_tensor(f"in_{name}_dram", a.shape, _mybir.dt.from_np(a.dtype), kind="ExternalInput").ap()
    out = nc.dram_tensor("out_0_dram", (1, SEQ, D), F32, kind="ExternalOutput").ap()
    build(nc, io, out)
    r = _run(nc, [arrays], core_ids=[0])
    return r.results[0]["out_0_dram"]
```

```python
from contextlib import ExitStack
import math

import numpy as np

import concourse.bass as bass
from concourse import mybir

F32 = mybir.dt.float32
U32 = mybir.dt.uint32
I32 = mybir.dt.int32
ALU = mybir.AluOpType
ACT = mybir.ActivationFunctionType
AX = mybir.AxisListType

P = 128
ARENA_KB = 204
D = 2048
SEQ = 256
CTX = 256
TT = SEQ // P
KD = D // P
C = D // 2
KC = C // P
GRID_W = 64
EPS = 1e-6
HEADS = 8
HD = 64
KV = CTX + SEQ
Q_OFF = 3 * C
K_OFF = Q_OFF + C
V_OFF = K_OFF + C
GATE_OFF = V_OFF + C
IN_COLS = GATE_OFF + 2 * D
N_MOD = 6
LAM_INIT = 0.8 - 0.6 * math.exp(0.0)
FILT_EMB = 33
FILT_ORDER = 64
PEER_HEADS = 8
N_KEYS = 128
N_EXPERTS = N_KEYS * N_KEYS
TOPK = 16
DK_HALF = 128
HP = 2 * PEER_HEADS
N = 512
KH = 8
RING = 4
SLOTS = 16
LOWEST = -3.0e38
TWO_PI_HI = 6.28125
TWO_PI_LO = 2.0 * math.pi - 6.28125
ROUND = 1.5 * 2.0 ** 23
MOD_BY_VECTOR = 1
MOD_BY_TENSOR = 2 * D // N - MOD_BY_VECTOR
MODULATE_END = 2 * MOD_BY_TENSOR
PROJECT_END = MODULATE_END + 2 * (2 * C // N) + 2 * (4 * C // N)
ATTEND_END = PROJECT_END + 2 * (2 * D // N)
BRANCH_END = ATTEND_END + 2 * (D // N)
OUT_END = BRANCH_END + 2 * (D // N)
ALL_END = OUT_END + 2 * (D // N)
HY_Q_ORDER = (0, 1, 2, 6, 3, 4, 5, 7)
V_C, V_CCTX, V_NORM, V_BSH, V_BSC = 0, 16, 32, 48, 64


def constants():
    f64 = np.float64
    t = np.arange(SEQ, dtype=f64)
    freq = np.arange(SEQ, dtype=f64) + 0.5
    ang = 2.0 * np.pi * np.outer(t, freq) / (2 * SEQ)
    scale = 2.0 / (2 * SEQ)
    bands_n = (FILT_EMB - 1) // 2
    tl = np.linspace(0.0, 1.0, SEQ)[:, None]
    w = 2.0 * math.pi * t[:, None] / SEQ
    bands = np.linspace(1e-4, bands_n - 1, bands_n)[None, :]
    z = np.concatenate([tl, np.cos(bands * w), -np.sin(bands * w)], axis=-1)
    deltas = np.abs(np.linspace(math.log(1e-2) / 1.5, math.log(1e-2) / 0.3, C))
    window = np.exp(-tl * deltas[None, :]) + 0.05
    window_b = window.copy()
    window_b[0] = 0.0
    half = HD // 4
    inv = 10000.0 ** (-np.arange(half, dtype=f64) / half)
    row = np.repeat(np.arange(SEQ // GRID_W), GRID_W)[:, None] * inv
    col = np.tile(np.arange(GRID_W), SEQ // GRID_W)[:, None] * inv
    cos = np.concatenate([np.cos(row), np.cos(row), np.cos(col), np.cos(col)], axis=1)
    sin = np.concatenate([-np.sin(row), np.sin(row), -np.sin(col), np.sin(col)], axis=1)
    f = lambda a: np.ascontiguousarray(a, dtype=np.float32)
    return {
        "k_ident": f(np.eye(P)), "k_cos": f(np.cos(ang)), "k_sin": f(np.sin(ang)),
        "k_icos": f(scale * np.cos(ang).T), "k_isin": f(-scale * np.sin(ang).T),
        "k_zT": f(z.T), "k_window": f(window), "k_window_b": f(window_b),
        "k_rope_cos": f(cos), "k_rope_sin": f(sin),
        "k_iota": f(np.tile(np.arange(TOPK), (P, 1))),
    }


def chunks():
    halves = []

    def full(name, col, banks):
        halves.append((name, 0, col, True, False, banks))
        halves.append((name, KH * P, col, False, True, banks))
    for j in range(MOD_BY_TENSOR):
        full("w_mod", j * N, 1)
    for j in range(2 * C // N):
        full("w_in", K_OFF + j * N, 2 * TT)
    for j in HY_Q_ORDER:
        full("w_in", j * N, TT)
    for j in range(2 * D // N):
        full("w_in", GATE_OFF + j * N, TT)
    for j in range(D // N):
        halves.append(("w_hy_out", 0, j * N, True, True, TT))
        halves.append(("w_da_out", 0, j * N, True, True, TT))
    for name in ("w_o", "peer_w_q"):
        for j in range(D // N):
            full(name, j * N, TT)
    return halves


def uses(halves):
    bank, partial, found = 0, 0, []
    for n, (_, _, _, _, ends, banks) in enumerate(halves):
        if n == MODULATE_END:
            bank += MOD_BY_VECTOR
        if ends:
            found.append((bank, 1, bank + banks))
            bank += banks
        else:
            partial += 1
            found.append((bank, 0, partial))
    return found


class Chain:

    def __init__(self, eng, sem, base=0):
        self.eng, self.sem, self.base, self.n = eng, sem, base, 0

    def link(self, ins, then=None):
        ins.then_inc(self.sem, 1)
        self.n += 1
        self.eng.wait_ge(self.sem, self.base + self.n)
        if then is not None:
            self.eng.sem_inc(then, 1)


def rsqrt(nc, ch, x, y, tmp):
    ch.link(nc.vector.tensor_scalar(tmp.bitcast(I32), x.bitcast(I32), 1, None, ALU.logical_shift_right))
    ch.link(nc.vector.tensor_scalar(y.bitcast(I32), tmp.bitcast(I32), -1.0, 1597463007.0, ALU.mult, ALU.add))
    for _ in range(4):
        ch.link(nc.vector.tensor_tensor(tmp, x, y, ALU.mult))
        ch.link(nc.vector.tensor_tensor(tmp, tmp, y, ALU.mult))
        ch.link(nc.vector.tensor_scalar(tmp, tmp, -0.5, 1.5, ALU.mult, ALU.add))
        ch.link(nc.vector.tensor_tensor(y, y, tmp, ALU.mult))


def build(nc, io, out):
    with ExitStack() as whole:
        def sem(name):
            return whole.enter_context(nc.semaphore(name))

        def scratch(name, shape):
            return nc.dram_tensor(name, shape, F32).ap()

        mod_rows = scratch("mod_rows", (4, D))
        filt_spec = scratch("filt_spec", (P, 4, C))
        shifted = scratch("shifted", (SEQ + 2, 3 * C))

        psA = whole.enter_context(nc.psum_tensor("psA", [P, 4, N], F32))
        psB = whole.enter_context(nc.psum_tensor("psB", [P, 4, N], F32))
        arena = whole.enter_context(nc.sbuf_tensor("arena", [P, ARENA_KB * 256], F32))
        ident = whole.enter_context(nc.sbuf_tensor("ident", [P, P], F32))
        ones = whole.enter_context(nc.sbuf_tensor("ones", [P, 1], F32))
        cols = whole.enter_context(nc.sbuf_tensor("cols", [P, 80], F32))
        small = whole.enter_context(nc.sbuf_tensor("small", [P, 8 + 4 * HD], F32))

        def at(kb, *shape):
            size = int(np.prod(shape))
            flat = arena[:, int(kb * 256):int(kb * 256) + size]
            if len(shape) == 1:
                return flat
            names = "abcd"[:len(shape)]
            return flat.rearrange(f"p ({' '.join(names)}) -> p {' '.join(names)}",
                                  **dict(zip(names[1:], shape[1:])))

        ring = at(0, RING, KH, N)
        uT = at(64, KD, SEQ)
        uctxT = at(80, KD, CTX)
        kT = at(80, HEADS, KV)
        v_all = at(96, 2 * TT, C)
        k_all = at(112, 2 * TT, C)
        q_lat = at(128, TT, C)
        hy_u = at(136, TT, C)
        hy_x0 = at(144, TT, C)
        qT = at(188, HEADS, SEQ)
        y_hyT = at(196, KC, SEQ)
        gates = at(112, TT, 2 * D)
        y_daT = at(96, KC, SEQ)

        w_landed = [sem(f"w_landed{i}") for i in range(RING)]
        w_used = sem("w_used")
        a_full = sem("a_full")
        a_free = sem("a_free")
        halves = chunks()
        place = uses(halves)

        def stream(sp, first, upto):
            for n in range(first, upto):
                name, row, col = halves[n][:3]
                if n >= RING:
                    _, which, value = place[n - RING]
                    sp.wait_ge((w_used, a_full)[which], value)
                src = io[name][0, row:row + KH * P, col:col + N].rearrange("(k p) n -> p k n", p=P)
                sp.dma_start(ring[:, n % RING, :, :], src).then_inc(w_landed[n % RING], 16)

        def gemm_half(pe, n, lefts, only=None):
            _, _, _, begins, ends, banks = halves[n]
            bank, which, _ = place[n]
            assert banks == len(lefts)
            pe.wait_ge(w_landed[n % RING], 16 * (n // RING + 1))
            for b, left in enumerate(lefts, bank):
                if only is not None and b != bank + only:
                    continue
                if begins and b >= 4:
                    pe.wait_ge(a_free, b - 3)
                for k in range(KH):
                    last = nc.tensor.matmul(psA[0:left(k).shape[1], b % 4, :], left(k), ring[:, n % RING, k, :],
                                            start=begins and k == 0, stop=ends and k == KH - 1)
                if ends:
                    last.then_inc(a_full, 1)
            if not ends and only in (None, banks - 1):
                last.then_inc(w_used, 1)

        def gemm_chunk_by_tile(pe, n, src):
            for t in range(TT):
                for half in range(2):
                    gemm_half(pe, n + half, [lambda k, t=t, half=half: src[:, half * KH + k, t * P:(t + 1) * P]] * TT, only=t)

        x_rows = [io["x"][0, 0:P, :], io["x"][0, P:SEQ, :], io["ctx"][0, 0:P, :], io["ctx"][0, P:CTX, :]]
        with ExitStack() as st:
            xin = at(96, 4, D)
            mod_row = at(128, 2 * D)[0:2]
            bias_row = mod_row[0:1, 3 * C:4 * C]
            filt = at(144, 2, TT, C)
            spec = at(160, 4, C)
            window = at(176, 2, C)
            fwout = at(184, 2 * C)[0:FILT_ORDER]
            dft = at(192, 2, TT, SEQ)
            vecs = at(196, P)
            zT = at(196.5, SEQ)[0:FILT_EMB]
            arg = at(197.5, 2, SEQ)[0:FILT_ORDER]
            feat = at(199.5, 2, SEQ)[0:FILT_ORDER]
            fw1 = at(201.5, FILT_ORDER)[0:FILT_EMB]
            fw23 = at(201.75, 2, FILT_ORDER)[0:FILT_ORDER]
            fcol = at(202.25, 4)[0:FILT_ORDER]
            shift = at(202.75, 2, KD)
            gain = at(203, 2, KD)
            rstd = at(203.25, 4)
            rtmp = at(203.5, 2)

            s_vec, s_x, s_con, s_flt = sem("s_vec"), [sem(f"s_x{i}") for i in range(4)], sem("s_con"), sem("s_flt")
            s_win = sem("s_win")
            silu_done, s_cols, cols_ready = sem("silu_done"), sem("s_cols"), sem("cols_ready")
            x_normed, x_turned, x_turned_kept = sem("x_normed"), sem("x_turned"), sem("x_turned_kept")
            mod_turned, s_mod, filter_full, sine_argument_ready, sine_done = sem("mod_turned"), sem("s_mod"), sem("filter_full"), sem("sine_argument_ready"), sem("sine_done")
            modulate_order, filter_windowed, spectrum_full, spectrum_kept, spectrum_stored, s_ones = (sem("modulate_order"), sem("filter_windowed"), sem("spectrum_full"), sem("spectrum_kept"),
                                                     sem("spectrum_stored"), sem("s_ones"))
            mod_w = at(96, 2, KH, N)
            mod_acc = at(176, MOD_BY_VECTOR, 2, N)
            pick = at(203.75, 3)
            filter_out_full, s_gain, s_pick, sums_ready = sem("filter_out_full"), sem("s_gain"), sem("s_pick"), sem("sums_ready")
            s_mw, sums_w_used = [sem("s_mw0"), sem("s_mw1")], sem("sums_w_used")
            block = st.enter_context(nc.Block())

            @block.sync
            def _(sp):
                sp.dma_start(vecs[V_C:V_C + 16, :], io["c"].rearrange("a (k p) -> (a k) p", p=P)).then_inc(s_vec, 16)
                sp.dma_start(vecs[V_CCTX:V_CCTX + 16, :], io["c_ctx"].rearrange("(k p) -> k p", p=P)).then_inc(s_vec, 16)
                sp.dma_start(vecs[V_NORM:V_NORM + 16, :], io["norm_pre_mix"].rearrange("a (k p) -> (a k) p", p=P)).then_inc(s_vec, 16)
                sp.dma_start(vecs[V_BSH:V_BSH + 32, :],
                             io["b_mod"][:, 0:2 * D].rearrange("a (k p) -> (a k) p", p=P)).then_inc(s_vec, 16)
                sp.dma_start(ident[:], io["k_ident"]).then_inc(s_con, 16)
                stream(sp, 0, RING)
                for i in range(4):
                    sp.dma_start(xin[:, i, :], x_rows[i]).then_inc(s_x[i], 16)
                    if i == 1:
                        stream(sp, RING, RING + 2)
                n = RING + 6
                stream(sp, RING + 2, n)
                for i in range(2 * MOD_BY_VECTOR):
                    if i < 2:
                        sp.wait_ge(x_turned, 8 * (i + 1))
                    else:
                        sp.wait_ge(sums_w_used, i - 1)
                    col = (MOD_BY_TENSOR + i // 2) * N
                    row = (i % 2) * KH * P
                    sp.dma_start(mod_w[:, i % 2, :, :],
                                 io["w_mod"][0, row:row + KH * P, col:col + N].rearrange("(k p) n -> p k n", p=P)
                                 ).then_inc(s_mw[i % 2], 16)
                    stream(sp, n, n + 1)
                    n += 1
                stream(sp, n, MODULATE_END + RING)

            @block.scalar
            def _(act):
                act.dma_start(zT[:], io["k_zT"]).then_inc(s_flt, 16)
                act.dma_start(fw1[:], io["filt_w1"][0]).then_inc(s_flt, 16)
                act.dma_start(fw23[:, 0, :], io["filt_w2"][0]).then_inc(s_flt, 16)
                act.dma_start(fw23[:, 1, :], io["filt_w3"][0]).then_inc(s_flt, 16)
                act.dma_start(fwout[:], io["filt_w_out"][0]).then_inc(s_flt, 16)
                for j, name in enumerate(("filt_b1", "filt_b2", "filt_b3", "filt_freq")):
                    act.dma_start(fcol[:, j:j + 1], io[name].rearrange("a f -> f a")).then_inc(s_flt, 16)
                act.dma_start(bias_row[:], io["hy_bias"]).then_inc(s_flt, 16)
                act.dma_start(dft[:, 0, :, :], io["k_cos"].rearrange("(t p) f -> p t f", p=P)).then_inc(s_flt, 16)
                act.dma_start(dft[:, 1, :, :], io["k_sin"].rearrange("(t p) f -> p t f", p=P)).then_inc(s_flt, 16)
                act.wait_ge(s_vec, 64)
                nc.scalar.activation(vecs[0:32, :], vecs[0:32, :], ACT.Silu).then_inc(silu_done, 1)
                for layer in range(3):
                    act.wait_ge(sine_argument_ready, layer + 1)
                    nc.scalar.activation(feat[:, layer % 2, :], arg[:, 0, :], ACT.Sin).then_inc(sine_done, 1)
                for i in range(4):
                    dst = uT if i < 2 else uctxT
                    for kq in range(4):
                        n = 4 * i + kq
                        act.wait_ge(x_turned, n + 1)
                        nc.scalar.activation(dst[:, 4 * kq:4 * kq + 4, (i % 2) * P:(i % 2) * P + P],
                                             psB[:, n % 2, :].rearrange("p (k t) -> p k t", k=4),
                                             ACT.Copy).then_inc(x_turned_kept, 1)
                for m in range(8):
                    act.wait_ge(spectrum_full, m + 1)
                    part, nh = m // 2, m % 2
                    nc.scalar.activation(spec[:, part, nh * N:(nh + 1) * N], psB[:, m % 4, :], ACT.Copy).then_inc(spectrum_kept, 1)
                act.wait_ge(spectrum_kept, 8)
                act.dma_start(filt_spec, spec[:]).then_inc(spectrum_stored, 16)
                for q in range(4):
                    act.wait_ge(s_gain, q + 1)
                    for k in range(4 * q, 4 * q + 4):
                        nc.scalar.activation(uctxT[:, k, :], uctxT[:, k, :], ACT.Identity, scale=gain[:, 1, k:k + 1],
                                             bias=shift[:, 1, k:k + 1]).then_inc(s_mod, 1)
                act.wait_ge(spectrum_stored, 16)

            @block.gpsimd
            def _(pool):
                nc.gpsimd.memset(ones[:], 1.0).then_inc(s_ones, 1)
                nc.gpsimd.memset(pick, 0.0).then_inc(s_pick, 1)
                pool.wait_ge(s_pick, 1)
                nc.gpsimd.memset(pick[:, 1:2], 1.0).then_inc(s_pick, 1)
                for t in range(TT):
                    if t:
                        pool.wait_ge(filter_windowed, 4)
                    pool.dma_start(window[:, 0, :], io["k_window"][t * P:(t + 1) * P, :]).then_inc(s_win, 16)
                    pool.dma_start(window[:, 1, :], io["k_window_b"][t * P:(t + 1) * P, :]).then_inc(s_win, 16)

            @block.tensor
            def _(pe):
                pe.wait_ge(s_con, 16)
                pe.wait_ge(silu_done, 1)
                nc.tensor.transpose(psB[:, 2, 0:80], vecs[0:80, :], ident[0:80, 0:80]).then_inc(s_cols, 1)

                def filter_layer(layer):
                    if layer == 0:
                        pe.wait_ge(s_flt, 16 * 12)
                        left, right = fw1, zT
                    else:
                        pe.wait_ge(sine_done, layer)
                        left, right = fw23[:, layer - 1, :], feat[:, (layer - 1) % 2, :]
                    nc.tensor.matmul(psB[0:FILT_ORDER, 3, 0:SEQ], left, right, start=True, stop=True).then_inc(filter_full, 1)

                def transpose_x(i):
                    pe.wait_ge(x_normed, i + 1)
                    for kq in range(4):
                        n = 4 * i + kq
                        if n >= 2:
                            pe.wait_ge(x_turned_kept, n - 1)
                        for k in range(4 * kq, 4 * kq + 4):
                            m = nc.tensor.transpose(psB[:, n % 2, (k % 4) * P:(k % 4) * P + P],
                                                    xin[:, i, k * P:(k + 1) * P], ident[:])
                        m.then_inc(x_turned, 1)

                def filter_out(t):
                    if t:
                        pe.wait_ge(filter_windowed, 4)
                    else:
                        pe.wait_ge(sine_done, 3)
                        pe.wait_ge(x_turned_kept, 16)
                    for j in range(4):
                        nc.tensor.matmul(psB[:, j, :], feat[:, 0, t * P:(t + 1) * P], fwout[:, j * N:(j + 1) * N],
                                         start=True, stop=True).then_inc(filter_out_full, 1)

                def filter_spectrum():
                    pe.wait_ge(filter_windowed, 8)
                    for part in range(4):
                        for nh in range(2):
                            q = 2 * part + nh
                            if q >= 4:
                                pe.wait_ge(spectrum_kept, q - 3)
                            f0 = (part % 2) * P
                            for t in range(TT):
                                m = nc.tensor.matmul(psB[:, q % 4, :], dft[:, part // 2, t, f0:f0 + P],
                                                     filt[:, part // 2, t, nh * N:(nh + 1) * N],
                                                     start=(t == 0), stop=(t == TT - 1))
                            m.then_inc(spectrum_full, 1)

                def rows_to_columns(first, upto):
                    pe.wait_ge(a_free, upto)
                    pe.wait_ge(spectrum_kept, 8)
                    for j in range(4 * first, 4 * upto):
                        m = nc.tensor.transpose(psB[:, 0, 2 * j:2 * j + 2], mod_row[:, j * P:(j + 1) * P], ident[0:2, 0:2])
                    m.then_inc(mod_turned, 1)

                pe.wait_ge(cols_ready, 1)
                for n in range(MODULATE_END):
                    gemm_half(pe, n, [lambda k, hf=n % 2: cols[:, hf * KH + k:hf * KH + k + 17:16]])
                    if n in (2, 3, 4):
                        filter_layer(n - 2)
                    if n in (4, 5, 6, 7):
                        transpose_x(n - 4)
                    if n in (8, 9):
                        filter_out(n - 8)
                    if n == 10:
                        filter_spectrum()
                rows_to_columns(0, MOD_BY_TENSOR)
                pe.wait_ge(s_pick, 2)
                for i in range(MOD_BY_VECTOR):
                    pe.wait_ge(sums_ready, i + 1)
                    bank = (MOD_BY_TENSOR + i) % 4
                    for r in range(2):
                        m = nc.tensor.matmul(psA[0:2, bank, :], pick[:, 1 - r:3 - r], mod_acc[:, i, r, :], start=(r == 0), stop=(r == 1))
                    m.then_inc(a_full, 1)
                rows_to_columns(MOD_BY_TENSOR, 2 * D // N)

            @block.vector
            def _(v):
                ch = Chain(v, modulate_order)
                v.wait_ge(s_cols, 1)
                nc.vector.tensor_copy(cols[:, 0:80], psB[:, 2, 0:80]).then_inc(cols_ready, 1)

                def sine_argument(layer):
                    v.wait_ge(s_flt, 16 * 12)
                    v.wait_ge(filter_full, layer + 1)
                    ch.link(nc.vector.tensor_scalar(arg[:, 0, :], psB[0:FILT_ORDER, 3, 0:SEQ], fcol[:, layer:layer + 1],
                                                    fcol[:, 3:4], ALU.add, ALU.mult))
                    ch.link(nc.vector.tensor_scalar(arg[:, 1, :], arg[:, 0, :], 0.5 / math.pi, ROUND, ALU.mult, ALU.add))
                    ch.link(nc.vector.tensor_scalar(arg[:, 1, :], arg[:, 1, :], -ROUND, None, ALU.add))
                    ch.link(nc.vector.scalar_tensor_tensor(arg[:, 0, :], arg[:, 1, :], -TWO_PI_HI, arg[:, 0, :], ALU.mult, ALU.add))
                    ch.link(nc.vector.scalar_tensor_tensor(arg[:, 0, :], arg[:, 1, :], -TWO_PI_LO, arg[:, 0, :], ALU.mult, ALU.add))
                    nc.vector.tensor_scalar(arg[:, 0, :], arg[:, 0, :], 3.1415925, -3.1415925, ALU.min, ALU.max).then_inc(sine_argument_ready, 1)

                def normalise(i):
                    v.wait_ge(s_x[i], 16)
                    ch.link(nc.vector.tensor_tensor_reduce(spec[:, 0:2, :].rearrange("p a c -> p (a c)"), xin[:, i, :],
                                                           xin[:, i, :], 1.0, 0.0, ALU.mult, ALU.add, rstd[:, i:i + 1]))
                    ch.link(nc.vector.tensor_scalar(rstd[:, i:i + 1], rstd[:, i:i + 1], 1.0 / D, EPS, ALU.mult, ALU.add))
                    rsqrt(nc, ch, rstd[:, i:i + 1], rtmp[:, 0:1], rtmp[:, 1:2])
                    nc.vector.tensor_scalar(xin[:, i, :], xin[:, i, :], rtmp[:, 0:1], None, ALU.mult).then_inc(x_normed, 1)

                def window_filter(t):
                    v.wait_ge(s_win, 32 * (t + 1))
                    for nh in range(2):
                        cs = slice(nh * N, (nh + 1) * N)
                        v.wait_ge(filter_out_full, 4 * t + nh + 3)
                        ch.link(nc.vector.tensor_tensor(window[:, 1, cs], psB[:, 2 + nh, :], window[:, 1, cs], ALU.mult))
                        ch.link(nc.vector.tensor_tensor(window[:, 0, cs], psB[:, nh, :], window[:, 0, cs], ALU.mult))
                        nc.vector.tensor_tensor(filt[:, 0, t, cs], window[:, 0, cs], window[:, 1, cs], ALU.add).then_inc(filter_windowed, 1)
                        nc.vector.tensor_tensor(filt[:, 1, t, cs], window[:, 1, cs], window[:, 0, cs], ALU.subtract).then_inc(filter_windowed, 1)
                    if t == 0:
                        v.wait_ge(filter_windowed, 4)
                        ch.link(nc.vector.tensor_tensor(filt[0:1, 0, 0, :], filt[0:1, 0, 0, :], bias_row[:], ALU.add))

                def keep_rows(j):
                    v.wait_ge(a_full, j + 1)
                    nc.vector.tensor_copy(mod_row[:, j * N:(j + 1) * N], psA[0:2, j % 4, :]).then_inc(a_free, 1)

                def sums(i):
                    c, hf = i // 2, i % 2
                    v.wait_ge(s_mw[hf], 16 * (c + 1))
                    for k in range(KH):
                        for r in range(2):
                            col, acc_ = cols[:, 16 * r + hf * KH + k:16 * r + hf * KH + k + 1], mod_acc[:, c, r, :]
                            if hf == 0 and k == 0:
                                ch.link(nc.vector.tensor_scalar(acc_, mod_w[:, hf, k, :], col, None, ALU.mult))
                            else:
                                ch.link(nc.vector.scalar_tensor_tensor(acc_, mod_w[:, hf, k, :], col, acc_, ALU.mult, ALU.add))
                    v.sem_inc(sums_w_used, 1)
                    if hf == 1:
                        v.sem_inc(sums_ready, 1)

                mc = psB[:, 0, 0:4 * KD].rearrange("p (j r) -> p j r", r=2)

                def scale(q0, q1, with_shift):
                    ks = slice(4 * q0, 4 * q1)
                    for r in range(2):
                        if with_shift:
                            ch.link(nc.vector.tensor_tensor(shift[:, r, :], mc[:, 0:KD, r], cols[:, V_BSH:V_BSH + KD], ALU.add))
                        ch.link(nc.vector.tensor_tensor(gain[:, r, ks], mc[:, KD + 4 * q0:KD + 4 * q1, r],
                                                        cols[:, V_BSC + 4 * q0:V_BSC + 4 * q1], ALU.add))
                        ch.link(nc.vector.scalar_tensor_tensor(gain[:, r, ks], gain[:, r, ks], 1.0,
                                                               cols[:, V_NORM + 4 * q0:V_NORM + 4 * q1], ALU.add, ALU.mult))
                    v.sem_inc(s_gain, q1 - q0)
                    for k in range(4 * q0, 4 * q1):
                        nc.vector.tensor_scalar(uT[:, k, :], uT[:, k, :], gain[:, 0, k:k + 1], shift[:, 0, k:k + 1],
                                                ALU.mult, ALU.add).then_inc(s_mod, 1)

                normalise(0)
                sine_argument(0)
                normalise(1)
                sine_argument(1)
                keep_rows(0)
                keep_rows(1)
                sine_argument(2)
                normalise(2)
                normalise(3)
                keep_rows(2)
                keep_rows(3)
                window_filter(0)
                window_filter(1)
                for i in range(2 * MOD_BY_VECTOR):
                    sums(i)
                    keep_rows(4 + i)
                for i in range(4 + 2 * MOD_BY_VECTOR, MOD_BY_TENSOR):
                    keep_rows(i)
                v.wait_ge(x_turned_kept, 16)
                v.wait_ge(mod_turned, 1)
                scale(0, MOD_BY_TENSOR - 4, True)
                for i in range(MOD_BY_VECTOR):
                    keep_rows(MOD_BY_TENSOR + i)
                v.wait_ge(mod_turned, 2)
                scale(MOD_BY_TENSOR - 4, 4, False)

        spec = at(184, 4, C)
        dft = at(200, 2, TT, SEQ)
        t_tmp = at(172, TT, N)
        z_tmp = at(176, TT, N)
        rope = at(180, 2, TT, HD)
        s_spec = sem("s_spec")

        def rotate(ch, x, t):
            heads = x.rearrange("p (h d) -> p h d", d=HD)
            quarter = HD // 4
            halves_ = lambda a: a.rearrange("p (h a b i) -> p h a b i", a=2, b=2, i=quarter)
            one, two = (a.rearrange("p t n -> p (t n)") for a in (z_tmp, t_tmp))
            cos = rope[:, 0, t, :].unsqueeze(1).broadcast_to((P, 2 * HEADS, HD))
            ch.link(nc.vector.tensor_tensor(one.rearrange("p (h d) -> p h d", d=HD), heads, cos, ALU.mult))
            for b in range(2):
                sin = rope[:, 1, t, :].rearrange("p (a b i) -> p a b i", a=2, b=2)[:, :, b, :]
                sin = sin.unsqueeze(1).broadcast_to((P, 2 * HEADS, 2, quarter))
                ch.link(nc.vector.tensor_tensor(halves_(two)[:, :, :, b, :], halves_(x)[:, :, :, 1 - b, :], sin, ALU.mult))
            ch.link(nc.vector.tensor_tensor(x, one, two, ALU.add))

        with ExitStack() as st:
            p_in = at(152, TT, N)
            p_prev = at(156, TT, N)
            p_next = at(160, TT, N)
            taps = at(164, 3, N)
            tap_bias = at(170, N)
            wm = at(164, 4, 2, C)
            acc = at(196, 2, C)
            H_CHUNKS = 3 * C // N
            KV_CHUNKS = 2 * C // N
            VECS = 4
            WM = 4

            s_wm = [sem(f"s_wm{b}") for b in range(WM)]
            mod_w_used, mod_acc_ready, mod_row_full, mod_row_kept = sem("mod_w_used"), sem("mod_acc_ready"), sem("mod_row_full"), sem("mod_row_kept")
            mod_row_stored, mod_acc_free = sem("mod_row_stored"), sem("mod_acc_free")
            s_zero, s_zout, p_stored, s_shift, s_taps, conv_done = (sem("s_zero"), sem("s_zout"), sem("p_stored"),
                                                               sem("s_shift"), sem("s_taps"), sem("conv_done"))
            s_rope, project_order, mod_order = sem("s_rope"), sem("project_order"), sem("mod_order")
            block = st.enter_context(nc.Block())
            first_bank = place[MODULATE_END][0]
            kv_bank = first_bank
            hy_bank = kv_bank + KV_CHUNKS * 2 * TT

            def bank_of(j):
                return hy_bank + TT * HY_Q_ORDER.index(j)

            @block.sync
            def _(sp):
                n = MODULATE_END + RING
                for i in range(8 * VECS * 2):
                    vec, half, kp = i // 16, (i // 8) % 2, i % 8
                    if i >= WM:
                        sp.wait_ge(mod_w_used, i - WM + 1)
                    col = (2 + vec) * D + half * C
                    sp.dma_start(wm[:, i % WM, :, :],
                                 io["w_mod"][0, 2 * kp * P:2 * (kp + 1) * P, col:col + C].rearrange("(k p) n -> p k n", p=P)
                                 ).then_inc(s_wm[i % WM], 16)
                    if i % 8 == 7:
                        stream(sp, n, n + 1)
                        n += 1
                stream(sp, n, PROJECT_END + RING)

            @block.scalar
            def _(act):
                act.sem_inc(mod_acc_free, 2)

                def evacuate(bank, dst):
                    act.wait_ge(a_full, bank + 1)
                    return nc.scalar.activation(dst, psA[:, bank % 4, :], ACT.Copy).then_inc(a_free, 1)

                def mod_row_out(i):
                    act.wait_ge(mod_row_full, i + 1)
                    nc.scalar.activation(acc[0:1, i % 2, :], psB[0:1, 2 * (i % 2):2 * (i % 2) + 2, :].rearrange("p a n -> p (a n)"),
                                         ACT.Copy).then_inc(mod_row_kept, 1)
                    act.wait_ge(mod_row_kept, i + 1)
                    act.dma_start(mod_rows[i // 2:i // 2 + 1, (i % 2) * C:(i % 2 + 1) * C], acc[0:1, i % 2, :]).then_inc(mod_row_stored, 16)
                    act.wait_ge(mod_row_stored, 16 * (i + 1))
                    act.sem_inc(mod_acc_free, 1)

                for j in range(KV_CHUNKS):
                    dst = (k_all, v_all)[j // 2]
                    if j:
                        mod_row_out(2 * j - 1)
                    for i in range(2 * TT):
                        evacuate(kv_bank + 2 * TT * j + i, dst[:, i, (j % 2) * N:(j % 2 + 1) * N])
                    mod_row_out(2 * j)
                for j in HY_Q_ORDER:
                    if j >= H_CHUNKS:
                        c0 = (j - H_CHUNKS) * N
                        for t in range(TT):
                            evacuate(bank_of(j) + t, q_lat[:, t, c0:c0 + N])
                        continue
                    if j:
                        act.wait_ge(conv_done, j)
                        act.wait_ge(p_stored, 16 * j)
                    for t in range(TT):
                        evacuate(bank_of(j) + t, p_in[:, t, :])
                    if j == 0:
                        mod_row_out(2 * VECS - 1)
                        act.dma_start(spec, filt_spec).then_inc(s_spec, 16)
                        act.dma_start(dft[:, 0, :, :], io["k_cos"].rearrange("(t p) f -> p t f", p=P)).then_inc(s_spec, 16)
                        act.dma_start(dft[:, 1, :, :], io["k_sin"].rearrange("(t p) f -> p t f", p=P)).then_inc(s_spec, 16)

            @block.gpsimd
            def _(pool):
                pool.wait_ge(mod_acc_ready, 2 * VECS)
                nc.gpsimd.memset(z_tmp[0:3, :, :], 0.0).then_inc(s_zero, 1)
                pool.wait_ge(s_zero, 1)
                zeros = z_tmp[0:3, :, :].rearrange("p t n -> p (t n)")
                pool.dma_start(shifted[0, :].rearrange("(a n) -> a n", n=C), zeros).then_inc(s_zout, 16)
                pool.dma_start(shifted[SEQ + 1, :].rearrange("(a n) -> a n", n=C), zeros).then_inc(s_zout, 16)
                pool.wait_ge(s_zout, 32)
                for j in range(H_CHUNKS):
                    cs = slice(j * N, (j + 1) * N)
                    if j:
                        pool.wait_ge(conv_done, j)
                    pool.dma_start(taps, io["hy_conv_w"][0, :, cs].partition_broadcast(P)).then_inc(s_taps, 16)
                    pool.dma_start(tap_bias, io["hy_conv_b"][0, cs].partition_broadcast(P)).then_inc(s_taps, 16)
                    pool.wait_ge(a_free, bank_of(j) + TT)
                    pool.dma_start(shifted[1:SEQ + 1, cs].rearrange("(t p) n -> p t n", p=P), p_in).then_inc(p_stored, 16)
                    pool.wait_ge(p_stored, 16 * (j + 1))
                    pool.dma_start(p_prev, shifted[0:SEQ, cs].rearrange("(t p) n -> p t n", p=P)).then_inc(s_shift, 16)
                    pool.dma_start(p_next, shifted[2:SEQ + 2, cs].rearrange("(t p) n -> p t n", p=P)).then_inc(s_shift, 16)
                    if j == 0:
                        pool.dma_start(rope[:, 0, :, :], io["k_rope_cos"].rearrange("(t p) d -> p t d", p=P)).then_inc(s_rope, 16)
                        pool.dma_start(rope[:, 1, :, :], io["k_rope_sin"].rearrange("(t p) d -> p t d", p=P)).then_inc(s_rope, 16)

            @block.tensor
            def _(pe):
                def token_tile(src, t, half):
                    return lambda k: src[:, half * KH + k, t * P:(t + 1) * P]

                def mod_sum(i):
                    pe.wait_ge(mod_acc_ready, i + 1)
                    if i >= 2:
                        pe.wait_ge(mod_row_kept, i - 1)
                    for q in range(2):
                        last = nc.tensor.matmul(psB[0:1, 2 * (i % 2) + q, :], ones[:], acc[:, i % 2, q * N:(q + 1) * N],
                                                start=True, stop=True)
                    last.then_inc(mod_row_full, 1)

                n = MODULATE_END
                for j in range(KV_CHUNKS):
                    for half in range(2):
                        gemm_half(pe, n, [token_tile(uT, t, half) for t in range(TT)]
                                  + [token_tile(uctxT, t, half) for t in range(TT)])
                        n += 1
                        if j or half:
                            mod_sum(2 * j + half - 1)
                for j in HY_Q_ORDER:
                    for half in range(2):
                        gemm_half(pe, n, [token_tile(uT, t, half) for t in range(TT)])
                        n += 1
                    if j == 0:
                        mod_sum(2 * VECS - 1)

            @block.vector
            def _(v):
                MOD_LINKS = KD
                with v.Fori(0, VECS) as vec:
                    for half in range(2):
                        ch = Chain(v, mod_order, (2 * vec + half) * MOD_LINKS)
                        for kp in range(8):
                            v.wait_ge(s_wm[kp % WM], (vec * 4 + half * 2 + kp // WM + 1) * 16)
                            if kp == 0:
                                v.wait_ge(mod_acc_free, 2 * vec + half + 1)
                            for j in range(2):
                                k = 2 * kp + j
                                if k == 0:
                                    ins = nc.vector.tensor_scalar(acc[:, half, :], wm[:, 0, 0, :], cols[:, 0:1], None, ALU.mult)
                                else:
                                    ins = nc.vector.scalar_tensor_tensor(acc[:, half, :], wm[:, kp % WM, j, :], cols[:, k:k + 1],
                                                                         acc[:, half, :], ALU.mult, ALU.add)
                                ch.link(ins)
                            v.sem_inc(mod_w_used, 1)
                        assert ch.n == MOD_LINKS
                        v.sem_inc(mod_acc_ready, 1)

                ch = Chain(v, project_order)

                def over_tiles(w):
                    return w.unsqueeze(1).broadcast_to((P, TT, N))

                for j in range(H_CHUNKS):
                    cs = slice((j % 2) * N, (j % 2 + 1) * N)
                    v.wait_ge(s_taps, 32 * (j + 1))
                    v.wait_ge(s_shift, 32 * (j + 1))
                    ch.link(nc.vector.tensor_tensor(z_tmp, p_in, over_tiles(taps[:, 1, :]), ALU.mult))
                    for other, w in ((p_prev, 0), (p_next, 2)):
                        ch.link(nc.vector.tensor_tensor(t_tmp, other, over_tiles(taps[:, w, :]), ALU.mult))
                        ch.link(nc.vector.tensor_tensor(z_tmp, z_tmp, t_tmp, ALU.add))
                    bias = over_tiles(tap_bias)
                    if j // 2 == 0:
                        ch.link(nc.vector.tensor_tensor(hy_u[:, :, cs], z_tmp, bias, ALU.add))
                    elif j // 2 == 1:
                        ch.link(nc.vector.tensor_tensor(z_tmp, z_tmp, bias, ALU.add))
                        ch.link(nc.vector.tensor_tensor(hy_u[:, :, cs], hy_u[:, :, cs], z_tmp, ALU.mult))
                    else:
                        ch.link(nc.vector.tensor_tensor(hy_x0[:, :, cs], z_tmp, bias, ALU.add))
                    v.sem_inc(conv_done, 1)
                    if j == 2:
                        v.wait_ge(s_rope, 32)
                        for t in range(TT):
                            rotate(ch, k_all[:, t, :], t)


        neg_lam = small[:, 0:1]
        with ExitStack() as st:
            tmp = at(152, 2, N)
            idft = at(156, 2, TT, SEQ)
            y_re = at(160, TT, C)
            y_im = hy_u
            lam_in = small[:, 8:8 + 4 * HD].rearrange("p (a d) -> p a d", a=4)
            lam_sum = small[:, 1:3]
            lam_exp = small[:, 3:5]
            s_idft, s_lam, s_lsum, s_lexp = sem("s_idft"), sem("s_lam"), sem("s_lsum"), sem("s_lexp")
            u_transformed, product_ready, kq_turned, kq_turned_kept, inverse_full, y_turned, s_yt_e, s_y = (
                sem("u_transformed"), sem("product_ready"), sem("kq_turned"), sem("kq_turned_kept"), sem("inverse_full"), sem("y_turned"), sem("s_yt_e"), sem("s_y"))
            convolve_order, s_qrot = sem("convolve_order"), sem("s_qrot")
            block = st.enter_context(nc.Block())

            @block.scalar
            def _(act):
                act.dma_start(idft[:, 0, :, :], io["k_icos"].rearrange("(t p) f -> p t f", p=P)).then_inc(s_idft, 16)
                act.dma_start(idft[:, 1, :, :], io["k_isin"].rearrange("(t p) f -> p t f", p=P)).then_inc(s_idft, 16)
                act.dma_start(small[:, 8:8 + 4 * HD], io["da_lambda"][0].rearrange("a d -> (a d)").partition_broadcast(P)).then_inc(s_lam, 16)
                for h in range(HEADS):
                    act.wait_ge(kq_turned, h + 1)
                    nc.scalar.activation(kT[:, h, :], psA[:, h % 4, :], ACT.Copy).then_inc(kq_turned_kept, 1)
                act.wait_ge(product_ready, 2)
                for h in range(0, HEADS, 2):
                    act.wait_ge(kq_turned, HEADS + h // 2 + 1)
                    nc.scalar.activation(qT[:, h:h + 2, :], psA[:, (h // 2) % 4, :].rearrange("p (h t) -> p h t", h=2),
                                         ACT.Copy).then_inc(kq_turned_kept, 1)
                for n in range(2 * TT):
                    act.wait_ge(y_turned, n + 1)
                    t, kq = n // 2, n % 2
                    nc.scalar.activation(y_hyT[:, 4 * kq:4 * kq + 4, t * P:(t + 1) * P],
                                         psA[:, n, :].rearrange("p (k t) -> p k t", k=4), ACT.Copy).then_inc(s_yt_e, 1)
                act.wait_ge(s_lsum, 1)
                nc.scalar.activation(lam_exp, lam_sum, ACT.Exp).then_inc(s_lexp, 1)

            @block.tensor
            def _(pe):
                pe.wait_ge(s_spec, 48)
                for nh, ps in ((0, psA), (1, psB)):
                    for part in range(4):
                        f0 = (part % 2) * P
                        for t in range(TT):
                            last = nc.tensor.matmul(ps[:, part, :], dft[:, part // 2, t, f0:f0 + P],
                                                    hy_u[:, t, nh * N:(nh + 1) * N], start=(t == 0), stop=(t == TT - 1))
                    last.then_inc(u_transformed, 1)
                pe.wait_ge(product_ready, 1)
                for h in range(HEADS):
                    if h >= 4:
                        pe.wait_ge(kq_turned_kept, h - 3)
                    for t in range(2 * TT):
                        last = nc.tensor.transpose(psA[:, h % 4, t * P:(t + 1) * P], k_all[:, t, h * P:(h + 1) * P], ident[:])
                    last.then_inc(kq_turned, 1)
                pe.wait_ge(s_qrot, 1)
                for h in range(0, HEADS, 2):
                    pe.wait_ge(kq_turned_kept, HEADS + h // 2 - 3)
                    for i in range(2):
                        for t in range(TT):
                            last = nc.tensor.transpose(psA[:, (h // 2) % 4, i * SEQ + t * P:i * SEQ + (t + 1) * P],
                                                       q_lat[:, t, (h + i) * P:(h + i + 1) * P], ident[:])
                    last.then_inc(kq_turned, 1)
                pe.wait_ge(s_idft, 32)
                pe.wait_ge(product_ready, 2)
                for t in range(TT):
                    for nh in range(2):
                        for f in range(TT):
                            nc.tensor.matmul(psB[:, 2 * t + nh, :], idft[:, 0, f, t * P:(t + 1) * P],
                                             y_re[:, f, nh * N:(nh + 1) * N], start=(f == 0), stop=False)
                        for f in range(TT):
                            last = nc.tensor.matmul(psB[:, 2 * t + nh, :], idft[:, 1, f, t * P:(t + 1) * P],
                                                    y_im[:, f, nh * N:(nh + 1) * N], start=False, stop=(f == TT - 1))
                        last.then_inc(inverse_full, 1)
                pe.wait_ge(kq_turned_kept, HEADS + HEADS // 2)
                for n in range(2 * TT):
                    t, kq = n // 2, n % 2
                    pe.wait_ge(s_y, n + 1)
                    for k in range(4):
                        c0 = (4 * kq + k) * P
                        last = nc.tensor.transpose(psA[:, n, k * P:(k + 1) * P], hy_x0[:, t, c0:c0 + P], ident[:])
                    last.then_inc(y_turned, 1)

            @block.vector
            def _(v):
                ch = Chain(v, convolve_order)
                for t in range(TT):
                    rotate(ch, q_lat[:, t, :], t)
                v.sem_inc(s_qrot, 1)
                for nh, ps in ((0, psA), (1, psB)):
                    v.wait_ge(u_transformed, 2)
                    cs = slice(nh * N, (nh + 1) * N)
                    for f in range(TT):
                        re, im, k_re, k_im = ps[:, f, :], ps[:, 2 + f, :], spec[:, f, cs], spec[:, 2 + f, cs]
                        ch.link(nc.vector.tensor_tensor(tmp[:, 0, :], re, k_re, ALU.mult))
                        ch.link(nc.vector.tensor_tensor(tmp[:, 1, :], im, k_im, ALU.mult))
                        ch.link(nc.vector.tensor_tensor(y_re[:, f, cs], tmp[:, 0, :], tmp[:, 1, :], ALU.add))
                        ch.link(nc.vector.tensor_tensor(tmp[:, 0, :], re, k_im, ALU.mult))
                        ch.link(nc.vector.tensor_tensor(tmp[:, 1, :], im, k_re, ALU.mult))
                        ch.link(nc.vector.tensor_tensor(y_im[:, f, cs], tmp[:, 0, :], tmp[:, 1, :], ALU.subtract))
                    v.sem_inc(product_ready, 1)
                v.wait_ge(s_lam, 16)
                for i in range(2):
                    ch.link(nc.vector.tensor_tensor_reduce(tmp[:, 0, 0:HD], lam_in[:, 2 * i, :], lam_in[:, 2 * i + 1, :],
                                                           1.0, 0.0, ALU.mult, ALU.add, lam_sum[:, i:i + 1]))
                v.sem_inc(s_lsum, 1)
                for t in range(TT):
                    for nh in range(2):
                        v.wait_ge(inverse_full, 2 * t + nh + 1)
                        cs = slice(nh * N, (nh + 1) * N)
                        nc.vector.tensor_tensor(hy_x0[:, t, cs], psB[:, 2 * t + nh, :], hy_x0[:, t, cs], ALU.mult).then_inc(s_y, 1)
                v.wait_ge(s_lexp, 1)
                ch.link(nc.vector.tensor_tensor(neg_lam, lam_exp[:, 1:2], lam_exp[:, 0:1], ALU.subtract))
                ch.link(nc.vector.tensor_scalar(neg_lam, neg_lam, -LAM_INIT, None, ALU.add))

        o_all = at(168, TT, C)
        squares = at(177, 2 * HEADS)
        o_rstd = at(177.25, 2 * HEADS)
        r_tmp = at(177.5, 2 * HEADS)
        subln = at(178.5, P)
        s_sub = sem("s_sub")
        with ExitStack() as st:
            probs = at(144, 2, 4, KV)
            aT = at(160, 2, 2 * TT, SEQ)
            stat = at(176, 2, 4, 4)
            junk = at(178, P)
            scores_full, s_max, s_exp, difference_ready, a_turned, a_turned_kept, pv_full, s_o, attend_order = (
                sem("scores_full"), sem("s_max"), sem("s_exp"), sem("difference_ready"), sem("a_turned"), sem("a_turned_kept"),
                sem("pv_full"), sem("s_o"), sem("attend_order"))
            block = st.enter_context(nc.Block())
            gate_bank = place[PROJECT_END][0]
            SCALE = HD ** -0.5

            @block.sync
            def _(sp):
                sp.dma_start(subln, io["da_subln"][0].partition_broadcast(P)).then_inc(s_sub, 16)
                stream(sp, PROJECT_END + RING, ATTEND_END + RING)

            @block.scalar
            def _(act):
                for h in range(HEADS):
                    for i in range(4):
                        act.wait_ge(s_max, 4 * h + i + 1)
                        nc.scalar.activation(probs[:, h % 2, i, :], psB[:, i, :], ACT.Exp, scale=SCALE,
                                             bias=stat[:, h % 2, 0, i:i + 1],
                                             accum_out=stat[:, h % 2, 1, i:i + 1]).then_inc(s_exp, 1)
                    for t in range(TT):
                        act.wait_ge(a_turned, TT * h + t + 1)
                        nc.scalar.activation(aT[:, h % 2, :, t * P:(t + 1) * P],
                                             psB[:, t, :].rearrange("p (k t) -> p k t", k=4), ACT.Copy).then_inc(a_turned_kept, 1)
                    for t in range(TT):
                        act.wait_ge(a_full, gate_bank + TT * h + t + 1)
                        nc.scalar.activation(gates[:, t, h * N:(h + 1) * N], psA[:, (gate_bank + TT * h + t) % 4, :],
                                             ACT.Tanh, scale=0.5).then_inc(a_free, 1)

            @block.tensor
            def _(pe):
                for h in range(HEADS):
                    if h:
                        pe.wait_ge(s_o, TT * h)
                    for i in range(4):
                        comp, t = i // TT, i % TT
                        d0 = comp * HD
                        nc.tensor.matmul(psB[:, i, :], qT[d0:d0 + HD, h, t * P:(t + 1) * P], kT[d0:d0 + HD, h, :],
                                         start=True, stop=True).then_inc(scores_full, 1)
                    n = PROJECT_END + 2 * h
                    gemm_half(pe, n, [lambda k, t=t: uT[:, k, t * P:(t + 1) * P] for t in range(TT)])
                    for t in range(TT):
                        pe.wait_ge(difference_ready, TT * h + t + 1)
                        for b in range(4):
                            last = nc.tensor.transpose(psB[:, t, b * P:(b + 1) * P], probs[:, h % 2, t, b * P:(b + 1) * P], ident[:])
                        last.then_inc(a_turned, 1)
                    gemm_half(pe, n + 1, [lambda k, t=t: uT[:, KH + k, t * P:(t + 1) * P] for t in range(TT)])
                    for t in range(TT):
                        pe.wait_ge(a_turned_kept, TT * h + t + 1)
                        for b in range(4):
                            last = nc.tensor.matmul(psB[:, 2 + t, 0:P], aT[:, h % 2, b, t * P:(t + 1) * P],
                                                    v_all[:, b, h * P:(h + 1) * P], start=(b == 0), stop=(b == 3))
                        last.then_inc(pv_full, 1)

            @block.vector
            def _(v):
                ch = Chain(v, attend_order)
                for h in range(HEADS):
                    st_ = stat[:, h % 2, :, :]
                    for i in range(4):
                        v.wait_ge(scores_full, 4 * h + i + 1)
                        ch.link(nc.vector.tensor_reduce(st_[:, 0, i:i + 1], psB[:, i, :], AX.X, ALU.max))
                        nc.vector.tensor_scalar(st_[:, 0, i:i + 1], st_[:, 0, i:i + 1], -SCALE, None, ALU.mult).then_inc(s_max, 1)
                    v.wait_ge(s_exp, 4 * h + 4)
                    ch.link(nc.vector.reciprocal(st_[:, 2, :], st_[:, 1, :]))
                    ch.link(nc.vector.tensor_scalar(st_[:, 2, TT:4], st_[:, 2, TT:4], neg_lam, None, ALU.mult))
                    for t in range(TT):
                        one, two = probs[:, h % 2, t, :], probs[:, h % 2, TT + t, :]
                        ch.link(nc.vector.tensor_scalar(one, one, st_[:, 2, t:t + 1], None, ALU.mult))
                        nc.vector.scalar_tensor_tensor(one, two, st_[:, 2, TT + t:TT + t + 1], one, ALU.mult, ALU.add).then_inc(difference_ready, 1)
                    for t in range(TT):
                        v.wait_ge(pv_full, TT * h + t + 1)
                        o = o_all[:, t, h * P:(h + 1) * P]
                        nc.vector.tensor_copy(o, psB[:, 2 + t, 0:P]).then_inc(s_o, 1)
                        v.wait_ge(s_o, TT * h + t + 1)
                        ch.link(nc.vector.tensor_tensor_reduce(junk, o, o, 1.0, 0.0, ALU.mult, ALU.add,
                                                               squares[:, t * HEADS + h:t * HEADS + h + 1]))

        x1 = at(128, TT, D)
        h = at(144, TT, D)
        scores = at(160, TT, HP, N_KEYS)
        g2_row = at(184, D)

        total = at(176, D)
        s_key = at(192, 2, 2, N_KEYS)
        cand = at(194, N_KEYS * 2)
        hot = at(195, TOPK, TOPK)
        iota = at(196, TOPK)
        top_v = at(196.25, 2, TOPK)
        top_vu = at(196.5, 2, TOPK).bitcast(U32)
        top_vf = at(196.75, 2, TOPK)
        best = at(197, 2, TOPK)
        best_u = at(197.25, TOPK).bitcast(U32)
        ab_u = at(197.5, 2, TOPK).bitcast(U32)
        ab = at(197.75, 2, TOPK)
        pick = at(198, 2, TOPK)
        rows = at(198.25, 2, TOPK).bitcast(U32)
        neg_max = at(198.5, 2)
        e_sum = at(198.75, 2, 2)
        e_g = at(199, 2, TOPK)
        dots = at(199.25, 2, TOPK)
        act_ = at(199.5, 2, TOPK)
        wgt = at(199.75, 2, TOPK)
        all_scores = scores.rearrange("p t b k -> p (t b) k")
        u_tab, v_tab = io["peer_u"][0], io["peer_v"][0]
        s_iota, rows_chosen, s_gathers, best_ready, exp_done, dots_ready, gelu_done, weigh_order, choose_order, s_step = (
            sem("s_iota"), sem("rows_chosen"), sem("s_gathers"), sem("best_ready"), sem("exp_done"), sem("dots_ready"), sem("gelu_done"),
            sem("weigh_order"), sem("choose_order"), sem("s_step"))
        TOP_LINKS = 27

        def gather(table, par, j, dst):
            return nc.gpsimd.indirect_dma_start(
                out=dst, out_offset=None, in_=table,
                in_offset=bass.IndirectOffsetOnAxis(ap=rows[:, par, j:j + 1], axis=0))

        def softmax_terms(act, head, par):
            act.wait_ge(best_ready, head + 1)
            nc.scalar.activation(e_g[:, par, :], best[:, par, :], ACT.Exp, bias=neg_max[:, par:par + 1],
                                 accum_out=e_sum[:, par, 0:1]).then_inc(exp_done, 1)

        def gelu(act, head, par):
            act.wait_ge(dots_ready, head + 1)
            nc.scalar.activation(act_[:, par, :], dots[:, par, :], ACT.Gelu).then_inc(gelu_done, 1)

        def top16(ch, values, out_v, out_i):
            ch.link(nc.vector.max(out=out_v[:, 0:8], in_=values), s_step)
            ch.link(nc.vector.max_index(out=out_i[:, 0:8], in_max=out_v[:, 0:8], in_values=values), s_step)
            ch.link(nc.vector.match_replace(out=values, in_to_replace=out_v[:, 0:8], in_values=values, imm_value=LOWEST), s_step)
            ch.link(nc.vector.max(out=out_v[:, 8:16], in_=values), s_step)
            ch.link(nc.vector.max_index(out=out_i[:, 8:16], in_max=out_v[:, 8:16], in_values=values), s_step)

        def choose(v, head, par):
            ch = Chain(v, choose_order, head * TOP_LINKS)
            ch.link(nc.vector.tensor_copy(s_key[:, par, :, :], all_scores[:, bass.ds(2 * head, 2), :]), s_step)
            for i in range(2):
                top16(ch, s_key[:, par, i, :], top_v[:, i, :], top_vu[:, i, :])
            ch.link(nc.vector.tensor_copy(top_vf, top_vu))
            a_side = top_v[:, 0, :].unsqueeze(2).broadcast_to((P, TOPK, TOPK))
            b_side = top_v[:, 1, :].unsqueeze(1).broadcast_to((P, TOPK, TOPK))
            ch.link(nc.vector.tensor_tensor(cand.rearrange("p (a b) -> p a b", b=TOPK), a_side, b_side, ALU.add), s_step)
            top16(ch, cand, best[:, par, :], best_u)
            nc.vector.tensor_scalar(neg_max[:, par:par + 1], best[:, par, 0:1], -1.0, None, ALU.mult).then_inc(best_ready, 1)
            ch.link(nc.vector.tensor_scalar(ab_u[:, 0, :], best_u, 4, None, ALU.logical_shift_right))
            ch.link(nc.vector.tensor_scalar(ab_u[:, 1, :], best_u, TOPK - 1, None, ALU.bitwise_and))
            ch.link(nc.vector.tensor_copy(ab, ab_u))
            for i in range(2):
                where = ab[:, i, :].unsqueeze(2).broadcast_to((P, TOPK, TOPK))
                numbers = iota.unsqueeze(1).broadcast_to((P, TOPK, TOPK))
                of_key = top_vf[:, i, :].unsqueeze(1).broadcast_to((P, TOPK, TOPK))
                ch.link(nc.vector.tensor_tensor(hot, where, numbers, ALU.is_equal))
                ch.link(nc.vector.tensor_tensor(hot, hot, of_key, ALU.mult))
                ch.link(nc.vector.tensor_reduce(pick[:, i, :], hot, AX.X, ALU.add))
            nc.vector.scalar_tensor_tensor(rows[:, par, :], pick[:, 0, :], float(N_KEYS), pick[:, 1, :],
                                           ALU.mult, ALU.add).then_inc(rows_chosen, 1)
            assert ch.n == TOP_LINKS, ch.n

        def dot(row, t, par, j):
            return nc.vector.tensor_tensor_reduce(row, row, h[:, t, :], 1.0, 0.0, ALU.mult, ALU.add, dots[:, par, j:j + 1])

        def weigh(v, head, par):
            v.wait_ge(exp_done, head + 1)
            ch = Chain(v, weigh_order, head * 3)
            ch.link(nc.vector.reciprocal(e_sum[:, par, 1:2], e_sum[:, par, 0:1]))
            ch.link(nc.vector.tensor_scalar(e_g[:, par, :], e_g[:, par, :], e_sum[:, par, 1:2], None, ALU.mult))
            v.wait_ge(gelu_done, head + 1)
            ch.link(nc.vector.tensor_tensor(wgt[:, par, :], e_g[:, par, :], act_[:, par, :], ALU.mult))

        def add_row(row, par, j):
            return nc.vector.scalar_tensor_tensor(total, row, wgt[:, par, j:j + 1], total, ALU.mult, ALU.add)

        with ExitStack() as st:
            m = at(64, TT, D)
            mT = at(80, KD, SEQ)
            da_part = at(144, TT, N)
            mix = h
            x_in = at(160, TT, D)
            g1_row = at(176, D)
            gain_row = at(112, D)
            shift_row = at(120, D)
            row_tmp = at(196, D)
            hT = at(64, KD, SEQ)
            q = at(80, TT, N)
            q_T = at(84, 4, SEQ)
            first_rows = [at(kb, D) for kb in (88, 96, 112, 120)]
            keys = at(96, HP, DK_HALF)
            keysT = at(104, HP, N_KEYS)
            rs = small[:, 8:16]
            mix_sq = small[:, 16:16 + TT * (D // N)].rearrange("p (t j) -> p t j", t=TT)
            x1_sq = small[:, 32:32 + TT]
            mix_junk = at(192, N)
            sq_junk = at(196, D)
            s_keys, keys_turned, keys_turned_kept, y_da_turned, y_da_kept, s_m, m_turned, m_turned_kept = (
                sem("s_keys"), sem("keys_turned"), sem("keys_turned_kept"), sem("y_da_turned"), sem("y_da_kept"), sem("s_m"), sem("m_turned"), sem("m_turned_kept"))
            s_row, s_rowd, s_xin, s_mix, s_h, h_turned, h_turned_kept, q_turned, q_turned_kept, peer_scores_full, peer_scores_kept, merge_order = (
                sem("s_row"), sem("s_rowd"), sem("s_xin"), sem("s_mix"), sem("s_h"), sem("h_turned"), sem("h_turned_kept"),
                sem("q_turned"), sem("q_turned_kept"), sem("peer_scores_full"), sem("peer_scores_kept"), sem("merge_order"))
            block = st.enter_context(nc.Block())
            s_rdst = [sem(f"s_rdst{r}") for r in range(4)]
            e_slot, e_used = [sem(f"e_slot{i}") for i in range(len(first_rows))], sem("e_used")
            s_onorm, squares_done, s_x1 = sem("s_onorm"), sem("squares_done"), sem("s_x1done")
            m_bank = place[ATTEND_END][0]
            o_bank = place[BRANCH_END][0]
            pq_bank = place[OUT_END][0]
            CH = D // N
            ROWS = [(0, 2, "norm_post_mix", g1_row), (1, 3, None, shift_row), (2, 4, "norm_pre_ffn", gain_row),
                    (3, 5, "norm_post_ffn", g2_row)]

            @block.sync
            def _(sp):
                stream(sp, ATTEND_END + RING, ALL_END)

            @block.gpsimd
            def _(pool):
                used = 0
                for r, b, norm, dst in ROWS:
                    if r == 0:
                        pool.wait_ge(a_full, m_bank + 4 * CH - TT)
                    if r == 1:
                        pool.wait_ge(s_m, TT * CH)
                    pool.dma_start(dst, mod_rows[r].partition_broadcast(P)).then_inc(s_rdst[r], 16)
                    if used:
                        pool.wait_ge(s_rowd, used)
                    pool.dma_start(row_tmp, io["b_mod"][0, b * D:(b + 1) * D].partition_broadcast(P)).then_inc(s_row, 16)
                    used += 1
                    if norm:
                        pool.wait_ge(s_rowd, used)
                        pool.dma_start(row_tmp, io[norm][0].partition_broadcast(P)).then_inc(s_row, 16)
                        used += 1
                pool.wait_ge(s_h, 4 * TT)
                pool.dma_start(iota, io["k_iota"]).then_inc(s_iota, 16)
                pool.wait_ge(rows_chosen, 1)
                slots_n = len(first_rows)
                for g in range(2 * TOPK):
                    if g >= slots_n:
                        pool.wait_ge(e_used, g - slots_n + 1)
                    gather((u_tab, v_tab)[g // TOPK], 0, g % TOPK, first_rows[g % slots_n]).then_inc(e_slot[g % slots_n], 16)

            @block.scalar
            def _(act):
                def evacuate(bank, dst, **how):
                    act.wait_ge(a_full, bank + 1)
                    return nc.scalar.activation(dst, psA[:, bank % 4, :], ACT.Copy, **how).then_inc(a_free, 1)

                for n in range(2 * TT):
                    act.wait_ge(y_da_turned, n + 1)
                    t, kq = n // 2, n % 2
                    nc.scalar.activation(y_daT[:, 4 * kq:4 * kq + 4, t * P:(t + 1) * P],
                                         psB[:, n, :].rearrange("p (k t) -> p k t", k=4), ACT.Copy).then_inc(y_da_kept, 1)
                act.wait_ge(y_da_turned, 4)
                for t in range(TT):
                    act.dma_start(x_in[:, t, :], io["x"][0, t * P:(t + 1) * P, :]).then_inc(s_xin, 16)
                for j in range(CH):
                    for t in range(TT):
                        act.wait_ge(m_turned, TT * j + t + 1)
                        nc.scalar.activation(mT[:, 4 * j:4 * j + 4, t * P:(t + 1) * P],
                                             psB[:, 2 * (j % 2) + t, :].rearrange("p (k t) -> p k t", k=4),
                                             ACT.Copy, scale=0.5).then_inc(m_turned_kept, 1)
                act.dma_start(keys.rearrange("n (h a) d -> n h a d", a=2)[:, :, 0, :],
                              io["peer_keys"][0, 0].rearrange("h n d -> n h d")).then_inc(s_keys, 16)
                act.dma_start(keys.rearrange("n (h a) d -> n h a d", a=2)[:, :, 1, :],
                              io["peer_keys"][0, 1].rearrange("h n d -> n h d")).then_inc(s_keys, 16)
                for j in range(CH):
                    for t in range(TT):
                        act.wait_ge(a_full, o_bank + TT * j + t + 1)
                        bank = psA[:, (o_bank + TT * j + t) % 4, :]
                        nc.scalar.activation(mix[:, t, j * N:(j + 1) * N], bank, ACT.Copy).then_inc(s_mix, 1)
                        nc.scalar.activation(mix_junk, bank, ACT.Square, accum_out=mix_sq[:, t, j:j + 1]).then_inc(squares_done, 1)
                        act.wait_ge(s_mix, TT * j + t + 1)
                        act.wait_ge(squares_done, TT * j + t + 1)
                        act.sem_inc(a_free, 1)
                    if j == 0:
                        for n in range(4):
                            act.wait_ge(keys_turned, n + 1)
                            nc.scalar.activation(keysT[:, 4 * n:4 * n + 4, :], psB[:, n, :].rearrange("p (b k) -> p b k", b=4),
                                                 ACT.Copy).then_inc(keys_turned_kept, 1)
                for n in range(TT * 4):
                    if n % 4 == 0:
                        act.wait_ge(s_x1, n // 4 + 1)
                        nc.scalar.activation(sq_junk, x1[:, n // 4, :], ACT.Square, accum_out=x1_sq[:, n // 4:n // 4 + 1]).then_inc(squares_done, 1)
                    act.wait_ge(h_turned, n + 1)
                    t, kq = n // 4, n % 4
                    nc.scalar.activation(hT[:, 4 * kq:4 * kq + 4, t * P:(t + 1) * P],
                                         psB[:, n % 4, :].rearrange("p (k t) -> p k t", k=4), ACT.Copy).then_inc(h_turned_kept, 1)
                for j in range(CH):
                    for t in range(TT):
                        evacuate(pq_bank + TT * j + t, q[:, t, :])
                    if j == 2:
                        gelu(act, 0, 0)
                    for t in range(TT):
                        act.wait_ge(q_turned, TT * j + t + 1)
                        nc.scalar.activation(q_T[:, :, t * P:(t + 1) * P],
                                             psB[:, t, :].rearrange("p (b t) -> p b t", b=4), ACT.Copy).then_inc(q_turned_kept, 1)
                    for t in range(TT):
                        act.wait_ge(peer_scores_full, TT * j + t + 1)
                        nc.scalar.activation(scores[:, t, 4 * j:4 * j + 4, :],
                                             psB[:, 2 + t, :].rearrange("p (b k) -> p b k", b=4), ACT.Copy).then_inc(peer_scores_kept, 1)
                    if j == 0:
                        softmax_terms(act, 0, 0)

            @block.tensor
            def _(pe):
                def part(src, t, half=0):
                    return lambda k: src[:, half * KH + k, t * P:(t + 1) * P]

                def turn(src, t, c0, bank):
                    for k in range(4):
                        last = nc.tensor.transpose(psB[:, bank, k * P:(k + 1) * P], src[:, t, c0 + k * P:c0 + (k + 1) * P], ident[:])
                    return last

                def turn_m(j):
                    for t in range(TT):
                        pe.wait_ge(s_m, TT * j + t + 1)
                        if j >= 2:
                            pe.wait_ge(m_turned_kept, TT * (j - 2) + t + 1)
                        turn(m, t, j * N, 2 * (j % 2) + t).then_inc(m_turned, 1)

                n = ATTEND_END
                for j in range(CH):
                    gemm_half(pe, n, [part(y_hyT, t) for t in range(TT)])
                    if j == 0:
                        pe.wait_ge(s_onorm, 1)
                        for i in range(2 * TT):
                            turn(o_all, i // 2, (i % 2) * N, i).then_inc(y_da_turned, 1)
                        pe.wait_ge(y_da_kept, 2 * TT)
                    else:
                        turn_m(j - 1)
                    gemm_half(pe, n + 1, [part(y_daT, t) for t in range(TT)])
                    n += 2
                turn_m(CH - 1)
                pe.wait_ge(m_turned_kept, TT * CH)
                for j in range(CH):
                    if j < CH - 1:
                        for half in range(2):
                            gemm_half(pe, n + half, [part(mT, t, half) for t in range(TT)])
                    else:
                        gemm_chunk_by_tile(pe, n, mT)
                    n += 2
                    if j == 0:
                        pe.wait_ge(s_keys, 32)
                        for b in range(4):
                            for k in range(4):
                                last = nc.tensor.transpose(psB[:, b, k * P:(k + 1) * P], keys[:, 4 * b + k, :], ident[:])
                            last.then_inc(keys_turned, 1)
                pe.wait_ge(keys_turned_kept, 4)
                for t in range(TT):
                    for kq in range(4):
                        pe.wait_ge(s_h, 4 * t + kq + 1)
                        if t:
                            pe.wait_ge(h_turned_kept, kq + 1)
                        turn(h, t, kq * N, kq).then_inc(h_turned, 1)
                    pe.wait_ge(h_turned_kept, 4 * (t + 1))
                    for half in range(2):
                        gemm_half(pe, n + half, [part(hT, t, half)] * TT, only=t)
                n += 2

                def score(j):
                    for t in range(TT):
                        pe.wait_ge(a_free, pq_bank + TT * j + t + 1)
                        turn(q, t, 0, t).then_inc(q_turned, 1)
                    for t in range(TT):
                        pe.wait_ge(q_turned_kept, TT * j + t + 1)
                        if j:
                            pe.wait_ge(peer_scores_kept, TT * (j - 1) + t + 1)
                        for k in range(4):
                            b = 4 * j + k
                            last = nc.tensor.matmul(psB[:, 2 + t, k * P:(k + 1) * P], q_T[:, k, t * P:(t + 1) * P], keysT[:, b, :],
                                                    start=True, stop=True)
                        last.then_inc(peer_scores_full, 1)

                score(0)
                for j in range(1, CH):
                    for half in range(2):
                        gemm_half(pe, n, [part(hT, t, half) for t in range(TT)])
                        n += 1
                        if half == 0 and j > 1:
                            score(j - 1)
                score(CH - 1)

            @block.vector
            def _(v):
                ch = Chain(v, merge_order)
                ch.link(nc.vector.tensor_scalar(squares, squares, 1.0 / P, EPS, ALU.mult, ALU.add))
                rsqrt(nc, ch, squares, o_rstd, r_tmp)
                v.wait_ge(s_sub, 16)
                ch.link(nc.vector.tensor_scalar(subln, subln, 1.0 - LAM_INIT, None, ALU.mult))
                heads = o_all.rearrange("p t (h d) -> p (t h) d", d=P)
                ch.link(nc.vector.tensor_tensor(heads, heads, o_rstd.unsqueeze(2).broadcast_to((P, 2 * HEADS, P)), ALU.mult))
                ch.link(nc.vector.tensor_tensor(heads, heads, subln.unsqueeze(1).broadcast_to((P, 2 * HEADS, P)), ALU.mult))
                v.sem_inc(s_onorm, 1)
                for j in range(CH):
                    cs = slice(j * N, (j + 1) * N)
                    for t in range(TT):
                        hy = m_bank + 4 * j + t
                        v.wait_ge(a_full, hy + 1)
                        ch.link(nc.vector.scalar_tensor_tensor(m[:, t, cs], gates[:, t, cs], 1.0, psA[:, hy % 4, :], ALU.add, ALU.mult))
                        v.sem_inc(a_free, 1)
                    for t in range(TT):
                        da = m_bank + 4 * j + TT + t
                        v.wait_ge(a_full, da + 1)
                        ch.link(nc.vector.scalar_tensor_tensor(da_part[:, t, :], gates[:, t, D + j * N:D + (j + 1) * N], 1.0,
                                                               psA[:, da % 4, :], ALU.add, ALU.mult))
                        v.sem_inc(a_free, 1)
                        nc.vector.tensor_tensor(m[:, t, cs], m[:, t, cs], da_part[:, t, :], ALU.add).then_inc(s_m, 1)
                loads = 0
                for r, b, norm, dst in ROWS:
                    loads += 1
                    v.wait_ge(s_rdst[r], 16)
                    v.wait_ge(s_row, 16 * loads)
                    ch.link(nc.vector.tensor_tensor(dst, dst, row_tmp, ALU.add))
                    v.sem_inc(s_rowd, 1)
                    if norm:
                        loads += 1
                        v.wait_ge(s_row, 16 * loads)
                        one = 1.0 if norm == "norm_pre_ffn" else 0.0
                        ch.link(nc.vector.scalar_tensor_tensor(dst, dst, one, row_tmp, ALU.add, ALU.mult))
                        v.sem_inc(s_rowd, 1)
                v.wait_ge(s_xin, 16 * TT)
                for t in range(TT):
                    ss, r, tmp = rs[:, 0:1], rs[:, 1:2], rs[:, 2:3]
                    v.wait_ge(a_free, o_bank + TT * (CH - 1) + t + 1)
                    ch.link(nc.vector.tensor_reduce(ss, mix_sq[:, t, :], AX.X, ALU.add))
                    ch.link(nc.vector.tensor_scalar(ss, ss, 1.0 / D, EPS, ALU.mult, ALU.add))
                    rsqrt(nc, ch, ss, r, tmp)
                    ch.link(nc.vector.scalar_tensor_tensor(x1[:, t, :], mix[:, t, :], r, g1_row, ALU.mult, ALU.mult))
                    ch.link(nc.vector.tensor_tensor(x1[:, t, :], x1[:, t, :], x_in[:, t, :], ALU.add))
                    v.sem_inc(s_x1, 1)
                    ch.link(nc.vector.tensor_tensor(h[:, t, :], x1[:, t, :], gain_row, ALU.mult))
                    v.wait_ge(squares_done, TT * CH + t + 1)
                    ch.link(nc.vector.tensor_scalar(ss, x1_sq[:, t:t + 1], 1.0 / D, EPS, ALU.mult, ALU.add))
                    rsqrt(nc, ch, ss, r, tmp)
                    for kq in range(4):
                        cs = slice(kq * N, (kq + 1) * N)
                        nc.vector.scalar_tensor_tensor(h[:, t, cs], h[:, t, cs], r, shift_row[:, cs], ALU.mult, ALU.add).then_inc(s_h, 1)
                v.wait_ge(s_h, 4 * TT)
                v.wait_ge(s_iota, 16)
                v.wait_ge(peer_scores_kept, 1)
                choose(v, 0, 0)
                choose(v, 1, 1)
                ch.link(nc.vector.memset(total, 0.0))
                slots_n = len(first_rows)
                for j in range(TOPK):
                    v.wait_ge(e_slot[j % slots_n], 16 * (j // slots_n + 1))
                    dot(first_rows[j % slots_n], 0, 0, j).then_inc(e_used, 1)
                v.wait_ge(e_used, TOPK)
                v.sem_inc(dots_ready, 1)
                weigh(v, 0, 0)
                for j in range(TOPK):
                    g = TOPK + j
                    v.wait_ge(e_slot[g % slots_n], 16 * (g // slots_n + 1))
                    add_row(first_rows[g % slots_n], 0, j).then_inc(e_used, 1)
                    v.wait_ge(e_used, g + 1)

        with ExitStack() as st:
            slots = at(0, SLOTS, D)
            rs = at(200, 4)
            s_slot = [sem(f"s_slot{i}") for i in range(SLOTS)]
            slot_used, result_order, s_out, s_done = sem("slot_used"), sem("result_order"), sem("s_out"), sem("s_done")
            block = st.enter_context(nc.Block())
            ALL = TT * PEER_HEADS

            @block.gpsimd
            def _(pool):
                pool.sem_inc(slot_used, SLOTS)

                def gather_head(head, par):
                    pool.wait_ge(rows_chosen, head + 1)
                    pool.sem_inc(s_gathers, 1)
                    for table in (u_tab, v_tab):
                        for j in range(TOPK):
                            pool.wait_ge(slot_used, (head - 1) * 2 * TOPK + (TOPK if table is v_tab else 0) + j + 1)
                            pool.sem_inc(s_gathers, 1)
                            gather(table, par, j, slots[:, j, :]).then_inc(s_slot[j], 16)

                with pool.Fori(0, ALL // 2 - 1) as pair:
                    gather_head(2 * pair + 1, 1)
                    gather_head(2 * pair + 2, 0)
                gather_head(ALL - 1, 1)

            @block.scalar
            def _(act):
                with act.Fori(0, ALL // 2 - 1) as pair:
                    for head, par in ((2 * pair + 1, 1), (2 * pair + 2, 0)):
                        softmax_terms(act, head, par)
                        gelu(act, head, par)
                softmax_terms(act, ALL - 1, 1)
                gelu(act, ALL - 1, 1)

            @block.vector
            def _(v):
                def one_head(head, t, par, last=False):
                    before = (head - 1) * 2 * TOPK
                    for j in range(TOPK):
                        v.wait_ge(s_slot[j], (head - 1) * 32 + 16)
                        dot(slots[:, j, :], t, par, j).then_inc(slot_used, 1)
                    v.wait_ge(slot_used, before + TOPK + SLOTS)
                    v.sem_inc(dots_ready, 1)
                    if not last:
                        choose(v, head + 1, 1 - par)
                    weigh(v, head, par)
                    for j in range(TOPK):
                        v.wait_ge(s_slot[j], (head - 1) * 32 + 32)
                        add_row(slots[:, j, :], par, j).then_inc(slot_used, 1)
                        v.wait_ge(slot_used, before + TOPK + j + 1 + SLOTS)

                end = Chain(v, result_order)
                for t in range(TT):
                    if t == 0:
                        with v.Fori(0, PEER_HEADS // 2 - 1) as pair:
                            one_head(2 * pair + 1, t, 1)
                            one_head(2 * pair + 2, t, 0)
                        one_head(PEER_HEADS - 1, t, 1)
                    else:
                        end.link(nc.vector.memset(total, 0.0))
                        with v.Fori(t * PEER_HEADS // 2, (t + 1) * PEER_HEADS // 2 - 1) as pair:
                            one_head(2 * pair, t, 0)
                            one_head(2 * pair + 1, t, 1)
                        one_head((t + 1) * PEER_HEADS - 2, t, 0)
                        one_head((t + 1) * PEER_HEADS - 1, t, 1, last=True)
                    ss, r, tmp = rs[:, 0:1], rs[:, 1:2], rs[:, 2:3]
                    res = x1[:, t, :]
                    sq = h[:, t, :]
                    end.link(nc.vector.tensor_tensor_reduce(sq, total, total, 1.0, 0.0, ALU.mult, ALU.add, ss))
                    end.link(nc.vector.tensor_scalar(ss, ss, 1.0 / D, EPS, ALU.mult, ALU.add))
                    rsqrt(nc, end, ss, r, tmp)
                    end.link(nc.vector.scalar_tensor_tensor(total, total, r, g2_row, ALU.mult, ALU.mult))
                    end.link(nc.vector.tensor_tensor(res, res, total, ALU.add))
                    v.sem_inc(s_done, 1)

            @block.sync
            def _(sp):
                for t in range(TT):
                    sp.wait_ge(s_done, t + 1)
                    sp.dma_start(out[0, t * P:(t + 1) * P, :], x1[:, t, :]).then_inc(s_out, 16)
                sp.wait_ge(s_out, 16 * TT)



_INS = ["x", "c", "ctx", "c_ctx", "w_mod", "b_mod", "norm_pre_mix", "norm_post_mix", "norm_pre_ffn", "norm_post_ffn",
        "w_in", "hy_conv_w", "hy_conv_b", "filt_w1", "filt_b1", "filt_w2", "filt_b2", "filt_w3", "filt_b3",
        "filt_w_out", "filt_freq", "hy_bias", "da_lambda", "da_subln", "w_hy_out", "w_da_out", "w_o",
        "peer_w_q", "peer_keys", "peer_u", "peer_v"]


def kernel(**inputs):
    import numpy as _np
    import concourse.bacc as _bacc
    from concourse import mybir as _mybir
    from concourse.bass_utils import run_bass_kernel_spmd as _run

    nc = _bacc.Bacc("TRN2", target_bir_lowering=False, num_devices=1)
    arrays, io = {}, {}
    for name, a in [(n, inputs[n]) for n in _INS] + list(constants().items()):
        a = _np.ascontiguousarray(a)
        arrays[f"in_{name}_dram"] = a
        io[name] = nc.dram_tensor(f"in_{name}_dram", a.shape, _mybir.dt.from_np(a.dtype), kind="ExternalInput").ap()
    out = nc.dram_tensor("out_0_dram", (1, SEQ, D), F32, kind="ExternalOutput").ap()
    build(nc, io, out)
    r = _run(nc, [arrays], core_ids=[0])
    return r.results[0]["out_0_dram"]
```
